# Optimizing a Trainium2 kernel written in Bass

```python
import math
import jax, jax.numpy as jnp
from jax import lax
import numpy as np

D_MODEL = 1024
BATCH = 1
SEQ = 256
DEPTH = 1

MEM_LEN = 256
HEAD_DIM = 128
ATTN_HEADS = 6
ATTN_KV_HEADS = 2
ATTN_GROUP = ATTN_HEADS // ATTN_KV_HEADS
WINDOW = 128
BLOCK = 128
ROPE_DIM = HEAD_DIM // 4
ROPE_THETA = 500000.0
LRU_WIDTH = 768
LRU_BLOCKS = 6
LRU_BLOCK_W = LRU_WIDTH // LRU_BLOCKS
CONV_WIDTH = 4
CONV_LEFT = CONV_WIDTH // 2
LRU_C = 8.0
MEM_HEADS = 4
N_BRANCH = 3
PEER_HEADS = 8
PEER_KEYS = 128
PEER_EXPERTS = PEER_KEYS * PEER_KEYS
PEER_QDIM = 256
PEER_HALF = PEER_QDIM // 2
PEER_TOPK = 16
PEER_CHUNK = 128
EPS = 1e-6
NEG_INF = -1e30

ATTN_Q_W = ATTN_HEADS * HEAD_DIM
ATTN_KV_W = ATTN_KV_HEADS * HEAD_DIM
MEM_Q_W = MEM_HEADS * HEAD_DIM
GATE_W = N_BRANCH * D_MODEL
IN_W = ATTN_Q_W + 2 * ATTN_KV_W + 2 * LRU_WIDTH + MEM_Q_W + GATE_W


def rmsnorm(x, g):
    xf = x.astype(jnp.float32)
    y = xf * lax.rsqrt(jnp.mean(xf * xf, axis=-1, keepdims=True) + EPS) * g.astype(jnp.float32)
    return y.astype(x.dtype)

def partial_rope(t, positions):
    half = ROPE_DIM // 2
    inv_freq = ROPE_THETA ** (-jnp.arange(0, ROPE_DIM, 2, dtype=jnp.float32) / ROPE_DIM)
    ang = positions.astype(jnp.float32)[..., None] * inv_freq
    cos = jnp.cos(ang)[:, :, None, :]
    sin = jnp.sin(ang)[:, :, None, :]
    tr = t[..., :ROPE_DIM].astype(jnp.float32)
    t1, t2 = tr[..., :half], tr[..., half:]
    rot = jnp.concatenate([t1 * cos - t2 * sin, t2 * cos + t1 * sin], axis=-1)
    return jnp.concatenate([rot.astype(t.dtype), t[..., ROPE_DIM:]], axis=-1)

def band_blocks(t, nb):
    b = t.shape[0]
    tp = jnp.pad(t, ((0, 0), (BLOCK, BLOCK), (0, 0), (0, 0)))
    tp = tp.reshape(b, nb + 2, BLOCK, t.shape[2], t.shape[3])
    return jnp.concatenate([tp[:, :-2], tp[:, 1:-1], tp[:, 2:]], axis=2)

def windowed_gqa(q, k, v, sink):
    b, s = q.shape[0], q.shape[1]
    nb = s // BLOCK
    qb = q.reshape(b, nb, BLOCK, ATTN_KV_HEADS, ATTN_GROUP, HEAD_DIM)
    kb = band_blocks(k, nb)
    vb = band_blocks(v, nb)
    scores = jnp.einsum('bnqkgd,bnskd->bnkgqs', qb, kb).astype(jnp.float32) * (HEAD_DIM ** -0.5)
    blk = jnp.arange(nb, dtype=jnp.int32)[:, None]
    q_pos = blk * BLOCK + jnp.arange(BLOCK, dtype=jnp.int32)[None, :]
    k_pos = blk * BLOCK - BLOCK + jnp.arange(3 * BLOCK, dtype=jnp.int32)[None, :]
    valid = ((k_pos[:, None, :] >= 0) & (k_pos[:, None, :] < s)
             & (jnp.abs(k_pos[:, None, :] - q_pos[:, :, None]) <= WINDOW))
    scores = jnp.where(valid[None, :, None, None], scores, NEG_INF)
    sink_b = jnp.broadcast_to(sink.astype(jnp.float32).reshape(ATTN_KV_HEADS, ATTN_GROUP)[None, None, :, :, None, None],
                              scores.shape[:-1] + (1,))
    p = jax.nn.softmax(jnp.concatenate([scores, sink_b], axis=-1), axis=-1)[..., :-1]
    out = jnp.einsum('bnkgqs,bnskd->bnqkgd', p.astype(v.dtype), vb)
    return out.reshape(b, s, ATTN_Q_W)

def centred_depthwise_conv(t, w, bias):
    s = t.shape[1]
    tp = jnp.pad(t, ((0, 0), (CONV_LEFT, CONV_WIDTH - 1 - CONV_LEFT), (0, 0)))
    y = bias[None, None, :]
    for j in range(CONV_WIDTH):
        y = y + w[j][None, None, :] * tp[:, j:j + s]
    return y

def _lin_comb(c1, c2):
    a1, b1 = c1
    a2, b2 = c2
    return a1 * a2, a2 * b1 + b2

def bidir_rglru(xc, w_r, b_r, w_i, b_i, lam):
    b, s = xc.shape[0], xc.shape[1]
    xf = xc.astype(jnp.float32)
    xblk = xf.reshape(b, s, LRU_BLOCKS, LRU_BLOCK_W)
    r = jax.nn.sigmoid(jnp.einsum('bshc,dhce->dbshe', xblk, w_r.astype(jnp.float32)).reshape(2, b, s, LRU_WIDTH)
                       + b_r.astype(jnp.float32)[:, None, None, :])
    i = jax.nn.sigmoid(jnp.einsum('bshc,dhce->dbshe', xblk, w_i.astype(jnp.float32)).reshape(2, b, s, LRU_WIDTH)
                       + b_i.astype(jnp.float32)[:, None, None, :])
    log_a = -LRU_C * r * jax.nn.softplus(-lam.astype(jnp.float32))[:, None, None, :]
    a = jnp.exp(log_a)
    bx = jnp.sqrt(-jnp.expm1(2.0 * log_a)) * (i * xf[None])
    _, h_fwd = lax.associative_scan(_lin_comb, (a[0], bx[0]), axis=1)
    _, h_bwd = lax.associative_scan(_lin_comb, (a[1], bx[1]), axis=1, reverse=True)
    return (h_fwd + h_bwd).astype(xc.dtype)

def memory_cross_attention(q, k, v):
    scores = jnp.einsum('bshd,bmhd->bhsm', q, k).astype(jnp.float32) * (HEAD_DIM ** -0.5)
    p = jax.nn.softmax(scores, axis=-1)
    out = jnp.einsum('bhsm,bmhd->bshd', p.astype(v.dtype), v)
    return out.reshape(q.shape[0], q.shape[1], MEM_Q_W)

def peer_ffn(h, w_q, sub_keys, u_tab, v_tab):
    b, s, d = h.shape
    q = (h @ w_q).reshape(b, s, PEER_HEADS, 2, PEER_HALF)
    sc = jnp.einsum('bshpc,hpkc->bshpk', q, sub_keys).astype(jnp.float32)
    top_v, top_i = lax.top_k(sc, PEER_TOPK)
    cand_v = (top_v[..., 0, :, None] + top_v[..., 1, None, :]).reshape(b, s, PEER_HEADS, PEER_TOPK * PEER_TOPK)
    cand_i = (top_i[..., 0, :, None] * PEER_KEYS + top_i[..., 1, None, :]).reshape(b, s, PEER_HEADS, PEER_TOPK * PEER_TOPK)
    best_v, best_pos = lax.top_k(cand_v, PEER_TOPK)
    idx = jnp.take_along_axis(cand_i, best_pos, axis=-1)
    gate = jax.nn.softmax(best_v, axis=-1)
    n_tok = b * s
    n_chunk = n_tok // PEER_CHUNK
    hc = h.reshape(n_chunk, PEER_CHUNK, d)
    ic = idx.reshape(n_chunk, PEER_CHUNK, PEER_HEADS, PEER_TOPK)
    gc = gate.reshape(n_chunk, PEER_CHUNK, PEER_HEADS, PEER_TOPK)

    def expert_chunk(args):
        hx, ix, gx = args
        u = u_tab[ix]
        act = jax.nn.gelu(jnp.einsum('chkd,cd->chk', u, hx).astype(jnp.float32))
        vv = v_tab[ix]
        return jnp.einsum('chk,chkd->cd', (gx * act).astype(vv.dtype), vv)

    out = lax.map(expert_chunk, (hc, ic, gc))
    return out.reshape(b, s, d)

def first_inputs(seed: int = 0) -> dict:
    key = jax.random.key(seed)
    ks = jax.random.split(key, 32)
    f32 = jnp.float32
    nrm = lambda k, shape, scale: jax.random.normal(k, shape, f32) * scale
    u = jax.random.uniform(ks[12], (DEPTH, 2, LRU_WIDTH), f32, 0.9, 0.999)
    a0 = u ** (1.0 / LRU_C)
    lam = jnp.log(a0) - jnp.log1p(-a0)
    return {
        "x": nrm(ks[0], (BATCH, SEQ, D_MODEL), 1.0),
        "mem": nrm(ks[1], (BATCH, MEM_LEN, D_MODEL), 1.0),
        "positions": jnp.broadcast_to(jnp.arange(SEQ, dtype=jnp.int32)[None, :], (BATCH, SEQ)),
        "g_mix": 1.0 + nrm(ks[2], (DEPTH, D_MODEL), 0.02),
        "g_mem": 1.0 + nrm(ks[3], (DEPTH, D_MODEL), 0.02),
        "w_in": nrm(ks[4], (DEPTH, D_MODEL, IN_W), D_MODEL ** -0.5),
        "gate_b": nrm(ks[5], (DEPTH, GATE_W), 0.02),
        "attn_sink": nrm(ks[6], (DEPTH, ATTN_HEADS), 0.5),
        "conv_w": nrm(ks[7], (DEPTH, CONV_WIDTH, LRU_WIDTH), CONV_WIDTH ** -0.5),
        "conv_b": nrm(ks[8], (DEPTH, LRU_WIDTH), 0.02),
        "lru_wr": nrm(ks[9], (DEPTH, 2, LRU_BLOCKS, LRU_BLOCK_W, LRU_BLOCK_W), LRU_BLOCK_W ** -0.5),
        "lru_br": nrm(ks[10], (DEPTH, 2, LRU_WIDTH), 0.02),
        "lru_wi": nrm(ks[11], (DEPTH, 2, LRU_BLOCKS, LRU_BLOCK_W, LRU_BLOCK_W), LRU_BLOCK_W ** -0.5),
        "lru_bi": nrm(ks[13], (DEPTH, 2, LRU_WIDTH), 0.02),
        "lru_lambda": lam,
        "w_mem_kv": nrm(ks[14], (DEPTH, D_MODEL, 2 * MEM_Q_W), D_MODEL ** -0.5),
        "p_attn": nrm(ks[15], (DEPTH, ATTN_Q_W, D_MODEL), ATTN_Q_W ** -0.5),
        "p_lru": nrm(ks[16], (DEPTH, LRU_WIDTH, D_MODEL), LRU_WIDTH ** -0.5),
        "p_mem": nrm(ks[17], (DEPTH, MEM_Q_W, D_MODEL), MEM_Q_W ** -0.5),
        "w_out": nrm(ks[18], (DEPTH, D_MODEL, D_MODEL), D_MODEL ** -0.5),
        "g_ffn": 1.0 + nrm(ks[19], (DEPTH, D_MODEL), 0.02),
        "w_peer_q": nrm(ks[20], (DEPTH, D_MODEL, PEER_HEADS * PEER_QDIM), D_MODEL ** -0.5),
        "peer_sub_keys": nrm(ks[21], (DEPTH, PEER_HEADS, 2, PEER_KEYS, PEER_HALF), PEER_HALF ** -0.5),
        "peer_u": nrm(ks[22], (DEPTH, PEER_EXPERTS, D_MODEL), D_MODEL ** -0.5),
        "peer_v": nrm(ks[23], (DEPTH, PEER_EXPERTS, D_MODEL), 0.25),
        "g_final": 1.0 + nrm(ks[24], (D_MODEL,), 0.02),
    }

def first_block(x, mem, positions, g_mix, g_mem, w_in, gate_b, attn_sink, conv_w, conv_b,
              lru_wr, lru_br, lru_wi, lru_bi, lru_lambda, w_mem_kv, p_attn, p_lru, p_mem,
              w_out, g_ffn, w_peer_q, peer_sub_keys, peer_u, peer_v, g_final):
    b, s, d = x.shape
    offs = [int(o) for o in np.cumsum([ATTN_Q_W, ATTN_KV_W, ATTN_KV_W, LRU_WIDTH, LRU_WIDTH, MEM_Q_W])]
    for l in range(DEPTH):
        h = rmsnorm(x, g_mix[l])
        proj = h @ w_in[l]
        q_a, k_a, v_a, x_l, gate_l, q_m, gates = jnp.split(proj, offs, axis=-1)
        q_a = partial_rope(q_a.reshape(b, s, ATTN_HEADS, HEAD_DIM), positions)
        k_a = partial_rope(k_a.reshape(b, s, ATTN_KV_HEADS, HEAD_DIM), positions)
        v_a = v_a.reshape(b, s, ATTN_KV_HEADS, HEAD_DIM)
        attn_out = windowed_gqa(q_a, k_a, v_a, attn_sink[l])
        xc = centred_depthwise_conv(x_l, conv_w[l], conv_b[l])
        lru_out = bidir_rglru(xc, lru_wr[l], lru_br[l], lru_wi[l], lru_bi[l], lru_lambda[l]) * jax.nn.gelu(gate_l)
        kv_m = rmsnorm(mem, g_mem[l]) @ w_mem_kv[l]
        k_m = kv_m[..., :MEM_Q_W].reshape(b, MEM_LEN, MEM_HEADS, HEAD_DIM)
        v_m = kv_m[..., MEM_Q_W:].reshape(b, MEM_LEN, MEM_HEADS, HEAD_DIM)
        mem_out = memory_cross_attention(q_m.reshape(b, s, MEM_HEADS, HEAD_DIM), k_m, v_m)
        g = jax.nn.sigmoid(gates + gate_b[l]).reshape(b, s, N_BRANCH, d)
        merged = (g[:, :, 0] * (attn_out @ p_attn[l])
                  + g[:, :, 1] * (lru_out @ p_lru[l])
                  + g[:, :, 2] * (mem_out @ p_mem[l]))
        x = x + merged @ w_out[l]
        h2 = rmsnorm(x, g_ffn[l])
        x = x + peer_ffn(h2, w_peer_q[l], peer_sub_keys[l], peer_u[l], peer_v[l])
    return rmsnorm(x, g_final)


DEPTH_2 = 2

CHUNK = 64
HEAD_DIM_2 = 64
N_MIX_HEADS = D_MODEL // HEAD_DIM_2
SELF_HEADS = N_MIX_HEADS - MEM_HEADS
SWA_KV_HEADS = 3
SWA_GROUP = SELF_HEADS // SWA_KV_HEADS
WINDOW_CHUNKS = WINDOW // CHUNK
ROT_DIM = HEAD_DIM_2 // 4
ROT_HALF = ROT_DIM // 2
FOX_BLOCK = 128
D_FF = ((8 * D_MODEL // 3 + 127) // 128) * 128
N_EXPERTS = 8
TOP_K = 2
EXPERT_BLOCK = 128
LN_EPS = 1e-5
NEG = -1e30
ATTN_SCALE = HEAD_DIM_2 ** -0.5
DN_ALPHA = (2.0 * DEPTH_2) ** 0.25
DN_BETA = (8.0 * DEPTH_2) ** -0.25
N_SWA_LAYERS = (DEPTH_2 + 1) // 2
N_FOX_LAYERS = DEPTH_2 // 2
SWA_IN = (SELF_HEADS + 2 * SWA_KV_HEADS + MEM_HEADS) * HEAD_DIM_2
FOX_IN = (3 * SELF_HEADS + MEM_HEADS) * HEAD_DIM_2 + SELF_HEADS


def layer_norm(x, g, b):
    xf = x.astype(jnp.float32)
    mu = jnp.mean(xf, axis=-1, keepdims=True)
    var = jnp.mean(jnp.square(xf - mu), axis=-1, keepdims=True)
    return ((xf - mu) * lax.rsqrt(var + LN_EPS) * g + b).astype(x.dtype)

def rope_tables(positions):
    inv_freq = ROPE_THETA ** (-jnp.arange(0, ROT_DIM, 2, dtype=jnp.float32) / ROT_DIM)
    ang = positions.astype(jnp.float32)[..., None] * inv_freq
    return jnp.cos(ang)[:, :, None, :], jnp.sin(ang)[:, :, None, :]

def partial_rope_2(t, cos, sin):
    r = t[..., :ROT_DIM].astype(jnp.float32)
    r1, r2 = r[..., :ROT_HALF], r[..., ROT_HALF:]
    rot = jnp.concatenate([r1 * cos - r2 * sin, r2 * cos + r1 * sin], axis=-1)
    return jnp.concatenate([rot.astype(t.dtype), t[..., ROT_DIM:]], axis=-1)

def swa_sink_attention(q, k, v, sinks):
    B, S = q.shape[0], q.shape[1]
    n_c = S // CHUNK
    pad = WINDOW_CHUNKS * CHUNK
    n_keys = (WINDOW_CHUNKS + 1) * CHUNK
    qb = q.reshape(B, n_c, CHUNK, SWA_KV_HEADS, SWA_GROUP, HEAD_DIM_2)

    def band(t):
        tp = jnp.pad(t, ((0, 0), (pad, 0), (0, 0), (0, 0)))
        tp = tp.reshape(B, n_c + WINDOW_CHUNKS, CHUNK, SWA_KV_HEADS, HEAD_DIM_2)
        return jnp.concatenate([tp[:, m:m + n_c] for m in range(WINDOW_CHUNKS + 1)], axis=2)

    kb, vb = band(k), band(v)
    s = jnp.einsum('bnqhgd,bnkhd->bnhgqk', qb, kb).astype(jnp.float32) * ATTN_SCALE
    key_chunk = jnp.arange(n_c)[:, None] - WINDOW_CHUNKS + (jnp.arange(n_keys) // CHUNK)[None, :]
    valid = key_chunk >= 0
    s = jnp.where(valid[None, :, None, None, None, :], s, NEG)
    sk = sinks.astype(jnp.float32).reshape(SWA_KV_HEADS, SWA_GROUP)[None, None, :, :, None]
    m = jnp.maximum(jnp.max(s, axis=-1), sk)
    p = jnp.exp(s - m[..., None])
    den = jnp.sum(p, axis=-1) + jnp.exp(sk - m)
    probs = (p / den[..., None]).astype(v.dtype)
    o = jnp.einsum('bnhgqk,bnkhd->bnqhgd', probs, vb)
    return o.reshape(B, S, SELF_HEADS * HEAD_DIM_2)

def forgetting_attention(q, k, v, log_f):
    B, S = q.shape[0], q.shape[1]
    cum = jnp.cumsum(log_f, axis=1).transpose(0, 2, 1)
    outs = []
    for i in range(S // FOX_BLOCK):
        lo, hi = i * FOX_BLOCK, (i + 1) * FOX_BLOCK
        s = jnp.einsum('bqhd,bkhd->bhqk', q[:, lo:hi], k[:, :hi]).astype(jnp.float32) * ATTN_SCALE
        bias = cum[:, :, lo:hi, None] - cum[:, :, None, :hi]
        causal = jnp.arange(lo, hi)[:, None] >= jnp.arange(hi)[None, :]
        s = jnp.where(causal, s + bias, NEG)
        p = jax.nn.softmax(s, axis=-1).astype(v.dtype)
        outs.append(jnp.einsum('bhqk,bkhd->bqhd', p, v[:, :hi]))
    return jnp.concatenate(outs, axis=1).reshape(B, S, SELF_HEADS * HEAD_DIM_2)

def memory_attention(qc, km, vm):
    B, S = qc.shape[0], qc.shape[1]
    s = jnp.einsum('bshd,bmhd->bhsm', qc, km).astype(jnp.float32) * ATTN_SCALE
    p = jax.nn.softmax(s, axis=-1).astype(vm.dtype)
    return jnp.einsum('bhsm,bmhd->bshd', p, vm).reshape(B, S, MEM_HEADS * HEAD_DIM_2)

def swiglu(x, w_in, w_out):
    h = x @ w_in
    a, b = h[..., :D_FF], h[..., D_FF:]
    return (jax.nn.silu(a) * b) @ w_out

def moe_swiglu(x, w_router, b_router, w_in, w_out):
    shp = x.shape
    x2 = x.reshape(-1, shp[-1])
    n_tok = x2.shape[0]
    logits = (x2 @ w_router).astype(jnp.float32) + b_router.astype(jnp.float32)
    top_vals, top_idx = lax.top_k(logits, TOP_K)
    gates = jax.nn.softmax(top_vals, axis=-1)
    n_asg = n_tok * TOP_K
    e_flat = top_idx.reshape(-1)
    t_flat = jnp.repeat(jnp.arange(n_tok, dtype=jnp.int32), TOP_K)
    g_flat = gates.reshape(-1)
    order = jnp.argsort(e_flat)
    se, st, sg = e_flat[order], t_flat[order], g_flat[order]
    counts = jnp.bincount(e_flat, length=N_EXPERTS)
    starts = jnp.cumsum(counts) - counts
    pcounts = (counts + EXPERT_BLOCK - 1) // EXPERT_BLOCK * EXPERT_BLOCK
    pends = jnp.cumsum(pcounts)
    pstarts = pends - pcounts
    dest = pstarts[se] + (jnp.arange(n_asg) - starts[se])
    n_blocks = -(-n_asg // EXPERT_BLOCK) + N_EXPERTS
    n_slots = n_blocks * EXPERT_BLOCK
    slot_tok = jnp.zeros((n_slots,), jnp.int32).at[dest].set(st)
    slot_gate = jnp.zeros((n_slots,), x2.dtype).at[dest].set(sg.astype(x2.dtype))
    block_exp = jnp.minimum(
        jnp.searchsorted(pends, jnp.arange(n_blocks) * EXPERT_BLOCK, side='right'), N_EXPERTS - 1)
    xs = x2[slot_tok].reshape(n_blocks, EXPERT_BLOCK, shp[-1])

    def expert_block(args):
        xb, e = args
        h = xb @ w_in[e]
        return (jax.nn.silu(h[:, :D_FF]) * h[:, D_FF:]) @ w_out[e]

    ys = lax.map(expert_block, (xs, block_exp)).reshape(n_slots, shp[-1])
    y = jnp.zeros_like(x2).at[slot_tok].add((ys * slot_gate[:, None]).astype(x2.dtype))
    return y.reshape(shp)

def second_inputs(seed: int = 0) -> dict:
    key = jax.random.key(seed)
    ks = jax.random.split(key, 20)
    nrm = jax.random.normal
    f32 = jnp.float32
    x = nrm(ks[0], (BATCH, SEQ, D_MODEL), f32)
    mem = nrm(ks[1], (BATCH, MEM_LEN, D_MODEL), f32)
    offset = jax.random.randint(ks[2], (BATCH, 1), 0, 1 << 16, dtype=jnp.int32)
    positions = offset + jnp.arange(SEQ, dtype=jnp.int32)[None, :]
    sd = D_MODEL ** -0.5
    sf = D_FF ** -0.5
    return {
        "x": x,
        "mem": mem,
        "positions": positions,
        "w_in_swa": nrm(ks[3], (N_SWA_LAYERS, D_MODEL, SWA_IN), f32) * sd,
        "attn_sinks": nrm(ks[4], (N_SWA_LAYERS, SELF_HEADS), f32) * 0.5,
        "w_in_fox": nrm(ks[5], (N_FOX_LAYERS, D_MODEL, FOX_IN), f32) * sd,
        "b_forget": jax.random.uniform(ks[6], (N_FOX_LAYERS, SELF_HEADS), f32, 1.0, 4.0),
        "w_mem_kv": nrm(ks[7], (DEPTH_2, D_MODEL, 2 * MEM_HEADS * HEAD_DIM_2), f32) * sd,
        "w_out": nrm(ks[8], (DEPTH_2, D_MODEL, D_MODEL), f32) * sd * DN_BETA,
        "ln_attn_g": 1.0 + 0.02 * nrm(ks[9], (DEPTH_2, D_MODEL), f32),
        "ln_attn_b": 0.02 * nrm(ks[10], (DEPTH_2, D_MODEL), f32),
        "w_ffn_in": nrm(ks[11], (N_SWA_LAYERS, D_MODEL, 2 * D_FF), f32) * sd,
        "w_ffn_out": nrm(ks[12], (N_SWA_LAYERS, D_FF, D_MODEL), f32) * sf * DN_BETA,
        "w_router": nrm(ks[13], (N_FOX_LAYERS, D_MODEL, N_EXPERTS), f32) * sd,
        "b_router": 0.01 * nrm(ks[14], (N_FOX_LAYERS, N_EXPERTS), f32),
        "w_exp_in": nrm(ks[15], (N_FOX_LAYERS, N_EXPERTS, D_MODEL, 2 * D_FF), f32) * sd,
        "w_exp_out": nrm(ks[16], (N_FOX_LAYERS, N_EXPERTS, D_FF, D_MODEL), f32) * sf * DN_BETA,
        "ln_ffn_g": 1.0 + 0.02 * nrm(ks[17], (DEPTH_2, D_MODEL), f32),
        "ln_ffn_b": 0.02 * nrm(ks[18], (DEPTH_2, D_MODEL), f32),
    }

def second_block(x, mem, positions, w_in_swa, attn_sinks, w_in_fox, b_forget, w_mem_kv, w_out,
              ln_attn_g, ln_attn_b, w_ffn_in, w_ffn_out, w_router, b_router, w_exp_in,
              w_exp_out, ln_ffn_g, ln_ffn_b):
    B, S = x.shape[0], x.shape[1]
    cos, sin = rope_tables(positions)
    hq = SELF_HEADS * HEAD_DIM_2
    hkv = SWA_KV_HEADS * HEAD_DIM_2
    hm = MEM_HEADS * HEAD_DIM_2
    for i in range(DEPTH_2):
        j = i // 2
        kvm = mem @ w_mem_kv[i]
        km = kvm[..., :hm].reshape(B, MEM_LEN, MEM_HEADS, HEAD_DIM_2)
        vm = kvm[..., hm:].reshape(B, MEM_LEN, MEM_HEADS, HEAD_DIM_2)
        if i % 2 == 0:
            proj = x @ w_in_swa[j]
            q = proj[..., :hq].reshape(B, S, SELF_HEADS, HEAD_DIM_2)
            k = proj[..., hq:hq + hkv].reshape(B, S, SWA_KV_HEADS, HEAD_DIM_2)
            v = proj[..., hq + hkv:hq + 2 * hkv].reshape(B, S, SWA_KV_HEADS, HEAD_DIM_2)
            qc = proj[..., hq + 2 * hkv:].reshape(B, S, MEM_HEADS, HEAD_DIM_2)
            q, k = partial_rope_2(q, cos, sin), partial_rope_2(k, cos, sin)
            self_out = swa_sink_attention(q, k, v, attn_sinks[j])
        else:
            proj = x @ w_in_fox[j]
            q = proj[..., :hq].reshape(B, S, SELF_HEADS, HEAD_DIM_2)
            k = proj[..., hq:2 * hq].reshape(B, S, SELF_HEADS, HEAD_DIM_2)
            v = proj[..., 2 * hq:3 * hq].reshape(B, S, SELF_HEADS, HEAD_DIM_2)
            qc = proj[..., 3 * hq:3 * hq + hm].reshape(B, S, MEM_HEADS, HEAD_DIM_2)
            f_logit = proj[..., 3 * hq + hm:].astype(jnp.float32) + b_forget[j].astype(jnp.float32)
            log_f = jax.nn.log_sigmoid(f_logit)
            self_out = forgetting_attention(q, k, v, log_f)
        cross_out = memory_attention(qc, km, vm)
        mix = jnp.concatenate([self_out, cross_out], axis=-1) @ w_out[i]
        x = layer_norm(DN_ALPHA * x + mix, ln_attn_g[i], ln_attn_b[i])
        if i % 2 == 0:
            ffn = swiglu(x, w_ffn_in[j], w_ffn_out[j])
        else:
            ffn = moe_swiglu(x, w_router[j], b_router[j], w_exp_in[j], w_exp_out[j])
        x = layer_norm(DN_ALPHA * x + ffn, ln_ffn_g[i], ln_ffn_b[i])
    return x


def setup_inputs(seed=0):
    out = dict(first_inputs(seed))
    for name, value in second_inputs(seed + 1).items():
        if name != "x":
            out[name + "_2"] = value
    return out


def reference(
    x, mem, positions, g_mix, g_mem, w_in, gate_b, attn_sink, conv_w, conv_b, lru_wr, lru_br,
    lru_wi, lru_bi, lru_lambda, w_mem_kv, p_attn, p_lru, p_mem, w_out, g_ffn, w_peer_q,
    peer_sub_keys, peer_u, peer_v, g_final, mem_2, positions_2, w_in_swa_2, attn_sinks_2,
    w_in_fox_2, b_forget_2, w_mem_kv_2, w_out_2, ln_attn_g_2, ln_attn_b_2, w_ffn_in_2,
    w_ffn_out_2, w_router_2, b_router_2, w_exp_in_2, w_exp_out_2, ln_ffn_g_2, ln_ffn_b_2,
):
    x = first_block(
        x, mem, positions, g_mix, g_mem, w_in, gate_b, attn_sink, conv_w, conv_b, lru_wr,
        lru_br, lru_wi, lru_bi, lru_lambda, w_mem_kv, p_attn, p_lru, p_mem, w_out, g_ffn,
        w_peer_q, peer_sub_keys, peer_u, peer_v, g_final,
    )
    return second_block(
        x, mem_2, positions_2, w_in_swa_2, attn_sinks_2, w_in_fox_2, b_forget_2, w_mem_kv_2,
        w_out_2, ln_attn_g_2, ln_attn_b_2, w_ffn_in_2, w_ffn_out_2, w_router_2, b_router_2,
        w_exp_in_2, w_exp_out_2, ln_ffn_g_2, ln_ffn_b_2,
    )


_drawn_inputs = setup_inputs


def setup_inputs(seed=0):
    import zlib

    import numpy as np

    out = dict(_drawn_inputs(seed))
    spreads = {}
    factors = {'g_mix': 2.704,
     'g_mem': 7.698,
     'gate_b': 7.988,
     'attn_sink': 64.0,
     'lru_br': 22.965,
     'lru_bi': 16.587,
     'attn_sinks_2': 8.0,
     'b_router_2': 6.066,
     'g_ffn': 8.0}
    for name, (base, spread) in spreads.items():
        noise = np.random.default_rng([zlib.crc32(name.encode()), seed]).standard_normal(out[name].shape)
        drawn = base * np.exp(spread * noise) if base else spread * noise
        out[name] = __import__('jax').numpy.asarray(drawn.astype(out[name].dtype))
    for name, factor in factors.items():
        out[name] = (out[name] * factor).astype(out[name].dtype)
    return out
```

```python
import math
from contextlib import ExitStack

import numpy as np

import concourse.bass as bass
from concourse import mybir

F32, I32, U32 = mybir.dt.float32, mybir.dt.int32, mybir.dt.uint32
ALU, ACT, AX = mybir.AluOpType, mybir.ActivationFunctionType, mybir.AxisListType

P = 128
S, D = 256, 1024
TILES, KD = S // P, D // P
HALVES = D // 512
EPS, LN_EPS = 1e-6, 1e-5
NEG = -1e30
THETA = 500000.0

AH, AKV, HD = 6, 2, 128
GROUP = AH // AKV
LW, LB = 768, 6
CONV = 4
MH = 4
PH, PK, TOPK = 8, 128, 16
PICKS = PH * TOPK
SH, SKV, MH2, HD2 = 12, 3, 4, 64
FF = 2816
FC = FF // P
NE = 8
ALPHA = 4.0 ** 0.25
SCALE2 = HD2 ** -0.5

C_Q, C_K, C_V, C_XL, C_GL, C_QM, C_G = 0, 6, 8, 10, 16, 22, 26
N_IN = 50

RING, UNIT = 6, KD * 512
BANKS = 8
UV = 8

COLS = {}
_at = 0
for _name, _n in (("gate_b", 24), ("conv_w", CONV * LB), ("conv_b", LB), ("lru_br", 12), ("lru_bi", 12), ("lam", 12),
                  ("sink", AH), ("sink2", SH), ("b_router", NE), ("b_forget", 1), ("w_forget", KD * SH),
                  ("w_router", KD * NE)):
    COLS[_name] = (_at, _n)
    _at += _n
N_COLS = _at
CONST = {}
_at = 0
for _name, _n in (("ident", P), ("rot1", P), ("rot2", P), ("iota", P), ("freq1", 1), ("freq2", 1),
                  ("band", TILES * S), ("chunks", TILES * S), ("causal", TILES * S)):
    CONST[_name] = (_at, _n)
    _at += _n
N_CONST = _at


def constants():
    c = np.zeros((P, N_CONST), np.float32)

    def put(name, value):
        at, n = CONST[name]
        c[:, at:at + n] = np.asarray(value, np.float32).reshape(P, n)

    def rotation(head, rot):
        m = np.zeros((P, P), np.float32)
        for base in range(0, P, head):
            for o in range(rot // 2):
                m[base + o + rot // 2, base + o] = -1.0
                m[base + o, base + o + rot // 2] = 1.0
        return m

    def freqs(head, rot):
        f = np.float32(THETA) ** (-np.arange(0, rot, 2, dtype=np.float32) / np.float32(rot))
        out = np.zeros(P, np.float32)
        for base in range(0, P, head):
            out[base:base + rot // 2] = f
            out[base + rot // 2:base + rot] = f
        return out

    put("ident", np.eye(P))
    put("rot1", rotation(HD, HD // 4))
    put("rot2", rotation(HD2, HD2 // 4))
    put("iota", np.broadcast_to(np.arange(P), (P, P)))
    put("freq1", freqs(HD, HD // 4))
    put("freq2", freqs(HD2, HD2 // 4))
    q = np.arange(S).reshape(TILES, P).T[:, :, None]
    k = np.arange(S)[None, None, :]
    put("band", np.where(np.abs(q - k) <= 128, 0.0, NEG))
    put("chunks", np.where((k // 64 <= q // 64) & (k // 64 >= q // 64 - 2), 0.0, NEG))
    put("causal", np.where(k <= q, 0.0, NEG))
    return c


class Plan:

    def __init__(self):
        self.products, self.nth, self.bank, self.freed = [], {}, {}, {}
        self.count = {"vector": 0, "scalar": 0}
        self.units, self.unit = [], {}
        self.loaded = [0] * RING
        self.at = 0

    def product(self, name, by):
        self.bank[name] = len(self.products) % BANKS
        self.products.append(name)
        self.nth[name] = len(self.products)
        self.count[by] += 1
        self.freed[name] = (by, self.count[by])

    def add_unit(self, name, loads, last):
        slot = self.at % RING
        self.loaded[slot] += 16 * len(loads)
        before = [u for u in self.units if u[1] == slot]
        self.units.append((name, slot, loads, last, before[-1][3] if before else None))
        self.unit[name] = (slot, self.loaded[slot])
        self.at += 1


HEADS = []
PEER_AT = "peer"


def make_plan():
    pl = Plan()
    pr = pl.product
    heads = []

    def transposed(tag):
        for k in range(KD):
            pr((tag, k), "scalar")

    def attention(kinds):
        base = len(heads)
        heads.extend(kinds)
        n = len(kinds)
        for i in range(n + 2):
            if i < n:
                pr(("S", base + i), "vector")
            if 1 <= i <= n:
                pr(("T", base + i - 1), "scalar")
            if i >= 2:
                pr(("V", base + i - 2), "vector")
        return base

    transposed("memT")
    for c in range(MH):
        pr(("km", c), "scalar")
    for t in range(TILES):
        pr(("vm", t), "scalar")
    transposed("hT")
    for c in range(C_V):
        pr(("in", c), "scalar")
        if c >= 1:
            pr(("rope", c - 1), "vector")
    for t in range(TILES):
        pr(("v", t), "scalar")
        if t == 0:
            pr(("rope", C_V - 1), "vector")
    for c in range(C_XL, N_IN):
        pr(("in", c), "scalar")
    pl.att1 = attention([("self1", h) for h in range(AH)] + [("mem1", h) for h in range(MH)])
    for d in range(2):
        for b in range(LB):
            pr(("lru", d, b), "scalar")
    for br in range(3):
        for c in range(KD):
            pr(("merge", br, c), "vector")
    for t in range(TILES):
        for h in range(HALVES):
            pr(("out1", t, h), "vector")
    transposed("h2T")
    for c in range(2 * PH):
        pr(("pq", c), "scalar")
    for t in range(TILES):
        for g in range(4):
            pr(("sc", t, g), "scalar")
    pl.before_peer = len(pl.products)
    transposed("x2T")
    pl.att2 = []
    for layer in range(2):
        for c in range(2):
            pr(("km2", layer, c), "vector")
        for t in range(TILES):
            pr(("vm2", layer, t), "scalar")
        nk = SKV if layer == 0 else SH // 2
        for c in range(SH // 2 + nk):
            pr(("in2", layer, c), "scalar")
            if c >= 1:
                if layer == 0:
                    pr(("rope2", c - 1), "vector")
        if layer == 0:
            pr(("rope2", SH // 2 + nk - 1), "vector")
        for t in range(TILES):
            for h in range(1 + layer):
                pr(("v2", layer, t, h), "scalar")
        for c in range(2):
            pr(("qm2", layer, c), "scalar")
        if layer == 1:
            pr(("forget",), "vector")
        kind = ("swa", "fox")[layer]
        pl.att2.append(attention([(kind, h) for h in range(SH)] + [("mem2", h) for h in range(MH2)]))
        for t in range(TILES):
            for h in range(HALVES):
                pr(("out2", layer, t, h), "vector")
        transposed(("aT", layer))
        if layer == 0:
            for f in range(FC):
                pr(("ff", f), "vector")
            for t in range(TILES):
                for h in range(HALVES):
                    pr(("down", t, h), "vector")
            transposed("x3T")
        else:
            for t in range(TILES):
                pr(("router", t), "vector")
            pr(("place",), "vector")
    pl.heads = heads
    return pl


def two_blocks(nc, a):
    pl = make_plan()
    ctx = ExitStack()
    sem = lambda name: ctx.enter_context(nc.semaphore(name))
    sb = lambda name, n, dt=F32: ctx.enter_context(nc.sbuf_tensor(name, [P, n], dt))

    def cols_of(w, c0, n):
        return w.rearrange("(k p) n -> p k n", p=P)[:, :, c0:c0 + n]

    def rows_of(w, k0, nk):
        return w.rearrange("(k p) n -> p k n", p=P)[:, k0:k0 + nk, :]

    for u in range(2):
        pl.add_unit(("mem_kv", u), [(0, KD, 512, cols_of(a["w_mem_kv"][0], 512 * u, 512))],
                    [("km", MH - 1), ("vm", TILES - 1)][u])
    for u in range(13):
        n = min(512, N_IN * P - 512 * u)
        last = ("in", min(4 * u + 3, N_IN - 1)) if u != 2 else ("in", 11)
        pl.add_unit(("w_in", u), [(0, KD, n, cols_of(a["w_in"][0], 512 * u, n))], last)
    pl.add_unit("lru_w", [(0, 12, P, a["lru_wr"][0].rearrange("d h c e -> c (d h) e")),
                          (12 * P, 12, P, a["lru_wi"][0].rearrange("d h c e -> c (d h) e"))], ("lru", 1, LB - 1))
    for br, (name, nk) in enumerate((("p_attn", AH), ("p_lru", LB), ("p_mem", MH))):
        for u in range(2):
            pl.add_unit((name, u), [(0, nk, 512, cols_of(a[name][0], 512 * u, 512))], ("merge", br, 4 * u + 3))
    for u in range(HALVES):
        pl.add_unit(("w_out", u), [(0, KD, 512, cols_of(a["w_out"][0], 512 * u, 512))], ("out1", TILES - 1, u))
    for u in range(4):
        pl.add_unit(("peer_q", u), [(0, KD, 512, cols_of(a["w_peer_q"][0], 512 * u, 512))], ("pq", 4 * u + 3))
    pl.add_unit("sub_keys", [(0, 2 * PH, PK, a["sub_keys_T"])], ("sc", TILES - 1, 3))
    for layer in range(2):
        pl.add_unit(("mem_kv2", layer), [(0, KD, 512, cols_of(a["w_mem_kv_2"][layer], 0, 512))],
                    ("vm2", layer, TILES - 1))
        w = a["w_swa"] if layer == 0 else a["w_in_fox_2"][0]
        width = w.shape[1] // P * P
        for u in range(-(-width // 512)):
            n = min(512, width - 512 * u)
            if layer == 0:
                last = (("in2", 0, 3), ("in2", 0, 7), ("v2", 0, 1, 0), ("qm2", 0, 1))[u]
            else:
                last = (("in2", 1, 3), ("in2", 1, 7), ("in2", 1, 11), ("v2", 1, 1, 0), ("qm2", 1, 1))[u]
            pl.add_unit(("w_in2", layer, u), [(0, KD, n, cols_of(w, 512 * u, n))], last)
        for u in range(HALVES):
            pl.add_unit(("w_out2", layer, u), [(0, KD, 512, cols_of(a["w_out_2"][layer], 512 * u, 512))],
                        ("out2", layer, TILES - 1, u))
        if layer == 0:
            ff_loads(pl, a)
    pl.at += -pl.at % RING

    OUT_ROWS = [3] * 6 + [4]
    e_units = [2] * (FC // 2) + [1] * len(OUT_ROWS)
    N_EU = len(e_units)
    assert N_EU % RING == 0
    e_loaded, per_expert = [], [0] * RING
    for j, n in enumerate(e_units):
        per_expert[j % RING] += 16 * n
        e_loaded.append(per_expert[j % RING])
    G0, G1, PT, UP0 = 0, 1, 2, 3
    PART0 = UP0 + FC // 2
    Y0 = PART0 + len(OUT_ROWS) - 1
    SUM0 = Y0 + HALVES
    N_EP = SUM0 + TILES * HALVES

    ring = sb("weight_ring", RING * UNIT)
    slot = lambda s: ring[:, s * UNIT:(s + 1) * UNIT]
    const = sb("constants", N_CONST)
    cols = sb("columns", N_COLS)
    C = lambda name: const[:, CONST[name][0]:sum(CONST[name])]
    col = lambda name, i=0, n=1: cols[:, COLS[name][0] + i:COLS[name][0] + i + n]
    ident = C("ident")
    tok = lambda ap: ap.rearrange("p (t n) -> p t n", t=TILES)
    x_tok = tok(sb("x_tok", TILES * D)[:, :])
    actT_flat = sb("actT", KD * S)
    actT = actT_flat[:, :].rearrange("p (k s) -> p k s", k=KD)
    work_flat = sb("work_tok", TILES * D)
    work = tok(work_flat[:, :])
    rows = sb("rows", 2 * D)[:, :].rearrange("p (r n) -> p r n", r=2)
    small = sb("small", 96)
    n_small = [0]

    def cell(n):
        n_small[0] += n
        assert n_small[0] <= 96
        return small[:, n_small[0] - n:n_small[0]]

    REGION = 17920
    region = sb("region", REGION)
    top = [0]

    def area(n, inner=None, dt=None):
        v = region[:, top[0]:top[0] + n]
        top[0] += n
        assert top[0] <= REGION, top[0]
        if dt is not None:
            v = v.bitcast(dt)
        return v if inner is None else v.rearrange("p (a b) -> p a b", b=inner)

    def attention_scratch():
        return [area(512, S) for _ in range(2)], [area(512, S) for _ in range(2)], [area(512, S) for _ in range(2)]

    s_buf, p_buf, pt_buf = attention_scratch()
    lru_ri = region[:, 0:12 * S].rearrange("p (b g s) -> p b g s", b=LB, g=2)
    lru_a = actT_flat[:, 0:LB * S].rearrange("p (b s) -> p b s", b=LB)
    xc = work_flat[:, 0:LB * S].rearrange("p (b s) -> p b s", b=LB)
    qa, ka, va = area(AH * S, S), area(AKV * S, S), area(TILES * AKV * HD, AKV * HD)
    xl, gl = area(LB * S, S), area(LB * S, S)
    qm, km, vm = area(MH * S, S), area(MH * S, S), area(TILES * MH * HD, MH * HD)
    gates = area(24 * S, S)
    rope_cos, rope_sin = region[:, 0:S], region[:, S:2 * S]
    ang, turns, rope_t = region[:, 2 * S:3 * S], region[:, 3 * S:4 * S], region[:, 4 * S:6 * S].rearrange("p (b s) -> p b s", b=2)
    pos_i = region[:, 6 * S:7 * S].bitcast(I32)

    top[0] = 0
    idx_all = area(TILES * PICKS, PICKS, I32)
    gate_all = area(TILES * PICKS, PICKS)
    stage = area(TILES * TOPK, TOPK, I32)
    u_dot, u_act, pick_w = area(TILES * TOPK, TOPK), area(TILES * TOPK, TOPK), area(TILES * TOPK, TOPK)
    NDIAG = 4
    diag = area(NDIAG * P, P)
    uv_base = top[0]
    u_ring, v_ring = area(UV * D, D), area(UV * D, D)
    top[0] = uv_base
    pq = area(2 * PH * S, S)
    sc = area(TILES * 2 * PH * PK).rearrange("p (t c k) -> p t c k", t=TILES, k=PK)
    sc_less = area(PK)
    top_v, top_u = area(2 * PH * TOPK, TOPK), area(2 * PH * TOPK, TOPK, U32)
    top_f = area(2 * PH * TOPK, TOPK)
    cand, cand_less = area(S), area(S)
    best, best_u = area(PICKS, TOPK), area(PICKS, TOPK, U32)
    half_u, half_f = area(2 * PICKS, PICKS, U32), area(2 * PICKS, PICKS)
    hot = area(PICKS * TOPK).rearrange("p (h k c) -> p h k c", h=PH, c=TOPK)
    key_f = area(2 * PICKS, PICKS)
    idx_f = area(PICKS)
    best_e = area(PICKS, TOPK)

    top[0] = 0
    attention_scratch()
    mem2T = region[:, REGION - KD * S:REGION].rearrange("p (k s) -> p k s", k=KD)
    q2, qm2 = area(SH // 2 * S, S), area(2 * S, S)
    kz = area(SH * S, S)
    kmz = area(MH2 * S, S)
    v2, vm2 = area(TILES * SH * HD2, SH * HD2), area(TILES * MH2 * HD2, MH2 * HD2)
    k_raw = area(2 * S, S)
    f_log, f_cum, f_tmp = area(S), area(S), area(S)
    ffT = region[:, 0:FC * S].rearrange("p (f s) -> p f s", f=FC)
    silu_ff = region[:, FC * S:(FC + 2) * S].rearrange("p (b s) -> p b s", b=2)
    assert (FC + 2) * S <= top[0] <= REGION - KD * S
    top[0] = 0
    pick = area(TILES * P, P)
    pickg = area(TILES * P, P)
    pickT = area(TILES * P, P)
    xeT = area(KD * P, P)
    silu_e = area(2 * 2 * P).rearrange("p (b f s) -> p b f s", b=2, f=2)
    geT = area(FC * P, P)
    ye = area(D)
    logits, r_gate, r_mask, r_slot, r_hot = (area(TILES * NE, NE) for _ in range(5))
    r_top, r_idx, r_idxf = area(TILES * 8, 8), area(TILES * 8, 8, U32), area(TILES * 8, 8)
    r_e, r_den, r_g = area(TILES), area(TILES), area(TILES * 2, 2)
    r_shift = area(2)
    count_i = area(NE, None, I32)
    ones, before = area(P), area(P)

    stat, rstd = cell(2), cell(2)
    bn, mv = cell(TILES * 12), cell(TILES * 2)
    nmax, esum, esink, den = cell(4), cell(4), cell(4), cell(4)
    sp_e, sp_z, sp_p = cell(12), cell(12), cell(12)
    psum = ctx.enter_context(nc.psum_tensor("psum", [P, BANKS, 512], F32))

    weight_in = [sem(f"weight_in{s}") for s in range(RING)]
    product_ready = sem("product_ready")
    freed = {"vector": sem("freed_by_vector"), "scalar": sem("freed_by_scalar")}
    x_in, const_in, mem_in, pos_in, mem2_in = (sem(n) for n in ("x_in", "const_in", "mem_in", "pos_in", "mem2_in"))
    row_in = [sem("row_in0"), sem("row_in1")]
    row_used = sem("row_used")
    vector_step, scalar_step, pool_step = sem("vector_step"), sem("scalar_step"), sem("pool_step")
    square_ready, root_ready, normed = sem("square_ready"), sem("root_ready"), sem("normed")
    angle_ready, table_ready, rope_ready = sem("angle_ready"), sem("table_ready"), sem("rope_ready")
    max_ready, exp_ready, probs_ready = sem("max_ready"), sem("exp_ready"), sem("probs_ready")
    lam_exp, lam_ready, conv_ready = sem("lam_exp"), sem("lam_ready"), sem("conv_ready")
    lru_at, lru_sq_in, lru_sq_out, lru_done = sem("lru_at"), sem("lru_sq_in"), sem("lru_sq_out"), sem("lru_done")
    merged = sem("merged")
    best_ready, best_exp = sem("best_ready"), sem("best_exp")
    search_done, staged, gathers = sem("search_done"), sem("staged"), sem("gathers")
    u_in, v_in = [sem(f"u_in{k}") for k in range(UV)], [sem(f"v_in{k}") for k in range(UV)]
    dots_done, gelu_done, weights_done, diag_done = (sem(n) for n in ("dots_done", "gelu_done", "pick_weights_done", "diag_done"))
    v_used, peer_sum, peer_added = sem("v_used"), sem("peer_sum"), sem("peer_added")
    zeros_ready, forget_exp, forget_e, cum_ready = (sem(n) for n in ("zeros_ready", "forget_exp", "forget_e", "cum_ready"))
    silu_ready, ff_ready, ff_out_used = sem("silu_ready"), sem("ff_ready"), sem("ff_out_used")
    router_exp, router_e, routed, picked = (sem(n) for n in ("router_exp", "router_e", "routed", "picked"))
    e_product = sem("expert_product")
    e_freed = {"vector": sem("expert_freed_by_vector"), "scalar": sem("expert_freed_by_scalar")}
    e_silu, pick_step = sem("expert_silu"), sem("pick_step")
    out_done = sem("out_done")

    rows_order = ["g_mem", "g_mix", "g_ffn", "g_final"]
    for layer in range(2):
        for part in ("attn", "ffn"):
            rows_order += [("ln_" + part + "_g_2", layer), ("ln_" + part + "_b_2", layer)]

    heads = pl.heads
    N1 = len([h for h in heads if h[0] in ("self1", "mem1")])

    def wait_product(eng, name):
        eng.wait_ge(product_ready, pl.nth[name])
        return psum[:, pl.bank[name], :]

    def wait_freed(eng, name):
        by, n = pl.freed[name]
        eng.wait_ge(freed[by], n)

    def wait_row(eng, i):
        eng.wait_ge(row_in[i % 2], 16 * (i // 2 + 1))
        return rows[:, i % 2, :]

    class Own:

        def __init__(self, eng, s):
            self.eng, self.s, self.n = eng, s, 0

        def __call__(self, ins):
            self.n += 1
            ins.then_inc(self.s, 1)
            self.eng.wait_ge(self.s, self.n)

    E_BANK = {G0: 4, G1: 5, PT: 6}
    for n in range(FC // 2):
        E_BANK[UP0 + n] = n % 4
    E_BANK[Y0], E_BANK[Y0 + 1] = 6, 7
    for n in range(TILES * HALVES):
        E_BANK[SUM0 + n] = 4 + n % 2
    E_BY = {G0: "scalar", G1: "scalar", PT: "scalar", Y0: "scalar", Y0 + 1: "scalar"}
    for j in list(range(UP0, PART0)) + list(range(SUM0, N_EP)):
        E_BY[j] = "vector"
    E_NTH, e_n = {}, {"vector": 0, "scalar": 0}
    for j in sorted(E_BANK):
        e_n[E_BY[j]] += 1
        E_NTH[j] = e_n[E_BY[j]]
    E_PREV = {}
    for j in E_BANK:
        same = [i for i in sorted(E_BANK) if E_BANK[i] == E_BANK[j]]
        at = same.index(j)
        E_PREV[j] = (same[at - 1], 0) if at else (same[-1], 1)

    def each_expert(eng, body, skip, prepare=None):
        with eng.Fori(0, NE) as e:
            body(e, e, False)
        with eng.Fori(0, NE) as e:
            n = eng.value_load(count_i[0:1, bass.ds(e, 1)], min_val=0, max_val=S)
            with eng.If(n > P):
                body(e, e + NE, True)
            with eng.Else():
                skip(e + NE)

    block = ctx.enter_context(nc.Block())

    @block.sync
    def _(sp):
        sp.dma_start(work[:, :, :], a["mem"][0].rearrange("(t p) n -> p t n", p=P)).then_inc(mem_in, 16)
        sp.dma_start(const[:, :], a["constants"]).then_inc(const_in, 16)
        sp.dma_start(cols[:, :], a["columns"]).then_inc(const_in, 16)
        sp.dma_start(x_tok[:, :, :], a["x"][0].rearrange("(t p) n -> p t n", p=P)).then_inc(x_in, 16)
        for name, s, loads, _, before in pl.units:
            if before is not None:
                if before[0] == "ff_out_used":
                    sp.wait_ge(ff_out_used, before[1] + 1)
                else:
                    sp.wait_ge(product_ready, pl.nth[before])
            for at, nk, n, src in loads:
                sp.dma_start(slot(s)[:, at:at + nk * n].rearrange("p (k n) -> p k n", k=nk), src).then_inc(weight_in[s], 16)
        sp.wait_ge(product_ready, len(pl.products))
        sp.wait_ge(routed, 1)

        def expert_loads(e, b, over):
            for j in range(N_EU):
                s = j % RING
                if j >= RING:
                    sp.wait_ge(e_product, b * N_EP + last_use(j - RING) + 1 + N_EP)
                else:
                    sp.wait_ge(e_product, b * N_EP + last_use(j - RING + N_EU) + 1)
                if j < FC // 2:
                    w = a["w_exp_in_2"][0][bass.ds(e, 1), :, :].rearrange("e (k p) n -> p (e k) n", p=P)
                    for half in range(2):
                        sp.dma_start(slot(s)[:, half * 8 * S:(half + 1) * 8 * S].rearrange("p (k n) -> p k n", k=KD),
                                     w[:, :, half * FF + S * j:half * FF + S * (j + 1)]).then_inc(weight_in[s], 16)
                else:
                    o = j - FC // 2
                    w = a["w_exp_out_2"][0][bass.ds(e, 1), :, :].rearrange("e (k p) n -> p (e k) n", p=P)
                    sp.dma_start(slot(s)[:, 0:OUT_ROWS[o] * D].rearrange("p (k n) -> p k n", n=D),
                                 w[:, 3 * o:3 * o + OUT_ROWS[o], :]).then_inc(weight_in[s], 16)

        def last_use(j):
            if j < FC // 2:
                return UP0 + j
            return PART0 + j - FC // 2 if j < N_EU - 1 else Y0 + 1

        def skip(b):
            for s in range(RING):
                sp.wait_ge(weight_in[s], b * per_expert[s] + pl.loaded[s])
                sp.sem_inc(weight_in[s], per_expert[s])

        each_expert(sp, expert_loads, skip)
        sp.wait_ge(normed, 8 * TILES)
        sp.dma_start(a["out"].rearrange("b (t p) n -> p (b t) n", p=P), x_tok[:, :, :]).then_inc(out_done, 16)
        sp.wait_ge(out_done, 16)

    @block.gpsimd
    def _(pool):
        own = Own(pool, pool_step)
        pool.dma_start(pos_i, a["positions"][0].partition_broadcast(P)).then_inc(pos_in, 16)

        def load_row(i):
            if i >= 2:
                pool.wait_ge(row_used, i - 1)
            name = rows_order[i]
            src = a[name[0]][name[1]] if isinstance(name, tuple) else (a[name] if name == "g_final" else a[name][0])
            pool.dma_start(rows[:, i % 2, :], src.partition_broadcast(P)).then_inc(row_in[i % 2], 16)

        for i in range(4):
            load_row(i)
        pool.wait_ge(search_done, TILES)
        with pool.Fori(0, PH) as h:
            for t in range(TILES):
                it = h * TILES + t
                pool.wait_ge(v_used, it * TOPK + 1)
                pool.tensor_copy(stage[:, t, :], idx_all[:, t, bass.ds(h * TOPK, TOPK)]).then_inc(staged, 1)
                pool.wait_ge(staged, it + 1)
                for k in range(TOPK):
                    if k >= UV:
                        pool.wait_ge(dots_done, it * TOPK + k - UV + 2)
                    else:
                        pool.wait_ge(dots_done, it * TOPK + 1)
                    pool.sem_inc(gathers, 1)
                    pool.indirect_dma_start(u_ring[:, k % UV, :], None, a["peer_u"][0],
                                            bass.IndirectOffsetOnAxis(stage[:, t, k:k + 1], 0)).then_inc(u_in[k % UV], 16)
                for k in range(TOPK):
                    if k >= UV:
                        pool.wait_ge(v_used, it * TOPK + k - UV + 2)
                        pool.sem_inc(gathers, 1)
                    pool.indirect_dma_start(v_ring[:, k % UV, :], None, a["peer_v"][0],
                                            bass.IndirectOffsetOnAxis(stage[:, t, k:k + 1], 0)).then_inc(v_in[k % UV], 16)
        pool.wait_ge(peer_added, 1 + HALVES * TILES * PH)
        pool.dma_start(mem2T[:, :, :], a["mem_2_T"].rearrange("(k p) s -> p k s", p=P)).then_inc(mem2_in, 16)
        pool.dma_start(pos_i, a["positions_2"][0].partition_broadcast(P)).then_inc(pos_in, 16)
        for i in range(4, len(rows_order)):
            load_row(i)

    @block.scalar
    def _(act):
        own = Own(act, scalar_step)

        def give(ins, name):
            ins.then_inc(freed["scalar"], 1)
            assert pl.freed[name] == ("scalar", give.n + 1), name
            give.n += 1

        give.n = 0

        def copy_out(name, dst, func=ACT.Copy, n=None, **kw):
            src = wait_product(act, name)
            n = n or dst.free_size()
            src = src[:, 0:n]
            if len(dst.shape) == 3:
                src = src.rearrange("p (a b) -> p a b", b=dst.shape[2])
            give(act.activation(dst, src, func, **kw), name)

        n_root = [0]

        def root():
            n_root[0] += 1
            act.wait_ge(square_ready, n_root[0])
            act.activation(rstd, stat, ACT.Sqrt).then_inc(root_ready, 1)

        def transposed(tag):
            for k in range(KD):
                copy_out((tag, k), actT[:, k, :])

        def rope_tables(i):
            act.wait_ge(angle_ready, 2 * i + 1)
            act.activation(rope_sin, ang, ACT.Sin).then_inc(table_ready, 1)
            act.wait_ge(angle_ready, 2 * i + 2)
            act.activation(rope_cos, turns, ACT.Sin).then_inc(table_ready, 1)

        def attention(base, n):
            for i in range(n + 2):
                if i < n:
                    g = base + i
                    b = g % 2
                    kind, h = heads[g]
                    act.wait_ge(max_ready, g + 1)
                    for t in range(TILES):
                        ins = act.activation(p_buf[b][:, t, :], s_buf[b][:, t, :], ACT.Exp, bias=nmax[:, 2 * b + t:2 * b + t + 1],
                                             accum_out=esum[:, 2 * b + t:2 * b + t + 1])
                    if kind in ("self1", "swa"):
                        sink = col("sink" if kind == "self1" else "sink2", h)
                        ins = act.activation(esink[:, 2 * b:2 * b + 2], nmax[:, 2 * b:2 * b + 2], ACT.Exp, bias=sink)
                    ins.then_inc(exp_ready, 1)
                if 1 <= i <= n:
                    g = base + i - 1
                    copy_out(("T", g), pt_buf[g % 2])

        root()
        transposed("memT")
        act.wait_ge(const_in, 32)
        for c in range(MH):
            copy_out(("km", c), km[:, c, :])
        for t in range(TILES):
            copy_out(("vm", t), vm[:, t, :])
        root()
        transposed("hT")
        rope_tables(0)
        for c in range(C_V):
            copy_out(("in", c), qa[:, c, :] if c < C_K else ka[:, c - C_K, :])
        for t in range(TILES):
            copy_out(("v", t), va[:, t, :])
        for c in range(C_XL, C_GL):
            copy_out(("in", c), xl[:, c - C_XL, :])
        for c in range(C_GL, C_QM):
            copy_out(("in", c), gl[:, c - C_GL, :], ACT.Gelu_apprx_tanh)
        for c in range(C_QM, C_G):
            copy_out(("in", c), qm[:, c - C_QM, :])
        for c in range(C_G, N_IN):
            copy_out(("in", c), gates[:, c - C_G, :], ACT.Sigmoid, bias=col("gate_b", c - C_G))
        attention(0, N1)
        act.wait_ge(lam_exp, 1)
        act.activation(sp_e, sp_z, ACT.Exp).then_inc(lam_exp, 1)
        act.wait_ge(lam_ready, 1)
        for d in range(2):
            if d:
                act.wait_ge(lru_done, 1)
            for b in range(LB):
                bank = wait_product(act, ("lru", d, b))
                act.activation(lru_ri[:, b, 0, :], bank[:, 0:S], ACT.Sigmoid, bias=col("lru_br", d * LB + b))
                give(act.activation(lru_ri[:, b, 1, :], bank[:, S:2 * S], ACT.Sigmoid, bias=col("lru_bi", d * LB + b)),
                     ("lru", d, b))
            act.wait_ge(freed["scalar"], pl.freed[("lru", d, LB - 1)][1])
            for b in range(LB):
                own(act.activation(lru_a[:, b, :], lru_ri[:, b, 0, :], ACT.Exp, scale=sp_e[:, d * LB + b:d * LB + b + 1]))
                act.activation(lru_ri[:, b, 0, :], lru_ri[:, b, 0, :], ACT.Tanh,
                               scale=sp_p[:, d * LB + b:d * LB + b + 1]).then_inc(lru_at, 1)
            for b in range(LB):
                act.wait_ge(lru_sq_in, d * LB + b + 1)
                act.activation(lru_ri[:, b, 0, :], lru_ri[:, b, 0, :], ACT.Sqrt).then_inc(lru_sq_out, 1)
        root()
        transposed("h2T")
        for c in range(2 * PH):
            copy_out(("pq", c), pq[:, c, :])
        for t in range(TILES):
            for g in range(4):
                copy_out(("sc", t, g), sc[:, t, 4 * g:4 * g + 4, :])
        for t in range(TILES):
            for h in range(PH):
                n = t * PH + h
                act.wait_ge(best_ready, n + 1)
                act.activation(best_e[:, h, :], best[:, h, :], ACT.Exp, accum_out=esum[:, h % 4:h % 4 + 1]).then_inc(best_exp, 1)
        act.sem_inc(gelu_done, 1)
        act.sem_inc(diag_done, 1)
        with act.Fori(0, PH) as h:
            for t in range(TILES):
                it = h * TILES + t
                act.wait_ge(dots_done, it * TOPK + TOPK + 1)
                act.activation(u_act[:, t, :], u_dot[:, t, :], ACT.Gelu_apprx_tanh).then_inc(gelu_done, 1)
                act.wait_ge(weights_done, it + 1)
                for k in range(TOPK):
                    if k >= NDIAG:
                        act.wait_ge(v_used, it * TOPK + k - NDIAG + 2)
                    else:
                        act.wait_ge(v_used, it * TOPK + 1)
                    act.activation(diag[:, k % NDIAG, :], ident, ACT.Copy, scale=pick_w[:, t, k:k + 1]).then_inc(diag_done, 1)
        root()
        transposed("x2T")
        rope_tables(1)
        for layer in range(2):
            for t in range(TILES):
                copy_out(("vm2", layer, t), vm2[:, t, :])
            nk = SKV if layer == 0 else SH // 2
            for c in range(SH // 2 + nk):
                name = ("in2", layer, c)
                if c < SH // 2:
                    copy_out(name, q2[:, c, :])
                elif layer == 0:
                    if c >= SH // 2 + 2:
                        act.wait_ge(rope_ready, C_V + c - 1)
                    copy_out(name, k_raw[:, c % 2, :])
                else:
                    bank = wait_product(act, name)
                    j = 2 * (c - SH // 2)
                    act.wait_ge(zeros_ready, 2)
                    act.activation(kz[0:HD2, j, :], bank[0:HD2, 0:S], ACT.Copy)
                    give(act.activation(kz[HD2:P, j + 1, :], bank[HD2:P, 0:S], ACT.Copy), name)
            for t in range(TILES):
                if layer == 0:
                    copy_out(("v2", 0, t, 0), v2[:, t, 0:2 * SKV * HD2])
                else:
                    copy_out(("v2", 1, t, 0), v2[:, t, 0:512])
                    copy_out(("v2", 1, t, 1), v2[:, t, 512:SH * HD2])
            for c in range(2):
                copy_out(("qm2", layer, c), qm2[:, c, :])
            if layer == 1:
                act.wait_ge(forget_exp, 1)
                own(act.activation(f_tmp[0:SH, :], f_tmp[0:SH, :], ACT.Exp))
                act.activation(f_tmp[0:SH, :], f_tmp[0:SH, :], ACT.Ln, bias=1.0).then_inc(forget_e, 1)
            attention(pl.att2[layer], SH + MH2)
            root()
            transposed(("aT", layer))
            if layer == 0:
                for f in range(FC):
                    bank = wait_product(act, ("ff", f))
                    if f >= 2:
                        act.wait_ge(ff_ready, f - 1)
                    act.activation(silu_ff[:, f % 2, :], bank[:, 0:S], ACT.Silu).then_inc(silu_ready, 1)
                root()
                transposed("x3T")
        act.wait_ge(router_exp, 1)
        act.activation(r_e, r_e, ACT.Exp).then_inc(router_e, 1)
        act.wait_ge(routed, 1)

        def wait_e(j, b):
            act.wait_ge(e_product, b * N_EP + j + 1 + N_EP)
            return psum[:, E_BANK[j], :]

        def expert(e, b, over):
            for j in (G0, G1):
                act.activation(xeT[:, 4 * j:4 * j + 4, :], wait_e(j, b).rearrange("p (k s) -> p k s", k=4), ACT.Copy)\
                   .then_inc(e_freed["scalar"], 1)
            act.activation(pickT[:, :, :], wait_e(PT, b)[:, 0:TILES * P].rearrange("p (t s) -> p t s", t=TILES), ACT.Copy)\
               .then_inc(e_freed["scalar"], 1)
            for n in range(FC // 2):
                bank = wait_e(UP0 + n, b).rearrange("p (f g s) -> p f g s", f=2, g=2)
                act.wait_ge(e_freed["vector"], b * e_n["vector"] + (e_n["vector"] + E_NTH[UP0 + n - 2] if n >= 2
                            else E_NTH[PART0 - 1 - n]))
                act.activation(silu_e[:, n % 2, :, :], bank[:, :, 0, :], ACT.Silu).then_inc(e_silu, 1)
            for h in range(HALVES):
                act.activation(ye[:, 512 * h:512 * h + 512], wait_e(Y0 + h, b), ACT.Copy).then_inc(e_freed["scalar"], 1)

        def skip(b):
            act.wait_ge(e_freed["scalar"], b * e_n["scalar"] + e_n["scalar"])
            act.sem_inc(e_freed["scalar"], e_n["scalar"])
            act.wait_ge(e_silu, b * (FC // 2))
            act.sem_inc(e_silu, FC // 2)

        act.sem_inc(e_freed["scalar"], e_n["scalar"])
        each_expert(act, expert, skip)
        root()

    @block.tensor
    def _(pe):
        def begin(name):
            i = pl.nth[name] - 1
            if i >= BANKS:
                wait_freed(pe, pl.products[i - BANKS])
            return psum[:, pl.bank[name], :]

        def end(ins, name):
            assert pl.nth[name] == end.n + 1, name
            end.n += 1
            ins.then_inc(product_ready, 1)

        end.n = 0

        def unit(name, nk, n, at=0):
            s, count = pl.unit[name]
            pe.wait_ge(weight_in[s], count)
            return slot(s)[:, at:at + nk * n].rearrange("p (k n) -> p k n", k=nk)

        def transposes(tag, src, nth):
            pe.wait_ge(normed, 2 * nth)
            for k in range(KD):
                bank = begin((tag, k))
                for t in range(TILES):
                    ins = pe.transpose(bank[:, t * P:(t + 1) * P], src[:, t, k * P:(k + 1) * P], ident)
                end(ins, (tag, k))

        def feature_major(name, w, c, src, nk):
            bank = begin(name)
            for k in range(nk):
                ins = pe.matmul(bank[:, 0:S], w[:, k, c * P:(c + 1) * P], src[:, k, :], start=(k == 0), stop=(k == nk - 1))
            end(ins, name)

        def token_major(name, w, t, n0, n, src, nk=KD):
            bank = begin(name)
            for k in range(nk):
                ins = pe.matmul(bank[:, 0:n], src[:, k, t * P:(t + 1) * P], w[:, k, n0:n0 + n], start=(k == 0), stop=(k == nk - 1))
            end(ins, name)

        def turn(name, rot, src, after):
            wait_freed(pe, after)
            end(pe.matmul(begin(name)[:, 0:S], C(rot), src, start=True, stop=True), name)

        def attention(base, n, queries, keys, values):
            for i in range(n + 2):
                if i < n:
                    g = base + i
                    kind, h = heads[g]
                    bank = begin(("S", g))
                    for t in range(TILES):
                        fox = kind == "fox"
                        ins = pe.matmul(bank[:, t * S:(t + 1) * S], queries(kind, h)[:, t * P:(t + 1) * P], keys(kind, h),
                                        start=True, stop=not fox)
                        if fox:
                            ins = pe.matmul(bank[:, t * S:(t + 1) * S], ident[0:SH, h:h + 1].to_broadcast([SH, P]), f_cum[0:SH, :],
                                            start=False, stop=True)
                    end(ins, ("S", g))
                if 1 <= i <= n:
                    g = base + i - 1
                    pe.wait_ge(probs_ready, g + 1)
                    bank = begin(("T", g))
                    for k in range(TILES):
                        for t in range(TILES):
                            ins = pe.transpose(bank[:, k * S + t * P:k * S + (t + 1) * P], p_buf[g % 2][:, t, k * P:(k + 1) * P], ident)
                    end(ins, ("T", g))
                if i >= 2:
                    g = base + i - 2
                    bank = begin(("V", g))
                    wait_freed(pe, ("T", g))
                    for k in range(TILES):
                        ins = pe.matmul(bank[:, 0:S], values(*heads[g], k), pt_buf[g % 2][:, k, :], start=(k == 0), stop=(k == TILES - 1))
                    end(ins, ("V", g))

        pe.wait_ge(const_in, 32)
        transposes("memT", work, 1)
        wait_freed(pe, ("memT", KD - 1))
        w = unit(("mem_kv", 0), KD, 512)
        for c in range(MH):
            feature_major(("km", c), w, c, actT, KD)
        w = unit(("mem_kv", 1), KD, 512)
        for t in range(TILES):
            token_major(("vm", t), w, t, 0, 512, actT)
        transposes("hT", work, 2)
        wait_freed(pe, ("hT", KD - 1))
        qk = lambda c: qa[:, c, :] if c < C_K else ka[:, c - C_K, :]
        for c in range(C_V):
            feature_major(("in", c), unit(("w_in", c // 4), KD, 512), c % 4, actT, KD)
            if c >= 1:
                turn(("rope", c - 1), "rot1", qk(c - 1), ("in", c - 1))
        for t in range(TILES):
            token_major(("v", t), unit(("w_in", 2), KD, 512), t, 0, AKV * HD, actT)
            if t == 0:
                turn(("rope", C_V - 1), "rot1", qk(C_V - 1), ("in", C_V - 1))
        for c in range(C_XL, N_IN):
            feature_major(("in", c), unit(("w_in", c // 4), KD, 512 if c < 48 else 256), c % 4, actT, KD)
        pe.wait_ge(rope_ready, C_V)
        attention(0, N1, lambda kind, h: (qa if kind == "self1" else qm)[:, h, :],
                  lambda kind, h: ka[:, h // GROUP, :] if kind == "self1" else km[:, h, :],
                  lambda kind, h, k: va[:, k, h // GROUP * HD:(h // GROUP + 1) * HD] if kind == "self1" else vm[:, k, h * HD:(h + 1) * HD])
        wr, wi = unit("lru_w", 12, P), unit("lru_w", 12, P, 12 * P)
        pe.wait_ge(conv_ready, LB)
        for d in range(2):
            for b in range(LB):
                bank = begin(("lru", d, b))
                pe.matmul(bank[:, 0:S], wr[:, d * LB + b, :], xc[:, b, :], start=True, stop=True)
                end(pe.matmul(bank[:, S:2 * S], wi[:, d * LB + b, :], xc[:, b, :], start=True, stop=True), ("lru", d, b))
        wait_freed(pe, ("V", N1 - 1))
        for br, (name, nk, src) in enumerate((("p_attn", AH, qa), ("p_lru", LB, gl), ("p_mem", MH, qm))):
            if br == 1:
                pe.wait_ge(lru_done, 2)
            for c in range(KD):
                feature_major(("merge", br, c), unit((name, c // 4), nk, 512), c % 4, src, nk)
        pe.wait_ge(merged, KD)
        for t in range(TILES):
            for h in range(HALVES):
                token_major(("out1", t, h), unit(("w_out", h), KD, 512), t, 0, 512, gates)
        transposes("h2T", work, 3)
        wait_freed(pe, ("h2T", KD - 1))
        for c in range(2 * PH):
            feature_major(("pq", c), unit(("peer_q", c // 4), KD, 512), c % 4, actT, KD)
        wait_freed(pe, ("pq", 2 * PH - 1))
        keys = unit("sub_keys", 2 * PH, PK)
        for t in range(TILES):
            for g in range(4):
                bank = begin(("sc", t, g))
                for c in range(4):
                    ins = pe.matmul(bank[:, c * PK:(c + 1) * PK], pq[:, 4 * g + c, t * P:(t + 1) * P], keys[:, 4 * g + c, :],
                                    start=True, stop=True)
                end(ins, ("sc", t, g))
        wait_freed(pe, ("sc", TILES - 1, 3))
        pe.sem_inc(v_used, 1)
        with pe.Fori(0, PH) as h:
            for t in range(TILES):
                it = h * TILES + t
                pe.wait_ge(peer_added, h * TILES * HALVES + 1)
                for k in range(TOPK):
                    pe.wait_ge(diag_done, it * TOPK + k + 2)
                    pe.wait_ge(v_in[k % UV], it * 32 + 16 * (k // UV + 1))
                    for half in range(HALVES):
                        ins = pe.matmul(psum[:, 2 * t + half, :], diag[:, k % NDIAG, :], v_ring[:, k % UV, 512 * half:512 * half + 512],
                                        start=(k == 0), stop=(k == TOPK - 1))
                    ins.then_inc(v_used, 1)
        transposes("x2T", x_tok, 4)
        wait_freed(pe, ("x2T", KD - 1))
        for layer in range(2):
            if layer == 0:
                pe.wait_ge(mem2_in, 16)
            w = unit(("mem_kv2", layer), KD, 512)
            for c in range(2):
                feature_major(("km2", layer, c), w, c, mem2T, KD)
            for t in range(TILES):
                token_major(("vm2", layer, t), w, t, 256, 256, mem2T)
            nk = SKV if layer == 0 else SH // 2
            raw = lambda c: q2[:, c, :] if c < SH // 2 else k_raw[:, c % 2, :]
            if layer == 1:
                wait_freed(pe, ("x3T", KD - 1))
            for c in range(SH // 2 + nk):
                feature_major(("in2", layer, c), unit(("w_in2", layer, c // 4), KD, 512), c % 4, actT, KD)
                if c >= 1 and layer == 0:
                    turn(("rope2", c - 1), "rot2", raw(c - 1), ("in2", 0, c - 1))
            if layer == 0:
                turn(("rope2", SH // 2 + nk - 1), "rot2", raw(SH // 2 + nk - 1), ("in2", 0, SH // 2 + nk - 1))
                for t in range(TILES):
                    token_major(("v2", 0, t, 0), unit(("w_in2", 0, 2), KD, 512), t, P, 3 * P, actT)
                for c in range(2):
                    feature_major(("qm2", 0, c), unit(("w_in2", 0, 3), KD, 256), c, actT, KD)
                pe.wait_ge(rope_ready, C_V + SH // 2 + nk)
            else:
                for t in range(TILES):
                    token_major(("v2", 1, t, 0), unit(("w_in2", 1, 3), KD, 512), t, 0, 512, actT)
                    token_major(("v2", 1, t, 1), unit(("w_in2", 1, 4), KD, 512), t, 0, 256, actT)
                for c in range(2):
                    feature_major(("qm2", 1, c), unit(("w_in2", 1, 4), KD, 512), 2 + c, actT, KD)
                bank = begin(("forget",))
                wf = col("w_forget", 0, KD * SH).rearrange("p (k n) -> p k n", k=KD)
                for k in range(KD):
                    ins = pe.matmul(bank[0:SH, 0:S], wf[:, k, :], actT[:, k, :], start=(k == 0), stop=(k == KD - 1))
                end(ins, ("forget",))
                pe.wait_ge(cum_ready, 1)
            wait_freed(pe, ("qm2", layer, 1))
            attention(pl.att2[layer], SH + MH2,
                      lambda kind, h: qm2[:, h // 2, :] if kind == "mem2" else q2[:, h // 2, :],
                      lambda kind, h: {"swa": lambda: kz[:, 2 * (h // 4) + h % 2, :], "fox": lambda: kz[:, h, :],
                                       "mem2": lambda: kmz[:, h, :]}[kind](),
                      lambda kind, h, k: {"swa": lambda: v2[:, k, h // 4 * P:(h // 4 + 1) * P],
                                          "fox": lambda: v2[:, k, h // 2 * P:(h // 2 + 1) * P],
                                          "mem2": lambda: vm2[:, k, h // 2 * P:(h // 2 + 1) * P]}[kind]())
            wait_freed(pe, ("V", pl.att2[layer] + SH + MH2 - 1))
            for t in range(TILES):
                for h in range(HALVES):
                    token_major(("out2", layer, t, h), unit(("w_out2", layer, h), KD, 512), t, 0, 512, actT)
            transposes(("aT", layer), x_tok, 5 + 2 * layer)
            wait_freed(pe, (("aT", layer), KD - 1))
            if layer == 0:
                for f in range(FC):
                    w = unit(("ff_in", f // 2), 2 * KD, S)
                    bank = begin(("ff", f))
                    for g in range(2):
                        for k in range(KD):
                            ins = pe.matmul(bank[:, g * S:(g + 1) * S], w[:, g * KD + k, f % 2 * P:(f % 2 + 1) * P], actT[:, k, :],
                                            start=(k == 0), stop=(k == KD - 1))
                    end(ins, ("ff", f))
                pe.wait_ge(ff_ready, FC)
                for t in range(TILES):
                    for h in range(HALVES):
                        begin(("down", t, h))
                f = 0
                for o, n in enumerate(OUT_ROWS):
                    w = unit(("ff_out", o), n, D)
                    for k in range(n):
                        for t in range(TILES):
                            for h in range(HALVES):
                                ins = pe.matmul(psum[:, pl.bank[("down", t, h)], :], ffT[:, f, t * P:(t + 1) * P],
                                                w[:, k, 512 * h:512 * h + 512], start=(f == 0), stop=(f == FC - 1))
                                if f == FC - 1:
                                    end(ins, ("down", t, h))
                        f += 1
                    if o < len(OUT_ROWS) - 1:
                        ins.then_inc(ff_out_used, 1)
                transposes("x3T", x_tok, 6)
        wr = col("w_router", 0, KD * NE).rearrange("p (k n) -> p k n", k=KD)
        for t in range(TILES):
            token_major(("router", t), wr, t, 0, NE, actT)
        pe.wait_ge(router_e, 2)
        bank = begin(("place",))
        pe.matmul(bank[:, 0:NE], before, r_mask[:, 0, :], start=True, stop=True)
        pe.matmul(bank[:, NE:2 * NE], before, r_mask[:, 1, :], start=True, stop=False)
        pe.matmul(bank[:, NE:2 * NE], ones, r_mask[:, 0, :], start=False, stop=True)
        pe.matmul(bank[:, 2 * NE:3 * NE], ones, r_mask[:, 0, :], start=True, stop=False)
        end(pe.matmul(bank[:, 2 * NE:3 * NE], ones, r_mask[:, 1, :], start=False, stop=True), ("place",))
        pe.wait_ge(routed, 1)
        wait_freed(pe, ("place",))

        def bank_of(j, b):
            i, back = E_PREV[j]
            by = E_BY[i]
            pe.wait_ge(e_freed[by], b * e_n[by] + E_NTH[i] + (0 if back else e_n[by]))
            return psum[:, E_BANK[j], :]

        def expert_unit(j, b):
            s = j % RING
            pe.wait_ge(weight_in[s], b * per_expert[s] + pl.loaded[s] + e_loaded[j])
            return slot(s)

        def expert(e, b, over):
            pe.wait_ge(picked, b + 1)
            for j in (G0, G1):
                bank = bank_of(j, b)
                for k in range(4):
                    for t in range(TILES):
                        ins = pe.matmul(bank[:, k * P:(k + 1) * P], x_tok[:, t, (4 * j + k) * P:(4 * j + k + 1) * P], pick[:, t, :],
                                        start=(t == 0), stop=(t == TILES - 1))
                ins.then_inc(e_product, 1)
            bank = bank_of(PT, b)
            for t in range(TILES):
                ins = pe.transpose(bank[:, t * P:(t + 1) * P], pickg[:, t, :], ident)
            ins.then_inc(e_product, 1)
            pe.wait_ge(e_freed["scalar"], b * e_n["scalar"] + e_n["scalar"] + E_NTH[G1])
            for n in range(FC // 2):
                bank = bank_of(UP0 + n, b)
                w = expert_unit(n, b).rearrange("p (g k f s) -> p g k f s", g=2, k=KD, f=2)
                for f in range(2):
                    for g in range(2):
                        for k in range(KD):
                            ins = pe.matmul(bank[:, (2 * f + g) * P:(2 * f + g + 1) * P], w[:, g, k, f, :], xeT[:, k, :],
                                            start=(k == 0), stop=(k == KD - 1))
                ins.then_inc(e_product, 1)
            banks = [bank_of(Y0 + h, b) for h in range(HALVES)]
            pe.wait_ge(e_freed["vector"], b * e_n["vector"] + e_n["vector"] + E_NTH[PART0 - 1])
            f = 0
            for o, n in enumerate(OUT_ROWS):
                w = expert_unit(FC // 2 + o, b)[:, 0:n * D].rearrange("p (k n) -> p k n", n=D)
                for k in range(n):
                    for h in range(HALVES):
                        ins = pe.matmul(banks[h], geT[:, f, :], w[:, k, 512 * h:512 * h + 512], start=(f == 0), stop=(f == FC - 1))
                        if f == FC - 1:
                            ins.then_inc(e_product, 1)
                    f += 1
                if o < len(OUT_ROWS) - 1:
                    ins.then_inc(e_product, 1)
            for t in range(TILES):
                for h in range(HALVES):
                    j = SUM0 + t * HALVES + h
                    bank = bank_of(j, b)
                    pe.wait_ge(e_freed["scalar"], b * e_n["scalar"] + e_n["scalar"] + E_NTH[Y0 + h])
                    pe.matmul(bank, pickT[:, t, :], ye[:, 512 * h:512 * h + 512], start=True, stop=True).then_inc(e_product, 1)

        def skip(b):
            pe.wait_ge(e_product, b * N_EP + N_EP)
            pe.sem_inc(e_product, N_EP)

        pe.sem_inc(e_product, N_EP)
        each_expert(pe, expert, skip)

    @block.vector
    def _(dve):
        own = Own(dve, vector_step)

        def give(ins, name, wait=False):
            ins.then_inc(freed["vector"], 1)
            assert pl.freed[name] == ("vector", give.n + 1), name
            give.n += 1
            if wait:
                dve.wait_ge(freed["vector"], give.n)

        give.n = 0
        n_square, n_normed, n_row, n_angle, n_rope = [0], [0], [0], [0], [0]

        def tell(ins, s, count, wait=False):
            count[0] += 1
            ins.then_inc(s, 1)
            if wait:
                dve.wait_ge(s, count[0])

        def rms_norm(src, dst):
            for t in range(TILES):
                own(dve.tensor_tensor_reduce(dst[:, t, :] if dst is not src else rms_junk, src[:, t, :], src[:, t, :], 1.0, 0.0, ALU.mult, ALU.add,
                                             stat[:, t:t + 1]))
            tell(dve.tensor_scalar(stat, stat, 1.0 / D, EPS, ALU.mult, ALU.add), square_ready, n_square)
            dve.wait_ge(root_ready, n_square[0])
            own(dve.reciprocal(rstd, rstd))
            row = wait_row(dve, n_row[0])
            n_row[0] += 1
            for t in range(TILES):
                tell(dve.scalar_tensor_tensor(dst[:, t, :], src[:, t, :], rstd[:, t:t + 1], row, ALU.mult, ALU.mult), normed, n_normed, True)
            dve.sem_inc(row_used, 1)

        rms_junk = work[:, 0, :]

        def layer_norm():
            for t in range(TILES):
                for h in range(2):
                    own(dve.bn_stats(bn[:, 12 * t + 6 * h:12 * t + 6 * h + 6], x_tok[:, t, 512 * h:512 * h + 512]))
                own(dve.bn_aggr(mv[:, 2 * t:2 * t + 2], bn[:, 12 * t:12 * t + 12]))
                own(dve.tensor_scalar(stat[:, t:t + 1], mv[:, 2 * t + 1:2 * t + 2], LN_EPS, None, ALU.add))
            dve.sem_inc(square_ready, 1)
            n_square[0] += 1
            dve.wait_ge(root_ready, n_square[0])
            own(dve.reciprocal(rstd, rstd))
            g, b = wait_row(dve, n_row[0]), wait_row(dve, n_row[0] + 1)
            n_row[0] += 2
            for t in range(TILES):
                own(dve.tensor_scalar(x_tok[:, t, :], x_tok[:, t, :], mv[:, 2 * t:2 * t + 1], rstd[:, t:t + 1], ALU.subtract, ALU.mult))
            for t in range(TILES):
                own(dve.tensor_tensor(x_tok[:, t, :], x_tok[:, t, :], g, ALU.mult))
            for t in range(TILES):
                tell(dve.tensor_tensor(x_tok[:, t, :], x_tok[:, t, :], b, ALU.add), normed, n_normed, True)
            dve.sem_inc(row_used, 2)

        TURN = 2 * math.pi
        T1 = 6.28125
        T2 = round((TURN - T1) * 2 ** 20) / 2 ** 20
        T3 = TURN - T1 - T2
        ROUND = 1.5 * 2 ** 23
        PI = 3.1415925

        def rope_tables(i):
            dve.wait_ge(pos_in, 16 * (i + 1))
            own(dve.tensor_copy(ang, pos_i))
            own(dve.tensor_scalar(ang, ang, C(("freq1", "freq2")[i]), None, ALU.mult))
            own(dve.tensor_scalar(turns, ang, 1.0 / TURN, ROUND, ALU.mult, ALU.add))
            own(dve.tensor_scalar(turns, turns, ROUND, None, ALU.subtract))
            for part in (T1, T2, T3):
                own(dve.scalar_tensor_tensor(ang, turns, -part, ang, ALU.mult, ALU.add))
            tell(dve.tensor_scalar(ang, ang, PI, -PI, ALU.min, ALU.max), angle_ready, n_angle, True)
            own(dve.scalar_tensor_tensor(turns, ang, -1.0, ang, ALU.mult, ALU.min))
            tell(dve.tensor_scalar(turns, turns, math.pi / 2, None, ALU.add), angle_ready, n_angle)

        def rope(name, raw, after, outs=None):
            bank = wait_product(dve, name)
            dve.wait_ge(table_ready, 2 if name[0] == "rope" else 4)
            t = rope_t[:, n_rope[0] % 2, :]
            wait_freed(dve, after)
            give(dve.tensor_tensor(t, bank[:, 0:S], rope_sin, ALU.mult), name, True)
            own(dve.tensor_tensor(raw, raw, rope_cos, ALU.mult))
            if outs is None:
                tell(dve.tensor_tensor(raw, raw, t, ALU.add), rope_ready, n_rope, True)
            else:
                own(dve.tensor_tensor(outs[0][0:HD2], raw[0:HD2], t[0:HD2], ALU.add))
                tell(dve.tensor_tensor(outs[1][HD2:P], raw[HD2:P], t[HD2:P], ALU.add), rope_ready, n_rope, True)

        n_max, n_probs = [0], [0]

        def attention(base, n, out):
            for i in range(n + 2):
                if i < n:
                    g = base + i
                    b = g % 2
                    kind, h = heads[g]
                    bank = wait_product(dve, ("S", g)).rearrange("p (t s) -> p t s", t=TILES)
                    mask = {"self1": "band", "swa": "chunks", "fox": "causal"}.get(kind)
                    scale = HD ** -0.5 if kind in ("self1", "mem1") else SCALE2
                    if mask:
                        ins = dve.scalar_tensor_tensor(s_buf[b], bank, scale, C(mask).rearrange("p (t s) -> p t s", t=TILES), ALU.mult, ALU.add)
                    else:
                        ins = dve.tensor_scalar(s_buf[b], bank, scale, None, ALU.mult)
                    give(ins, ("S", g), True)
                    m = nmax[:, 2 * b:2 * b + 2]
                    own(dve.tensor_reduce(m, s_buf[b], AX.X, ALU.max))
                    if kind in ("self1", "swa"):
                        ins = dve.tensor_scalar(m, m, col("sink" if kind == "self1" else "sink2", h), -1.0, ALU.max, ALU.mult)
                    else:
                        ins = dve.tensor_scalar(m, m, -1.0, None, ALU.mult)
                    tell(ins, max_ready, n_max)
                if 1 <= i <= n:
                    g = base + i - 1
                    b = g % 2
                    kind, h = heads[g]
                    dve.wait_ge(exp_ready, g + 1)
                    dd, ss = den[:, 2 * b:2 * b + 2], esum[:, 2 * b:2 * b + 2]
                    if kind in ("self1", "swa"):
                        own(dve.tensor_tensor(dd, ss, esink[:, 2 * b:2 * b + 2], ALU.add))
                        ss = dd
                    own(dve.reciprocal(dd, ss))
                    for t in range(TILES):
                        ins = dve.tensor_scalar(p_buf[b][:, t, :], p_buf[b][:, t, :], den[:, 2 * b + t:2 * b + t + 1], None, ALU.mult)
                    tell(ins, probs_ready, n_probs)
                if i >= 2:
                    g = base + i - 2
                    bank = wait_product(dve, ("V", g))
                    p0, p1, dst = out(*heads[g])
                    give(dve.tensor_copy(dst[p0:p1], bank[p0:p1, 0:S]), ("V", g))

        dve.wait_ge(mem_in, 16)
        dve.wait_ge(const_in, 32)
        for t in range(TILES):
            own(dve.tensor_tensor_reduce(region[:, 4096 + t * D:4096 + (t + 1) * D], work[:, t, :], work[:, t, :], 1.0, 0.0, ALU.mult, ALU.add, stat[:, t:t + 1]))
        tell(dve.tensor_scalar(stat, stat, 1.0 / D, EPS, ALU.mult, ALU.add), square_ready, n_square)
        dve.wait_ge(root_ready, 1)
        own(dve.reciprocal(rstd, rstd))
        row = wait_row(dve, 0)
        n_row[0] = 1
        for t in range(TILES):
            tell(dve.scalar_tensor_tensor(work[:, t, :], work[:, t, :], rstd[:, t:t + 1], row, ALU.mult, ALU.mult), normed, n_normed, True)
        dve.sem_inc(row_used, 1)
        rope_tables(0)
        dve.wait_ge(x_in, 16)
        dve.wait_ge(product_ready, pl.nth[("memT", KD - 1)])
        rms_norm(x_tok, work)
        for c in range(C_V):
            rope(("rope", c), qa[:, c, :] if c < C_K else ka[:, c - C_K, :], ("in", c))
        dve.wait_ge(product_ready, pl.nth[("hT", KD - 1)])
        for b in range(LB):
            wait_freed(dve, ("in", C_XL + b))
            w = lambda j: col("conv_w", j * LB + b)
            own(dve.tensor_scalar(xc[:, b, :], xl[:, b, :], w(2), col("conv_b", b), ALU.mult, ALU.add))
            own(dve.scalar_tensor_tensor(xc[:, b, 2:S], xl[:, b, 0:S - 2], w(0), xc[:, b, 2:S], ALU.mult, ALU.add))
            own(dve.scalar_tensor_tensor(xc[:, b, 1:S], xl[:, b, 0:S - 1], w(1), xc[:, b, 1:S], ALU.mult, ALU.add))
            dve.scalar_tensor_tensor(xc[:, b, 0:S - 1], xl[:, b, 1:S], w(3), xc[:, b, 0:S - 1], ALU.mult, ALU.add).then_inc(conv_ready, 1)
        attention(0, N1, lambda kind, h: (0, P, (qa if kind == "self1" else qm)[:, h, :]))
        lam = col("lam", 0, 12)
        own(dve.tensor_scalar(sp_p, lam, -1.0, None, ALU.mult))
        dve.tensor_tensor(sp_z, sp_p, lam, ALU.min).then_inc(lam_exp, 1)
        dve.wait_ge(lam_exp, 2)
        own(dve.tensor_scalar(sp_z, sp_e, 2.0, None, ALU.add))
        own(dve.reciprocal(sp_z, sp_z))
        own(dve.tensor_tensor(sp_e, sp_e, sp_z, ALU.mult))
        own(dve.tensor_tensor(sp_z, sp_e, sp_e, ALU.mult))
        own(dve.tensor_scalar(sp_p, sp_z, 1.0 / 17, 1.0 / 15, ALU.mult, ALU.add))
        for n in (13, 11, 9, 7, 5, 3, 1):
            own(dve.tensor_tensor(sp_p, sp_p, sp_z, ALU.mult))
            own(dve.tensor_scalar(sp_p, sp_p, 1.0 / n, None, ALU.add))
        own(dve.scalar_tensor_tensor(sp_e, sp_e, 2.0, sp_p, ALU.mult, ALU.mult))
        own(dve.tensor_scalar(sp_p, lam, -1.0, 0.0, ALU.mult, ALU.max))
        own(dve.tensor_tensor(sp_p, sp_p, sp_e, ALU.add))
        own(dve.tensor_scalar(sp_e, sp_p, -8.0, None, ALU.mult))
        dve.tensor_scalar(sp_p, sp_p, 8.0, None, ALU.mult).then_inc(lam_ready, 1)
        for d in range(2):
            for b in range(LB):
                r, i = lru_ri[:, b, 0, :], lru_ri[:, b, 1, :]
                dve.wait_ge(lru_at, d * LB + b + 1)
                own(dve.tensor_tensor(i, i, xc[:, b, :], ALU.mult))
                tmp = actT_flat[:, LB * S:LB * S + S]
                own(dve.tensor_tensor(tmp, lru_a[:, b, :], lru_a[:, b, :], ALU.mult))
                dve.scalar_tensor_tensor(r, tmp, 1.0, r, ALU.add, ALU.mult).then_inc(lru_sq_in, 1)
                dve.wait_ge(lru_sq_in, d * LB + b + 1)
            for b in range(LB):
                r, i = lru_ri[:, b, 0, :], lru_ri[:, b, 1, :]
                dve.wait_ge(lru_sq_out, d * LB + b + 1)
                own(dve.tensor_tensor(i, i, r, ALU.mult))
                if d == 0:
                    own(dve.tensor_tensor_scan(xl[:, b, :], lru_a[:, b, :], i, 0.0, ALU.mult, ALU.add))
                else:
                    own(dve.tensor_tensor_scan(r[:, ::-1], lru_a[:, b, ::-1], i[:, ::-1], 0.0, ALU.mult, ALU.add))
                    own(dve.tensor_tensor(r, r, xl[:, b, :], ALU.add))
                    own(dve.tensor_tensor(gl[:, b, :], gl[:, b, :], r, ALU.mult))
            dve.sem_inc(lru_done, 1)
        for br in range(3):
            for c in range(KD):
                bank = wait_product(dve, ("merge", br, c))[:, 0:S]
                if br == 0:
                    give(dve.tensor_tensor(gates[:, c, :], gates[:, c, :], bank, ALU.mult), ("merge", br, c), True)
                else:
                    gg = gates[:, br * KD + c, :]
                    give(dve.tensor_tensor(gg, gg, bank, ALU.mult), ("merge", br, c), True)
                    ins = dve.tensor_tensor(gates[:, c, :], gates[:, c, :], gg, ALU.add)
                    if br == 1:
                        own(ins)
                    else:
                        ins.then_inc(merged, 1)
        for t in range(TILES):
            for h in range(HALVES):
                bank = wait_product(dve, ("out1", t, h))
                xx = x_tok[:, t, 512 * h:512 * h + 512]
                give(dve.tensor_tensor(xx, xx, bank, ALU.add), ("out1", t, h), True)
        rms_norm(x_tok, work)
        n_best = [0]
        for t in range(TILES):
            for g in range(4):
                wait_freed(dve, ("sc", t, g))
            for c in range(2 * PH):
                v, u = top_v[:, c, :], top_u[:, c, :]
                s = sc[:, t, c, :]
                own(dve.max(v[:, 0:8], s))
                own(dve.max_index(u[:, 0:8], v[:, 0:8], s))
                own(dve.match_replace(sc_less, v[:, 0:8], s, -3.0e38))
                own(dve.max(v[:, 8:16], sc_less))
                own(dve.max_index(u[:, 8:16], v[:, 8:16], sc_less))
            own(dve.tensor_copy(top_f, top_u))
            for h in range(PH):
                grid = cand.rearrange("p (i j) -> p i j", i=TOPK)
                own(dve.tensor_tensor(grid, top_v[:, 2 * h, :].unsqueeze(2).to_broadcast([P, TOPK, TOPK]),
                                      top_v[:, 2 * h + 1, :].unsqueeze(1).to_broadcast([P, TOPK, TOPK]), ALU.add))
                v, u = best[:, h, :], best_u[:, h, :]
                own(dve.max(v[:, 0:8], cand))
                own(dve.max_index(u[:, 0:8], v[:, 0:8], cand))
                own(dve.match_replace(cand_less, v[:, 0:8], cand, -3.0e38))
                own(dve.max(v[:, 8:16], cand_less))
                own(dve.max_index(u[:, 8:16], v[:, 8:16], cand_less))
                own(dve.tensor_copy(den[:, 0:1], v[:, 0:1]))
                dve.tensor_scalar(v, v, den[:, 0:1], None, ALU.subtract).then_inc(best_ready, 1)
                dve.wait_ge(best_exp, t * PH + h + 1)
                own(dve.reciprocal(den[:, 0:1], esum[:, h % 4:h % 4 + 1]))
                own(dve.tensor_scalar(gate_all[:, t, h * TOPK:(h + 1) * TOPK], best_e[:, h, :], den[:, 0:1], None, ALU.mult))
            flat_u = best_u.rearrange("p h k -> p (h k)")
            own(dve.tensor_scalar(half_u[:, 0, :], flat_u, 4, None, ALU.logical_shift_right))
            own(dve.tensor_scalar(half_u[:, 1, :], flat_u, 15, None, ALU.bitwise_and))
            own(dve.tensor_copy(half_f, half_u))
            for half in range(2):
                place = half_f[:, half, :].rearrange("p (h k) -> p h k", h=PH)
                own(dve.tensor_tensor(hot.rearrange("p h k c -> p (h k) c"), half_f[:, half, :].unsqueeze(2).to_broadcast([P, PICKS, TOPK]),
                                      C("iota")[:, 0:TOPK].unsqueeze(1).to_broadcast([P, PICKS, TOPK]), ALU.is_equal))
                keys = top_f.rearrange("p (h x) k -> p h x k", x=2)[:, :, half, :]
                own(dve.tensor_tensor(hot, hot, keys.unsqueeze(2).to_broadcast([P, PH, TOPK, TOPK]), ALU.mult))
                own(dve.tensor_reduce(key_f[:, half, :], hot.rearrange("p h k c -> p (h k) c"), AX.X, ALU.add))
            own(dve.scalar_tensor_tensor(idx_f, key_f[:, 0, :], float(PK), key_f[:, 1, :], ALU.mult, ALU.add))
            dve.tensor_copy(idx_all[:, t, :], idx_f).then_inc(search_done, 1)
            dve.wait_ge(search_done, t + 1)
        dve.sem_inc(dots_done, 1)
        dve.sem_inc(peer_added, 1)
        with dve.Fori(0, PH) as h:
            for t in range(TILES):
                it = h * TILES + t
                for k in range(TOPK):
                    dve.wait_ge(u_in[k % UV], it * 32 + 16 * (k // UV + 1))
                    if k == 0:
                        dve.wait_ge(gelu_done, h * TILES + 1)
                    dve.tensor_tensor_reduce(u_ring[:, k % UV, :], u_ring[:, k % UV, :], work[:, t, :], 1.0, 0.0, ALU.mult, ALU.add,
                                             u_dot[:, t, k:k + 1]).then_inc(dots_done, 1)
                dve.wait_ge(gelu_done, it + 2)
                dve.wait_ge(diag_done, it * TOPK + 1)
                dve.tensor_tensor(pick_w[:, t, :], u_act[:, t, :], gate_all[:, t, bass.ds(h * TOPK, TOPK)], ALU.mult).then_inc(weights_done, 1)
                dve.wait_ge(v_used, it * TOPK + TOPK + 1)
                for half in range(HALVES):
                    xx = x_tok[:, t, 512 * half:512 * half + 512]
                    dve.tensor_tensor(xx, xx, psum[:, 2 * t + half, :], ALU.add).then_inc(peer_added, 1)
                dve.wait_ge(peer_added, it * HALVES + HALVES + 1)
        for t in range(TILES):
            own(dve.tensor_tensor_reduce(work[:, t, :], x_tok[:, t, :], x_tok[:, t, :], 1.0, 0.0, ALU.mult, ALU.add, stat[:, t:t + 1]))
        tell(dve.tensor_scalar(stat, stat, 1.0 / D, EPS, ALU.mult, ALU.add), square_ready, n_square)
        dve.wait_ge(root_ready, n_square[0])
        own(dve.reciprocal(rstd, rstd))
        row = wait_row(dve, n_row[0])
        n_row[0] += 1
        for t in range(TILES):
            tell(dve.scalar_tensor_tensor(x_tok[:, t, :], x_tok[:, t, :], rstd[:, t:t + 1], row, ALU.mult, ALU.mult), normed, n_normed, True)
        dve.sem_inc(row_used, 1)
        own(dve.memset(kz, 0.0))
        dve.memset(kmz, 0.0).then_inc(zeros_ready, 1)
        dve.wait_ge(zeros_ready, 1)
        rope_tables(1)
        for layer in range(2):
            if layer == 1:
                own(dve.memset(kz, 0.0))
                dve.sem_inc(zeros_ready, 1)
            for c in range(2):
                bank = wait_product(dve, ("km2", layer, c))
                own(dve.tensor_copy(kmz[0:HD2, 2 * c, :], bank[0:HD2, 0:S]))
                give(dve.tensor_copy(kmz[HD2:P, 2 * c + 1, :], bank[HD2:P, 0:S]), ("km2", layer, c))
            if layer == 0:
                for c in range(SH // 2 + SKV):
                    if c < SH // 2:
                        rope(("rope2", c), q2[:, c, :], ("in2", 0, c))
                    else:
                        j = 2 * (c - SH // 2)
                        rope(("rope2", c), k_raw[:, c % 2, :], ("in2", 0, c), (kz[:, j, :], kz[:, j + 1, :]))
            else:
                bank = wait_product(dve, ("forget",))
                z = f_log[0:SH, :]
                t = f_tmp[0:SH, :]
                give(dve.tensor_scalar(z, bank[0:SH, 0:S], col("b_forget")[0:SH], None, ALU.add), ("forget",), True)
                own(dve.tensor_scalar(t, z, -1.0, None, ALU.mult))
                dve.tensor_tensor(t, t, z, ALU.min).then_inc(forget_exp, 1)
                dve.wait_ge(forget_e, 1)
                own(dve.tensor_scalar(z, z, 0.0, None, ALU.min))
                own(dve.tensor_tensor(z, z, t, ALU.subtract))
                own(dve.memset(t, 1.0))
                own(dve.tensor_tensor_scan(f_cum[0:SH, :], t, z, 0.0, ALU.mult, ALU.add))
                dve.tensor_scalar(f_cum[0:SH, :], f_cum[0:SH, :], -1.0 / SCALE2, None, ALU.mult).then_inc(cum_ready, 1)

            def out(kind, h):
                c = h // 2 if kind != "mem2" else SH // 2 + h // 2
                return h % 2 * HD2, h % 2 * HD2 + HD2, actT[:, c, :]

            attention(pl.att2[layer], SH + MH2, out)
            for t in range(TILES):
                for h in range(HALVES):
                    bank = wait_product(dve, ("out2", layer, t, h))
                    xx = x_tok[:, t, 512 * h:512 * h + 512]
                    give(dve.scalar_tensor_tensor(xx, xx, ALPHA, bank, ALU.mult, ALU.add), ("out2", layer, t, h), True)
            layer_norm()
            if layer == 0:
                for f in range(FC):
                    dve.wait_ge(silu_ready, f + 1)
                    bank = psum[:, pl.bank[("ff", f)], :]
                    give(dve.tensor_tensor(ffT[:, f, :], silu_ff[:, f % 2, :], bank[:, S:2 * S], ALU.mult), ("ff", f), True)
                    dve.sem_inc(ff_ready, 1)
                for t in range(TILES):
                    for h in range(HALVES):
                        bank = wait_product(dve, ("down", t, h))
                        xx = x_tok[:, t, 512 * h:512 * h + 512]
                        give(dve.scalar_tensor_tensor(xx, xx, ALPHA, bank, ALU.mult, ALU.add), ("down", t, h), True)
                layer_norm()
        own(dve.memset(ones, 1.0))
        own(dve.tensor_scalar(before, C("causal")[:, 0:P], -1.0, None, ALU.is_lt))
        for t in range(TILES):
            bank = wait_product(dve, ("router", t))
            give(dve.tensor_tensor(logits[:, t, :], bank[:, 0:NE], col("b_router", 0, NE), ALU.add), ("router", t), True)
            own(dve.max(r_top[:, t, :], logits[:, t, :]))
            own(dve.max_index(r_idx[:, t, :], r_top[:, t, :], logits[:, t, :]))
        own(dve.tensor_copy(r_idxf, r_idx))
        own(dve.tensor_tensor(r_e, r_top[:, :, 1], r_top[:, :, 0], ALU.subtract))
        dve.sem_inc(router_exp, 1)
        dve.wait_ge(router_e, 1)
        own(dve.tensor_scalar(r_den, r_e, 1.0, None, ALU.add))
        own(dve.reciprocal(r_g[:, :, 0], r_den))
        own(dve.tensor_tensor(r_g[:, :, 1], r_g[:, :, 0], r_e, ALU.mult))
        for t in range(TILES):
            own(dve.tensor_scalar(r_mask[:, t, :], C("iota")[:, 0:NE], r_idxf[:, t, 0:1], None, ALU.is_equal))
            own(dve.tensor_scalar(r_gate[:, t, :], r_mask[:, t, :], r_g[:, t, 0:1], None, ALU.mult))
            own(dve.tensor_scalar(r_hot[:, t, :], C("iota")[:, 0:NE], r_idxf[:, t, 1:2], None, ALU.is_equal))
            own(dve.tensor_tensor(r_mask[:, t, :], r_mask[:, t, :], r_hot[:, t, :], ALU.add))
            own(dve.scalar_tensor_tensor(r_gate[:, t, :], r_hot[:, t, :], r_g[:, t, 1:2], r_gate[:, t, :], ALU.mult, ALU.add))
        dve.sem_inc(router_e, 1)
        bank = wait_product(dve, ("place",))
        places = bank[:, 0:TILES * NE].rearrange("p (t e) -> p t e", t=TILES)
        own(dve.tensor_scalar(r_slot, r_mask, -1.0e6, 1.0e6, ALU.mult, ALU.add))
        own(dve.tensor_tensor(r_slot, r_slot, places, ALU.add))
        give(dve.tensor_copy(count_i, bank[:, 2 * NE:3 * NE]), ("place",), True)
        for t in range(TILES):
            own(dve.tensor_scalar(work[:, t, :], x_tok[:, t, :], ALPHA, None, ALU.mult))
        dve.sem_inc(e_freed["vector"], e_n["vector"])
        dve.sem_inc(routed, 1)

        def wait_e(j, b):
            dve.wait_ge(e_product, b * N_EP + j + 1 + N_EP)
            return psum[:, E_BANK[j], :]

        def expert(e, b, over):
            dve.wait_ge(e_product, b * N_EP + N_EP)
            dve.tensor_copy(r_shift, r_slot[:, :, bass.ds(e, 1)].rearrange("p t e -> p (t e)")).then_inc(pick_step, 1)
            dve.wait_ge(pick_step, 3 * b + 1)
            if over:
                dve.tensor_scalar(r_shift, r_shift, float(-P), None, ALU.add).then_inc(pick_step, 1)
            else:
                dve.sem_inc(pick_step, 1)
            dve.wait_ge(pick_step, 3 * b + 2)
            dve.tensor_copy(r_den, r_gate[:, :, bass.ds(e, 1)].rearrange("p t e -> p (t e)")).then_inc(pick_step, 1)
            dve.wait_ge(pick_step, 3 * b + 3)
            for t in range(TILES):
                dve.tensor_scalar(pick[:, t, :], C("iota"), r_shift[:, t:t + 1], None, ALU.is_equal)
                ins = dve.tensor_scalar(pickg[:, t, :], C("iota"), r_shift[:, t:t + 1], r_den[:, t:t + 1], ALU.is_equal, ALU.mult)
            ins.then_inc(picked, 1)
            for n in range(FC // 2):
                dve.wait_ge(e_silu, b * (FC // 2) + n + 1)
                bank = psum[:, E_BANK[UP0 + n], :].rearrange("p (f g s) -> p f g s", f=2, g=2)
                dve.tensor_tensor(geT[:, 2 * n:2 * n + 2, :], silu_e[:, n % 2, :, :], bank[:, :, 1, :], ALU.mult)\
                   .then_inc(e_freed["vector"], 1)
            for t in range(TILES):
                for h in range(HALVES):
                    bank = wait_e(SUM0 + t * HALVES + h, b)
                    ww = work[:, t, 512 * h:512 * h + 512]
                    dve.tensor_tensor(ww, ww, bank, ALU.add).then_inc(e_freed["vector"], 1)

        def skip(b):
            dve.sem_inc(pick_step, 3)
            dve.wait_ge(picked, b)
            dve.sem_inc(picked, 1)
            dve.wait_ge(e_freed["vector"], b * e_n["vector"] + e_n["vector"])
            dve.sem_inc(e_freed["vector"], e_n["vector"])

        each_expert(dve, expert, skip)
        dve.wait_ge(e_freed["vector"], (2 * NE + 1) * e_n["vector"])
        for t in range(TILES):
            own(dve.tensor_copy(x_tok[:, t, :], work[:, t, :]))
        layer_norm()

    ctx.close()


def ff_loads(pl, a):
    w = a["w_ffn_in_2"][0].rearrange("(k p) n -> p k n", p=P)
    for u in range(FC // 2):
        pl.add_unit(("ff_in", u), [(half * KD * S, KD, S, w[:, :, half * FF + S * u:half * FF + S * (u + 1)]) for half in range(2)],
                    ("ff", 2 * u + 1))
    w = a["w_ffn_out_2"][0].rearrange("(k p) n -> p k n", p=P)
    for o, n in enumerate([3] * 6 + [4]):
        pl.add_unit(("ff_out", o), [(0, n, D, w[:, 3 * o:3 * o + n, :])],
                    ("ff_out_used", o) if o < 6 else ("down", TILES - 1, HALVES - 1))


PLAIN = ["x", "mem", "positions", "positions_2", "w_mem_kv", "w_in", "lru_wr", "lru_wi", "p_attn", "p_lru", "p_mem", "w_out",
         "w_peer_q", "peer_u", "peer_v", "w_mem_kv_2", "w_in_fox_2", "w_out_2", "w_ffn_in_2", "w_ffn_out_2", "w_exp_in_2",
         "w_exp_out_2", "g_mem", "g_mix", "g_ffn", "g_final", "ln_attn_g_2", "ln_attn_b_2", "ln_ffn_g_2", "ln_ffn_b_2"]


def layouts(v):
    def by_partition(x):
        return np.ascontiguousarray(x).reshape(-1, P).T

    def on_all(x):
        return np.broadcast_to(x.reshape(1, -1), (P, x.size))

    def chunks(x):
        return x.reshape(KD, P, -1).transpose(1, 0, 2).reshape(P, -1)

    f = v["w_in_fox_2"][0]
    b_forget = np.zeros((P, 1), np.float32)
    b_forget[:SH, 0] = v["b_forget_2"][0]
    parts = {"gate_b": by_partition(v["gate_b"][0]), "conv_w": by_partition(v["conv_w"][0]), "conv_b": by_partition(v["conv_b"][0]),
             "lru_br": by_partition(v["lru_br"][0]), "lru_bi": by_partition(v["lru_bi"][0]), "lam": by_partition(v["lru_lambda"][0]),
             "sink": on_all(v["attn_sink"][0]), "sink2": on_all(v["attn_sinks_2"][0]), "b_router": on_all(v["b_router_2"][0]),
             "b_forget": b_forget, "w_forget": chunks(f[:, -SH:]), "w_router": chunks(v["w_router_2"][0])}
    out = {name: v[name] for name in PLAIN}
    out["columns"] = np.concatenate([parts[name] for name in COLS], axis=1)
    out["constants"] = constants()
    out["sub_keys_T"] = v["peer_sub_keys"][0].reshape(2 * PH, PK, P).transpose(2, 0, 1)
    out["mem_2_T"] = v["mem_2"][0].T
    w = v["w_in_swa_2"][0]
    q, kv = SH * HD2, SKV * HD2
    twice = lambda x: np.repeat(x.reshape(D, SKV, 1, HD2), 2, axis=2).reshape(D, 2 * kv)
    out["w_swa"] = np.concatenate([w[:, :q], twice(w[:, q:q + kv]), twice(w[:, q + kv:q + 2 * kv]), w[:, q + 2 * kv:]], axis=1)
    return {name: np.ascontiguousarray(x) for name, x in out.items()}


def kernel(**inputs):
    import concourse.bacc as bacc
    from concourse.bass_utils import run_bass_kernel_spmd

    arrays = layouts({name: np.asarray(x) for name, x in inputs.items()})
    nc = bacc.Bacc("TRN2", target_bir_lowering=False, num_devices=1)
    a = {name: nc.dram_tensor("in_" + name, x.shape, mybir.dt.from_np(x.dtype), kind="ExternalInput").ap() for name, x in arrays.items()}
    a["out"] = nc.dram_tensor("out", (1, S, D), F32, kind="ExternalOutput").ap()
    two_blocks(nc, a)
    r = run_bass_kernel_spmd(nc, [{"in_" + name: x for name, x in arrays.items()}], core_ids=[0])
    return r.results[0]["out"]
```

```python
import math
from contextlib import ExitStack

import numpy as np

import concourse.bass as bass
from concourse import mybir

F32, I32, U32 = mybir.dt.float32, mybir.dt.int32, mybir.dt.uint32
ALU, ACT, AX = mybir.AluOpType, mybir.ActivationFunctionType, mybir.AxisListType

P = 128
S, D = 256, 1024
TILES, KD = S // P, D // P
HALVES = D // 512
EPS, LN_EPS = 1e-6, 1e-5
NEG = -1e30
THETA = 500000.0

AH, AKV, HD = 6, 2, 128
GROUP = AH // AKV
LW, LB = 768, 6
CONV = 4
MH = 4
PH, PK, TOPK = 8, 128, 16
PICKS = PH * TOPK
SH, SKV, MH2, HD2 = 12, 3, 4, 64
FF = 2816
FC = FF // P
NE = 8
ALPHA = 4.0 ** 0.25
SCALE2 = HD2 ** -0.5

C_Q, C_K, C_V, C_XL, C_GL, C_QM, C_G = 0, 6, 8, 10, 16, 22, 26
N_IN = 50

RING, UNIT = 6, KD * 512
BANKS = 8
UV = 8

COLS = {}
_at = 0
for _name, _n in (("gate_b", 24), ("conv_w", CONV * LB), ("conv_b", LB), ("lru_br", 12), ("lru_bi", 12), ("lam", 12),
                  ("sink", AH), ("sink2", SH), ("b_router", NE), ("b_forget", 1), ("w_forget", KD * SH),
                  ("w_router", KD * NE)):
    COLS[_name] = (_at, _n)
    _at += _n
N_COLS = _at
CONST = {}
_at = 0
for _name, _n in (("ident", P), ("rot1", P), ("rot2", P), ("iota", P), ("freq1", 1), ("freq2", 1),
                  ("band", TILES * S), ("chunks", TILES * S), ("causal", TILES * S)):
    CONST[_name] = (_at, _n)
    _at += _n
N_CONST = _at


def constants():
    c = np.zeros((P, N_CONST), np.float32)

    def put(name, value):
        at, n = CONST[name]
        c[:, at:at + n] = np.asarray(value, np.float32).reshape(P, n)

    def rotation(head, rot):
        m = np.zeros((P, P), np.float32)
        for base in range(0, P, head):
            for o in range(rot // 2):
                m[base + o + rot // 2, base + o] = -1.0
                m[base + o, base + o + rot // 2] = 1.0
        return m

    def freqs(head, rot):
        f = np.float32(THETA) ** (-np.arange(0, rot, 2, dtype=np.float32) / np.float32(rot))
        out = np.zeros(P, np.float32)
        for base in range(0, P, head):
            out[base:base + rot // 2] = f
            out[base + rot // 2:base + rot] = f
        return out

    put("ident", np.eye(P))
    put("rot1", rotation(HD, HD // 4))
    put("rot2", rotation(HD2, HD2 // 4))
    put("iota", np.broadcast_to(np.arange(P), (P, P)))
    put("freq1", freqs(HD, HD // 4))
    put("freq2", freqs(HD2, HD2 // 4))
    q = np.arange(S).reshape(TILES, P).T[:, :, None]
    k = np.arange(S)[None, None, :]
    put("band", np.where(np.abs(q - k) <= 128, 0.0, NEG))
    put("chunks", np.where((k // 64 <= q // 64) & (k // 64 >= q // 64 - 2), 0.0, NEG))
    put("causal", np.where(k <= q, 0.0, NEG))
    return c


class Plan:

    def __init__(self):
        self.products, self.nth, self.bank, self.freed = [], {}, {}, {}
        self.count = {"vector": 0, "scalar": 0}
        self.units, self.unit = [], {}
        self.loaded = [0] * RING
        self.at = 0

    def product(self, name, by):
        self.bank[name] = len(self.products) % BANKS
        self.products.append(name)
        self.nth[name] = len(self.products)
        self.count[by] += 1
        self.freed[name] = (by, self.count[by])

    def add_unit(self, name, loads, last):
        slot = self.at % RING
        self.loaded[slot] += 16 * len(loads)
        before = [u for u in self.units if u[1] == slot]
        self.units.append((name, slot, loads, last, before[-1][3] if before else None))
        self.unit[name] = (slot, self.loaded[slot])
        self.at += 1


def make_plan():
    pl = Plan()
    pr = pl.product
    heads = []

    def transposed(tag):
        for k in range(KD):
            pr((tag, k), "scalar")

    def attention(kinds):
        base = len(heads)
        heads.extend(kinds)
        n = len(kinds)
        for i in range(n + 2):
            if i < n:
                pr(("S", base + i), "vector")
            if 1 <= i <= n:
                pr(("T", base + i - 1), "scalar")
            if i >= 2:
                pr(("V", base + i - 2), "vector")
        return base

    transposed("memT")
    for c in range(MH):
        pr(("km", c), "scalar")
    for t in range(TILES):
        pr(("vm", t), "scalar")
    transposed("hT")
    for c in range(C_V):
        pr(("in", c), "scalar")
        if c >= 1:
            pr(("rope", c - 1), "vector")
    for t in range(TILES):
        pr(("v", t), "scalar")
        if t == 0:
            pr(("rope", C_V - 1), "vector")
    for c in range(C_XL, N_IN):
        pr(("in", c), "scalar")
    pl.att1 = attention([("self1", h) for h in range(AH)] + [("mem1", h) for h in range(MH)])
    for d in range(2):
        for b in range(LB):
            pr(("lru", d, b), "scalar")
    for br in range(3):
        for c in range(KD):
            pr(("merge", br, c), "vector")
    for t in range(TILES):
        for h in range(HALVES):
            pr(("out1", t, h), "vector")
    transposed("h2T")
    for c in range(2 * PH):
        pr(("pq", c), "scalar")
    for t in range(TILES):
        for g in range(4):
            pr(("sc", t, g), "scalar")

    def memory2(layer):
        for c in range(2):
            pr(("km2", layer, c), "vector")
        for t in range(TILES):
            pr(("vm2", layer, t), "scalar")

    memory2(0)
    transposed("x2T")
    pl.att2 = []
    for layer in range(2):
        if layer:
            memory2(layer)
        nk = SKV if layer == 0 else SH // 2
        for c in range(SH // 2 + nk):
            pr(("in2", layer, c), "scalar")
            if c >= 1:
                if layer == 0:
                    pr(("rope2", c - 1), "vector")
        if layer == 0:
            pr(("rope2", SH // 2 + nk - 1), "vector")
        for t in range(TILES):
            for h in range(1 + layer):
                pr(("v2", layer, t, h), "scalar")
        for c in range(2):
            pr(("qm2", layer, c), "scalar")
        if layer == 1:
            pr(("forget",), "vector")
        kind = ("swa", "fox")[layer]
        pl.att2.append(attention([(kind, h) for h in range(SH)] + [("mem2", h) for h in range(MH2)]))
        for t in range(TILES):
            for h in range(HALVES):
                pr(("out2", layer, t, h), "vector")
        transposed(("aT", layer))
        if layer == 0:
            for f in range(FC):
                pr(("ff", f), "vector")
            for t in range(TILES):
                for h in range(HALVES):
                    pr(("down", t, h), "vector")
            transposed("x3T")
        else:
            for t in range(TILES):
                pr(("router", t), "vector")
            pr(("place",), "vector")
    pl.heads = heads
    return pl


def two_blocks(nc, a):
    pl = make_plan()
    ctx = ExitStack()
    sem = lambda name: ctx.enter_context(nc.semaphore(name))
    sb = lambda name, n, dt=F32: ctx.enter_context(nc.sbuf_tensor(name, [P, n], dt))

    def cols_of(w, c0, n):
        return w.rearrange("(k p) n -> p k n", p=P)[:, :, c0:c0 + n]

    def rows_of(w, k0, nk):
        return w.rearrange("(k p) n -> p k n", p=P)[:, k0:k0 + nk, :]

    for u in range(2):
        pl.add_unit(("mem_kv", u), [(0, KD, 512, cols_of(a["w_mem_kv"][0], 512 * u, 512))],
                    [("km", MH - 1), ("vm", TILES - 1)][u])
    for u in range(13):
        n = min(512, N_IN * P - 512 * u)
        last = ("in", min(4 * u + 3, N_IN - 1)) if u != 2 else ("in", 11)
        pl.add_unit(("w_in", u), [(0, KD, n, cols_of(a["w_in"][0], 512 * u, n))], last)
    pl.add_unit("lru_w", [(0, 12, P, a["lru_wr"][0].rearrange("d h c e -> c (d h) e")),
                          (12 * P, 12, P, a["lru_wi"][0].rearrange("d h c e -> c (d h) e"))], ("lru", 1, LB - 1))
    for br, (name, nk) in enumerate((("p_attn", AH), ("p_lru", LB), ("p_mem", MH))):
        for u in range(2):
            pl.add_unit((name, u), [(0, nk, 512, cols_of(a[name][0], 512 * u, 512))], ("merge", br, 4 * u + 3))
    for u in range(HALVES):
        pl.add_unit(("w_out", u), [(0, KD, 512, cols_of(a["w_out"][0], 512 * u, 512))], ("out1", TILES - 1, u))
    for u in range(4):
        pl.add_unit(("peer_q", u), [(0, KD, 512, cols_of(a["w_peer_q"][0], 512 * u, 512))], ("pq", 4 * u + 3))
    pl.add_unit("sub_keys", [(0, 2 * PH, PK, a["sub_keys_T"])], ("sc", TILES - 1, 3))
    for layer in range(2):
        pl.add_unit(("mem_kv2", layer), [(0, KD, 512, cols_of(a["w_mem_kv_2"][layer], 0, 512))],
                    ("vm2", layer, TILES - 1))
        w = a["w_swa"] if layer == 0 else a["w_in_fox_2"][0]
        width = w.shape[1] // P * P
        for u in range(-(-width // 512)):
            n = min(512, width - 512 * u)
            if layer == 0:
                last = (("in2", 0, 3), ("in2", 0, 7), ("v2", 0, 1, 0), ("qm2", 0, 1))[u]
            else:
                last = (("in2", 1, 3), ("in2", 1, 7), ("in2", 1, 11), ("v2", 1, 1, 0), ("qm2", 1, 1))[u]
            pl.add_unit(("w_in2", layer, u), [(0, KD, n, cols_of(w, 512 * u, n))], last)
        for u in range(HALVES):
            pl.add_unit(("w_out2", layer, u), [(0, KD, 512, cols_of(a["w_out_2"][layer], 512 * u, 512))],
                        ("out2", layer, TILES - 1, u))
        if layer == 0:
            ff_loads(pl, a)
    pl.at += -pl.at % RING

    OUT_ROWS = [3] * 6 + [4]
    e_units = [2] * (FC // 2) + [1] * len(OUT_ROWS)
    N_EU = len(e_units)
    assert N_EU % RING == 0
    e_loaded, per_expert = [], [0] * RING
    for j, n in enumerate(e_units):
        per_expert[j % RING] += 16 * n
        e_loaded.append(per_expert[j % RING])
    G0, G1, PT, UP0 = 0, 1, 2, 3
    PART0 = UP0 + FC // 2
    Y0 = PART0 + len(OUT_ROWS) - 1
    SUM0 = Y0 + HALVES
    N_EP = SUM0 + TILES * HALVES

    ring = sb("weight_ring", RING * UNIT)
    slot = lambda s: ring[:, s * UNIT:(s + 1) * UNIT]
    const = sb("constants", N_CONST)
    cols = sb("columns", N_COLS)
    C = lambda name: const[:, CONST[name][0]:sum(CONST[name])]
    col = lambda name, i=0, n=1: cols[:, COLS[name][0] + i:COLS[name][0] + i + n]
    ident = C("ident")
    tok = lambda ap: ap.rearrange("p (t n) -> p t n", t=TILES)
    x_tok = tok(sb("x_tok", TILES * D)[:, :])
    actT_flat = sb("actT", KD * S)
    actT = actT_flat[:, :].rearrange("p (k s) -> p k s", k=KD)
    work_flat = sb("work_tok", TILES * D)
    work = tok(work_flat[:, :])
    rows = sb("rows", 2 * D)[:, :].rearrange("p (r n) -> p r n", r=2)
    small = sb("small", 96)
    n_small = [0]

    def cell(n):
        n_small[0] += n
        assert n_small[0] <= 96
        return small[:, n_small[0] - n:n_small[0]]

    REGION = 17920
    region = sb("region", REGION)
    top = [0]

    def area(n, inner=None, dt=None):
        v = region[:, top[0]:top[0] + n]
        top[0] += n
        assert top[0] <= REGION, top[0]
        if dt is not None:
            v = v.bitcast(dt)
        return v if inner is None else v.rearrange("p (a b) -> p a b", b=inner)

    def attention_scratch():
        return [area(512, S) for _ in range(2)], [area(512, S) for _ in range(2)], [area(512, S) for _ in range(2)]

    s_buf, p_buf, pt_buf = attention_scratch()
    lru_ri = region[:, 0:12 * S].rearrange("p (b g s) -> p b g s", b=LB, g=2)
    lru_a = actT_flat[:, 0:LB * S].rearrange("p (b s) -> p b s", b=LB)
    xc = work_flat[:, 0:LB * S].rearrange("p (b s) -> p b s", b=LB)
    qa, ka, va = area(AH * S, S), area(AKV * S, S), area(TILES * AKV * HD, AKV * HD)
    xl, gl = area(LB * S, S), area(LB * S, S)
    qm, km, vm = area(MH * S, S), area(MH * S, S), area(TILES * MH * HD, MH * HD)
    gates = area(24 * S, S)
    rope_cos, rope_sin = region[:, 0:S], region[:, S:2 * S]
    ang, turns, rope_t = region[:, 2 * S:3 * S], region[:, 3 * S:4 * S], region[:, 4 * S:6 * S].rearrange("p (b s) -> p b s", b=2)
    pos_i = region[:, 6 * S:7 * S].bitcast(I32)

    top[0] = 7 * S
    pq = area(2 * PH * S, S)
    sc = area(TILES * 2 * PH * PK).rearrange("p (t c k) -> p t c k", t=TILES, k=PK)
    diag = area(TOPK * P, P)
    idx_u, idx_v, gate_st, u_dot, u_act, pick_w = (area(TILES * TOPK, TOPK, dt) for dt in (I32, I32, None, None, None, None))
    find, find_less = area(2 * PK, PK), area(2 * PK, PK)
    top_v, top_u, top_f = area(2 * TOPK, TOPK), area(2 * TOPK, TOPK, U32), area(2 * TOPK, TOPK)
    cand, cand_less = area(TOPK * TOPK), area(TOPK * TOPK)
    best, best_u, best_z, best_e = area(TOPK), area(TOPK, None, U32), area(TOPK), area(TOPK)
    place_u, place_f, key_f, idx_f = area(2 * TOPK, TOPK, U32), area(2 * TOPK, TOPK), area(2 * TOPK, TOPK), area(TOPK)
    hot = area(2 * TOPK * TOPK).rearrange("p (x k c) -> p x k c", x=2, c=TOPK)
    peer_top = top[0]
    U_SLOTS, V_SLOTS = (0, 1), (2, 3)
    assert UV * D == 2 * UNIT
    rows_of_slots = lambda ss: ring[:, ss[0] * UNIT:(ss[1] + 1) * UNIT].rearrange("p (r n) -> p r n", n=D)
    u_ring, v_ring = rows_of_slots(U_SLOTS), rows_of_slots(V_SLOTS)

    top[0] = 0
    attention_scratch()
    mem2T = region[:, REGION - KD * S:REGION].rearrange("p (k s) -> p k s", k=KD)
    q2, qm2 = area(SH // 2 * S, S), area(2 * S, S)
    kz = area(SH * S, S)
    assert top[0] <= 7 * S + 4 * PH * S
    v2 = area(TILES * SH * HD2, SH * HD2)
    k_raw = area(2 * S, S)
    f_log, f_cum, f_tmp = area(S), area(S), area(S)
    top[0] = max(top[0], peer_top)
    kmz, vm2 = area(MH2 * S, S), area(TILES * MH2 * HD2, MH2 * HD2)
    ffT = region[:, 0:FC * S].rearrange("p (f s) -> p f s", f=FC)
    silu_ff = region[:, FC * S:(FC + 2) * S].rearrange("p (b s) -> p b s", b=2)
    assert (FC + 2) * S <= top[0] <= REGION - KD * S
    top[0] = 0
    pick = area(TILES * P, P)
    pickg = area(TILES * P, P)
    pickT = area(TILES * P, P)
    xeT = area(KD * P, P)
    silu_e = area(2 * 2 * P).rearrange("p (b f s) -> p b f s", b=2, f=2)
    geT = area(FC * P, P)
    ye = area(D)
    logits, r_gate, r_mask, r_slot, r_hot = (area(TILES * NE, NE) for _ in range(5))
    r_top, r_idx, r_idxf = area(TILES * 8, 8), area(TILES * 8, 8, U32), area(TILES * 8, 8)
    r_e, r_den, r_g = area(TILES), area(TILES), area(TILES * 2, 2)
    r_shift = area(2)
    count_i = area(NE, None, I32)
    ones, before = area(P), area(P)

    stat, rstd = cell(2), cell(2)
    bn, mv = cell(TILES * 12), cell(TILES * 2)
    nmax, esum, esink, den = cell(4), cell(4), cell(4), cell(4)
    sp_e, sp_z, sp_p = cell(12), cell(12), cell(12)
    psum = ctx.enter_context(nc.psum_tensor("psum", [P, BANKS, 512], F32))

    weight_in = [sem(f"weight_in{s}") for s in range(RING)]
    product_ready = sem("product_ready")
    freed = {"vector": sem("freed_by_vector"), "scalar": sem("freed_by_scalar")}
    x_in, const_in, mem_in, pos_in, mem2_in = (sem(n) for n in ("x_in", "const_in", "mem_in", "pos_in", "mem2_in"))
    row_in = [sem("row_in0"), sem("row_in1")]
    row_used = sem("row_used")
    vector_step, scalar_step, pool_step = sem("vector_step"), sem("scalar_step"), sem("pool_step")
    square_ready, root_ready, normed = sem("square_ready"), sem("root_ready"), sem("normed")
    angle_ready, table_ready, rope_ready = sem("angle_ready"), sem("table_ready"), sem("rope_ready")
    max_ready, exp_ready, probs_ready = sem("max_ready"), sem("exp_ready"), sem("probs_ready")
    lam_exp, lam_ready, conv_ready = sem("lam_exp"), sem("lam_ready"), sem("conv_ready")
    lru_at, lru_sq_in, lru_sq_out, lru_done = sem("lru_at"), sem("lru_sq_in"), sem("lru_sq_out"), sem("lru_done")
    merged = sem("merged")
    best_ready, best_exp = sem("best_ready"), sem("best_exp")
    search_step, search_done, v_index, gathers = sem("search_step"), sem("search_done"), sem("v_index"), sem("gathers")
    u_in, v_in = [sem(f"u_in{k}") for k in range(UV)], [sem(f"v_in{k}") for k in range(UV)]
    dots_done, gelu_done, weights_done, diag_done = (sem(n) for n in ("dots_done", "gelu_done", "pick_weights_done", "diag_done"))
    v_used = sem("v_used")
    zeros_ready, forget_exp, forget_e, cum_ready = (sem(n) for n in ("zeros_ready", "forget_exp", "forget_e", "cum_ready"))
    silu_ready, ff_ready, ff_out_used = sem("silu_ready"), sem("ff_ready"), sem("ff_out_used")
    router_exp, router_e, routed, picked = (sem(n) for n in ("router_exp", "router_e", "routed", "picked"))
    e_product = sem("expert_product")
    e_freed = {"vector": sem("expert_freed_by_vector"), "scalar": sem("expert_freed_by_scalar")}
    e_silu, pick_step = sem("expert_silu"), sem("pick_step")
    out_done = sem("out_done")

    rows_order = ["g_mem", "g_mix", "g_ffn", "g_final"]
    for layer in range(2):
        for part in ("attn", "ffn"):
            rows_order += [("ln_" + part + "_g_2", layer), ("ln_" + part + "_b_2", layer)]

    heads = pl.heads
    N1 = len([h for h in heads if h[0] in ("self1", "mem1")])

    def wait_product(eng, name):
        eng.wait_ge(product_ready, pl.nth[name])
        return psum[:, pl.bank[name], :]

    def wait_freed(eng, name):
        by, n = pl.freed[name]
        eng.wait_ge(freed[by], n)

    def wait_row(eng, i):
        eng.wait_ge(row_in[i % 2], 16 * (i // 2 + 1))
        return rows[:, i % 2, :]

    class Own:

        def __init__(self, eng, s):
            self.eng, self.s, self.n = eng, s, 0

        def __call__(self, ins):
            self.n += 1
            ins.then_inc(self.s, 1)
            self.eng.wait_ge(self.s, self.n)

    STEPS = PH * TILES
    DOTS0, USED0 = UV, TOPK + 1

    def peer_steps(eng, step):
        step((0, 0), None, (1, 1))
        with eng.Fori(0, PH - 1) as h:
            step((h * TILES + 1, 1), (h * TILES, 0), (h * TILES + 2, 0))
            step((h * TILES + 2, 0), (h * TILES + 1, 1), (h * TILES + 3, 1))
        step((STEPS - 1, 1), (STEPS - 2, 0), None)
        step(None, (STEPS - 1, 1), None)

    E_BANK = {G0: 4, G1: 5, PT: 6}
    for n in range(FC // 2):
        E_BANK[UP0 + n] = n % 4
    E_BANK[Y0], E_BANK[Y0 + 1] = 6, 7
    for n in range(TILES * HALVES):
        E_BANK[SUM0 + n] = 4 + n % 2
    E_BY = {G0: "scalar", G1: "scalar", PT: "scalar", Y0: "scalar", Y0 + 1: "scalar"}
    for j in list(range(UP0, PART0)) + list(range(SUM0, N_EP)):
        E_BY[j] = "vector"
    E_NTH, e_n = {}, {"vector": 0, "scalar": 0}
    for j in sorted(E_BANK):
        e_n[E_BY[j]] += 1
        E_NTH[j] = e_n[E_BY[j]]
    E_PREV = {}
    for j in E_BANK:
        same = [i for i in sorted(E_BANK) if E_BANK[i] == E_BANK[j]]
        at = same.index(j)
        E_PREV[j] = (same[at - 1], 0) if at else (same[-1], 1)

    def each_expert(eng, body, skip, prepare=None):
        with eng.Fori(0, NE) as e:
            body(e, e, False)
        with eng.Fori(0, NE) as e:
            n = eng.value_load(count_i[0:1, bass.ds(e, 1)], min_val=0, max_val=S)
            with eng.If(n > P):
                body(e, e + NE, True)
            with eng.Else():
                skip(e + NE)

    block = ctx.enter_context(nc.Block())

    @block.sync
    def _(sp):
        after = [u[0] for u in pl.units].index("sub_keys") + 1
        peer_slots = [next(n for n in range(after, len(pl.units)) if pl.units[n][1] == s) for s in U_SLOTS + V_SLOTS]
        sp.dma_start(work[:, :, :], a["mem"][0].rearrange("(t p) n -> p t n", p=P)).then_inc(mem_in, 16)
        sp.dma_start(const[:, :], a["constants"]).then_inc(const_in, 16)
        sp.dma_start(cols[:, :], a["columns"]).then_inc(const_in, 16)
        sp.dma_start(x_tok[:, :, :], a["x"][0].rearrange("(t p) n -> p t n", p=P)).then_inc(x_in, 16)
        for n, (name, s, loads, _, before) in enumerate(pl.units):
            if n in peer_slots:
                sp.wait_ge(*((dots_done, DOTS0 + STEPS * TOPK) if s in U_SLOTS else (v_used, USED0 + STEPS * TOPK)))
            elif before is not None:
                if before[0] == "ff_out_used":
                    sp.wait_ge(ff_out_used, before[1] + 1)
                else:
                    sp.wait_ge(product_ready, pl.nth[before])
            for at, nk, n, src in loads:
                sp.dma_start(slot(s)[:, at:at + nk * n].rearrange("p (k n) -> p k n", k=nk), src).then_inc(weight_in[s], 16)
        sp.wait_ge(product_ready, len(pl.products))
        sp.wait_ge(routed, 1)

        def expert_loads(e, b, over):
            for j in range(N_EU):
                s = j % RING
                if j >= RING:
                    sp.wait_ge(e_product, b * N_EP + last_use(j - RING) + 1 + N_EP)
                else:
                    sp.wait_ge(e_product, b * N_EP + last_use(j - RING + N_EU) + 1)
                if j < FC // 2:
                    w = a["w_exp_in_2"][0][bass.ds(e, 1), :, :].rearrange("e (k p) n -> p (e k) n", p=P)
                    for half in range(2):
                        sp.dma_start(slot(s)[:, half * 8 * S:(half + 1) * 8 * S].rearrange("p (k n) -> p k n", k=KD),
                                     w[:, :, half * FF + S * j:half * FF + S * (j + 1)]).then_inc(weight_in[s], 16)
                else:
                    o = j - FC // 2
                    w = a["w_exp_out_2"][0][bass.ds(e, 1), :, :].rearrange("e (k p) n -> p (e k) n", p=P)
                    sp.dma_start(slot(s)[:, 0:OUT_ROWS[o] * D].rearrange("p (k n) -> p k n", n=D),
                                 w[:, 3 * o:3 * o + OUT_ROWS[o], :]).then_inc(weight_in[s], 16)

        def last_use(j):
            if j < FC // 2:
                return UP0 + j
            return PART0 + j - FC // 2 if j < N_EU - 1 else Y0 + 1

        def skip(b):
            for s in range(RING):
                sp.wait_ge(weight_in[s], b * per_expert[s] + pl.loaded[s])
                sp.sem_inc(weight_in[s], per_expert[s])

        each_expert(sp, expert_loads, skip)
        sp.wait_ge(normed, 8 * TILES)
        sp.dma_start(a["out"].rearrange("b (t p) n -> p (b t) n", p=P), x_tok[:, :, :]).then_inc(out_done, 16)
        sp.wait_ge(out_done, 16)

    @block.gpsimd
    def _(pool):
        own = Own(pool, pool_step)
        pool.dma_start(pos_i, a["positions"][0].partition_broadcast(P)).then_inc(pos_in, 16)

        def load_row(i):
            if i >= 2:
                pool.wait_ge(row_used, i - 1)
            name = rows_order[i]
            src = a[name[0]][name[1]] if isinstance(name, tuple) else (a[name] if name == "g_final" else a[name][0])
            pool.dma_start(rows[:, i % 2, :], src.partition_broadcast(P)).then_inc(row_in[i % 2], 16)

        for i in range(4):
            load_row(i)
        pool.wait_ge(product_ready, pl.nth[("out1", TILES - 1, HALVES - 1)])
        pool.dma_start(mem2T[:, :, :], a["mem_2_T"].rearrange("(k p) s -> p k s", p=P)).then_inc(mem2_in, 16)
        pool.dma_start(pos_i, a["positions_2"][0].partition_broadcast(P)).then_inc(pos_in, 16)
        pool.wait_ge(product_ready, pl.nth[("pq", 2 * PH - 1)])

        def gather_u(s, t, k):
            if k == 0:
                pool.wait_ge(search_done, s + 1)
            pool.wait_ge(dots_done, s * TOPK + k + 1)
            pool.sem_inc(gathers, 1)
            pool.indirect_dma_start(u_ring[:, k % UV, :], None, a["peer_u"][0],
                                    bass.IndirectOffsetOnAxis(idx_u[:, t, k:k + 1], 0)).then_inc(u_in[k % UV], 16)

        def gather_v(s, t, k):
            if k == 0:
                pool.wait_ge(v_index, s + 1)
            pool.wait_ge(v_used, USED0 + s * TOPK + k - UV + 1)
            pool.sem_inc(gathers, 1)
            pool.indirect_dma_start(v_ring[:, k % UV, :], None, a["peer_v"][0],
                                    bass.IndirectOffsetOnAxis(idx_v[:, t, k:k + 1], 0)).then_inc(v_in[k % UV], 16)

        AHEAD = 4

        def gathers_of_step(dots, total, search):
            for k in range(-AHEAD, TOPK):
                if dots is not None and k + AHEAD < TOPK:
                    gather_u(*dots, k + AHEAD)
                if total is not None and k >= 0:
                    gather_v(*total, k)

        peer_steps(pool, gathers_of_step)
        for i in range(4, len(rows_order)):
            load_row(i)

    @block.scalar
    def _(act):
        own = Own(act, scalar_step)

        def give(ins, name):
            ins.then_inc(freed["scalar"], 1)
            assert pl.freed[name] == ("scalar", give.n + 1), name
            give.n += 1

        give.n = 0

        def copy_out(name, dst, func=ACT.Copy, n=None, **kw):
            src = wait_product(act, name)
            n = n or dst.free_size()
            src = src[:, 0:n]
            if len(dst.shape) == 3:
                src = src.rearrange("p (a b) -> p a b", b=dst.shape[2])
            give(act.activation(dst, src, func, **kw), name)

        n_root = [0]

        def root():
            n_root[0] += 1
            act.wait_ge(square_ready, n_root[0])
            act.activation(rstd, stat, ACT.Sqrt).then_inc(root_ready, 1)

        def transposed(tag):
            for k in range(KD):
                copy_out((tag, k), actT[:, k, :])

        def rope_tables(i):
            act.wait_ge(angle_ready, 2 * i + 1)
            act.activation(rope_sin, ang, ACT.Sin).then_inc(table_ready, 1)
            act.wait_ge(angle_ready, 2 * i + 2)
            act.activation(rope_cos, turns, ACT.Sin).then_inc(table_ready, 1)

        def attention(base, n):
            for i in range(n + 2):
                if i < n:
                    g = base + i
                    b = g % 2
                    kind, h = heads[g]
                    act.wait_ge(max_ready, g + 1)
                    for t in range(TILES):
                        ins = act.activation(p_buf[b][:, t, :], s_buf[b][:, t, :], ACT.Exp, bias=nmax[:, 2 * b + t:2 * b + t + 1],
                                             accum_out=esum[:, 2 * b + t:2 * b + t + 1])
                    if kind in ("self1", "swa"):
                        sink = col("sink" if kind == "self1" else "sink2", h)
                        ins = act.activation(esink[:, 2 * b:2 * b + 2], nmax[:, 2 * b:2 * b + 2], ACT.Exp, bias=sink)
                    ins.then_inc(exp_ready, 1)
                if 1 <= i <= n:
                    g = base + i - 1
                    copy_out(("T", g), pt_buf[g % 2])

        root()
        transposed("memT")
        act.wait_ge(const_in, 32)
        for c in range(MH):
            copy_out(("km", c), km[:, c, :])
        for t in range(TILES):
            copy_out(("vm", t), vm[:, t, :])
        root()
        transposed("hT")
        rope_tables(0)
        for c in range(C_V):
            copy_out(("in", c), qa[:, c, :] if c < C_K else ka[:, c - C_K, :])
        for t in range(TILES):
            copy_out(("v", t), va[:, t, :])
        for c in range(C_XL, C_GL):
            copy_out(("in", c), xl[:, c - C_XL, :])
        for c in range(C_GL, C_QM):
            copy_out(("in", c), gl[:, c - C_GL, :], ACT.Gelu_apprx_tanh)
        for c in range(C_QM, C_G):
            copy_out(("in", c), qm[:, c - C_QM, :])
        for c in range(C_G, N_IN):
            copy_out(("in", c), gates[:, c - C_G, :], ACT.Sigmoid, bias=col("gate_b", c - C_G))
        attention(0, N1)
        act.wait_ge(lam_exp, 1)
        act.activation(sp_e, sp_z, ACT.Exp).then_inc(lam_exp, 1)
        act.wait_ge(lam_ready, 1)
        for d in range(2):
            if d:
                act.wait_ge(lru_done, 1)
            for b in range(LB):
                bank = wait_product(act, ("lru", d, b))
                act.activation(lru_ri[:, b, 0, :], bank[:, 0:S], ACT.Sigmoid, bias=col("lru_br", d * LB + b))
                give(act.activation(lru_ri[:, b, 1, :], bank[:, S:2 * S], ACT.Sigmoid, bias=col("lru_bi", d * LB + b)),
                     ("lru", d, b))
            act.wait_ge(freed["scalar"], pl.freed[("lru", d, LB - 1)][1])
            for b in range(LB):
                own(act.activation(lru_a[:, b, :], lru_ri[:, b, 0, :], ACT.Exp, scale=sp_e[:, d * LB + b:d * LB + b + 1]))
                act.activation(lru_ri[:, b, 0, :], lru_ri[:, b, 0, :], ACT.Tanh,
                               scale=sp_p[:, d * LB + b:d * LB + b + 1]).then_inc(lru_at, 1)
            for b in range(LB):
                act.wait_ge(lru_sq_in, d * LB + b + 1)
                act.activation(lru_ri[:, b, 0, :], lru_ri[:, b, 0, :], ACT.Sqrt).then_inc(lru_sq_out, 1)
        root()
        transposed("h2T")
        for c in range(2 * PH):
            copy_out(("pq", c), pq[:, c, :])
        for t in range(TILES):
            for g in range(4):
                copy_out(("sc", t, g), sc[:, t, 4 * g:4 * g + 4, :])
        for t in range(TILES):
            copy_out(("vm2", 0, t), vm2[:, t, :])

        def best_exps(s):
            act.wait_ge(best_ready, s + 1)
            act.activation(best_e, best_z, ACT.Exp, accum_out=esum[:, 0:1]).then_inc(best_exp, 1)

        def peer_step(dots, total, search):
            if total is not None:
                s, t = total
                act.wait_ge(weights_done, s + 1)
                for k in range(TOPK):
                    act.wait_ge(v_used, USED0 + (s - 1) * TOPK + k + 1)
                    act.activation(diag[:, k, :], ident, ACT.Copy, scale=pick_w[:, t, k:k + 1]).then_inc(diag_done, 1)
            if search is not None:
                best_exps(search[0])
            if dots is not None:
                s, t = dots
                act.wait_ge(dots_done, DOTS0 + s * TOPK + TOPK)
                act.activation(u_act[:, t, :], u_dot[:, t, :], ACT.Gelu_apprx_tanh).then_inc(gelu_done, 1)

        best_exps(0)
        peer_steps(act, peer_step)
        rope_tables(1)
        root()
        transposed("x2T")
        for layer in range(2):
            if layer:
                for t in range(TILES):
                    copy_out(("vm2", layer, t), vm2[:, t, :])
            nk = SKV if layer == 0 else SH // 2
            for c in range(SH // 2 + nk):
                name = ("in2", layer, c)
                if c < SH // 2:
                    copy_out(name, q2[:, c, :])
                elif layer == 0:
                    if c >= SH // 2 + 2:
                        act.wait_ge(rope_ready, C_V + c - 1)
                    copy_out(name, k_raw[:, c % 2, :])
                else:
                    bank = wait_product(act, name)
                    j = 2 * (c - SH // 2)
                    act.wait_ge(zeros_ready, 2)
                    act.activation(kz[0:HD2, j, :], bank[0:HD2, 0:S], ACT.Copy)
                    give(act.activation(kz[HD2:P, j + 1, :], bank[HD2:P, 0:S], ACT.Copy), name)
            for t in range(TILES):
                if layer == 0:
                    copy_out(("v2", 0, t, 0), v2[:, t, 0:2 * SKV * HD2])
                else:
                    copy_out(("v2", 1, t, 0), v2[:, t, 0:512])
                    copy_out(("v2", 1, t, 1), v2[:, t, 512:SH * HD2])
            for c in range(2):
                copy_out(("qm2", layer, c), qm2[:, c, :])
            if layer == 1:
                act.wait_ge(forget_exp, 1)
                own(act.activation(f_tmp[0:SH, :], f_tmp[0:SH, :], ACT.Exp))
                act.activation(f_tmp[0:SH, :], f_tmp[0:SH, :], ACT.Ln, bias=1.0).then_inc(forget_e, 1)
            attention(pl.att2[layer], SH + MH2)
            root()
            transposed(("aT", layer))
            if layer == 0:
                for f in range(FC):
                    bank = wait_product(act, ("ff", f))
                    if f >= 2:
                        act.wait_ge(ff_ready, f - 1)
                    act.activation(silu_ff[:, f % 2, :], bank[:, 0:S], ACT.Silu).then_inc(silu_ready, 1)
                root()
                transposed("x3T")
        act.wait_ge(router_exp, 1)
        act.activation(r_e, r_e, ACT.Exp).then_inc(router_e, 1)
        act.wait_ge(routed, 1)

        def wait_e(j, b):
            act.wait_ge(e_product, b * N_EP + j + 1 + N_EP)
            return psum[:, E_BANK[j], :]

        def expert(e, b, over):
            for j in (G0, G1):
                act.activation(xeT[:, 4 * j:4 * j + 4, :], wait_e(j, b).rearrange("p (k s) -> p k s", k=4), ACT.Copy)\
                   .then_inc(e_freed["scalar"], 1)
            act.activation(pickT[:, :, :], wait_e(PT, b)[:, 0:TILES * P].rearrange("p (t s) -> p t s", t=TILES), ACT.Copy)\
               .then_inc(e_freed["scalar"], 1)
            for n in range(FC // 2):
                bank = wait_e(UP0 + n, b).rearrange("p (f g s) -> p f g s", f=2, g=2)
                act.wait_ge(e_freed["vector"], b * e_n["vector"] + (e_n["vector"] + E_NTH[UP0 + n - 2] if n >= 2
                            else E_NTH[PART0 - 1 - n]))
                act.activation(silu_e[:, n % 2, :, :], bank[:, :, 0, :], ACT.Silu).then_inc(e_silu, 1)
            for h in range(HALVES):
                act.activation(ye[:, 512 * h:512 * h + 512], wait_e(Y0 + h, b), ACT.Copy).then_inc(e_freed["scalar"], 1)

        def skip(b):
            act.wait_ge(e_freed["scalar"], b * e_n["scalar"] + e_n["scalar"])
            act.sem_inc(e_freed["scalar"], e_n["scalar"])
            act.wait_ge(e_silu, b * (FC // 2))
            act.sem_inc(e_silu, FC // 2)

        act.sem_inc(e_freed["scalar"], e_n["scalar"])
        each_expert(act, expert, skip)
        root()

    @block.tensor
    def _(pe):
        def begin(name):
            i = pl.nth[name] - 1
            if i >= BANKS:
                wait_freed(pe, pl.products[i - BANKS])
            return psum[:, pl.bank[name], :]

        def end(ins, name):
            assert pl.nth[name] == end.n + 1, name
            end.n += 1
            ins.then_inc(product_ready, 1)

        end.n = 0

        def unit(name, nk, n, at=0):
            s, count = pl.unit[name]
            pe.wait_ge(weight_in[s], count)
            return slot(s)[:, at:at + nk * n].rearrange("p (k n) -> p k n", k=nk)

        def transposes(tag, src, nth):
            pe.wait_ge(normed, 2 * nth)
            for k in range(KD):
                bank = begin((tag, k))
                for t in range(TILES):
                    ins = pe.transpose(bank[:, t * P:(t + 1) * P], src[:, t, k * P:(k + 1) * P], ident)
                end(ins, (tag, k))

        def feature_major(name, w, c, src, nk):
            bank = begin(name)
            for k in range(nk):
                ins = pe.matmul(bank[:, 0:S], w[:, k, c * P:(c + 1) * P], src[:, k, :], start=(k == 0), stop=(k == nk - 1))
            end(ins, name)

        def token_major(name, w, t, n0, n, src, nk=KD):
            bank = begin(name)
            for k in range(nk):
                ins = pe.matmul(bank[:, 0:n], src[:, k, t * P:(t + 1) * P], w[:, k, n0:n0 + n], start=(k == 0), stop=(k == nk - 1))
            end(ins, name)

        def turn(name, rot, src, after):
            wait_freed(pe, after)
            end(pe.matmul(begin(name)[:, 0:S], C(rot), src, start=True, stop=True), name)

        def attention(base, n, queries, keys, values):
            for i in range(n + 2):
                if i < n:
                    g = base + i
                    kind, h = heads[g]
                    bank = begin(("S", g))
                    for t in range(TILES):
                        fox = kind == "fox"
                        ins = pe.matmul(bank[:, t * S:(t + 1) * S], queries(kind, h)[:, t * P:(t + 1) * P], keys(kind, h),
                                        start=True, stop=not fox)
                        if fox:
                            ins = pe.matmul(bank[:, t * S:(t + 1) * S], ident[0:SH, h:h + 1].to_broadcast([SH, P]), f_cum[0:SH, :],
                                            start=False, stop=True)
                    end(ins, ("S", g))
                if 1 <= i <= n:
                    g = base + i - 1
                    pe.wait_ge(probs_ready, g + 1)
                    bank = begin(("T", g))
                    for k in range(TILES):
                        for t in range(TILES):
                            ins = pe.transpose(bank[:, k * S + t * P:k * S + (t + 1) * P], p_buf[g % 2][:, t, k * P:(k + 1) * P], ident)
                    end(ins, ("T", g))
                if i >= 2:
                    g = base + i - 2
                    bank = begin(("V", g))
                    wait_freed(pe, ("T", g))
                    for k in range(TILES):
                        ins = pe.matmul(bank[:, 0:S], values(*heads[g], k), pt_buf[g % 2][:, k, :], start=(k == 0), stop=(k == TILES - 1))
                    end(ins, ("V", g))

        pe.wait_ge(const_in, 32)
        transposes("memT", work, 1)
        wait_freed(pe, ("memT", KD - 1))
        w = unit(("mem_kv", 0), KD, 512)
        for c in range(MH):
            feature_major(("km", c), w, c, actT, KD)
        w = unit(("mem_kv", 1), KD, 512)
        for t in range(TILES):
            token_major(("vm", t), w, t, 0, 512, actT)
        transposes("hT", work, 2)
        wait_freed(pe, ("hT", KD - 1))
        qk = lambda c: qa[:, c, :] if c < C_K else ka[:, c - C_K, :]
        for c in range(C_V):
            feature_major(("in", c), unit(("w_in", c // 4), KD, 512), c % 4, actT, KD)
            if c >= 1:
                turn(("rope", c - 1), "rot1", qk(c - 1), ("in", c - 1))
        for t in range(TILES):
            token_major(("v", t), unit(("w_in", 2), KD, 512), t, 0, AKV * HD, actT)
            if t == 0:
                turn(("rope", C_V - 1), "rot1", qk(C_V - 1), ("in", C_V - 1))
        for c in range(C_XL, N_IN):
            feature_major(("in", c), unit(("w_in", c // 4), KD, 512 if c < 48 else 256), c % 4, actT, KD)
        pe.wait_ge(rope_ready, C_V)
        attention(0, N1, lambda kind, h: (qa if kind == "self1" else qm)[:, h, :],
                  lambda kind, h: ka[:, h // GROUP, :] if kind == "self1" else km[:, h, :],
                  lambda kind, h, k: va[:, k, h // GROUP * HD:(h // GROUP + 1) * HD] if kind == "self1" else vm[:, k, h * HD:(h + 1) * HD])
        wr, wi = unit("lru_w", 12, P), unit("lru_w", 12, P, 12 * P)
        pe.wait_ge(conv_ready, LB)
        for d in range(2):
            for b in range(LB):
                bank = begin(("lru", d, b))
                pe.matmul(bank[:, 0:S], wr[:, d * LB + b, :], xc[:, b, :], start=True, stop=True)
                end(pe.matmul(bank[:, S:2 * S], wi[:, d * LB + b, :], xc[:, b, :], start=True, stop=True), ("lru", d, b))
        wait_freed(pe, ("V", N1 - 1))
        for br, (name, nk, src) in enumerate((("p_attn", AH, qa), ("p_lru", LB, gl), ("p_mem", MH, qm))):
            if br == 1:
                pe.wait_ge(lru_done, 2)
            for c in range(KD):
                feature_major(("merge", br, c), unit((name, c // 4), nk, 512), c % 4, src, nk)
        pe.wait_ge(merged, KD)
        for t in range(TILES):
            for h in range(HALVES):
                token_major(("out1", t, h), unit(("w_out", h), KD, 512), t, 0, 512, gates)
        transposes("h2T", work, 3)
        wait_freed(pe, ("h2T", KD - 1))
        for c in range(2 * PH):
            feature_major(("pq", c), unit(("peer_q", c // 4), KD, 512), c % 4, actT, KD)
        wait_freed(pe, ("pq", 2 * PH - 1))
        keys = unit("sub_keys", 2 * PH, PK)
        for t in range(TILES):
            for g in range(4):
                bank = begin(("sc", t, g))
                for c in range(4):
                    ins = pe.matmul(bank[:, c * PK:(c + 1) * PK], pq[:, 4 * g + c, t * P:(t + 1) * P], keys[:, 4 * g + c, :],
                                    start=True, stop=True)
                end(ins, ("sc", t, g))

        def memory2(layer):
            w = unit(("mem_kv2", layer), KD, 512)
            for c in range(2):
                feature_major(("km2", layer, c), w, c, mem2T, KD)
            for t in range(TILES):
                token_major(("vm2", layer, t), w, t, 256, 256, mem2T)

        pe.wait_ge(mem2_in, 16)
        memory2(0)
        wait_freed(pe, ("km2", 0, 1))
        wait_freed(pe, ("vm2", 0, TILES - 1))
        pe.sem_inc(v_used, USED0)

        def weighted_sum(s, t, first):
            for k in range(TOPK):
                pe.wait_ge(diag_done, s * TOPK + k + 1)
                pe.wait_ge(v_in[k % UV], s * 32 + 16 * (k // UV + 1))
                for half in range(HALVES):
                    ins = pe.matmul(psum[:, 2 * t + half, :], diag[:, k, :], v_ring[:, k % UV, 512 * half:512 * half + 512],
                                    start=(first and k == 0), stop=(k == TOPK - 1), skip_group_check=True)
                ins.then_inc(v_used, 1)

        for t in range(TILES):
            weighted_sum(t, t, True)
        with pe.Fori(1, PH) as h:
            for t in range(TILES):
                weighted_sum(h * TILES + t, t, False)
        transposes("x2T", x_tok, 4)
        wait_freed(pe, ("x2T", KD - 1))
        for layer in range(2):
            if layer:
                memory2(layer)
            nk = SKV if layer == 0 else SH // 2
            raw = lambda c: q2[:, c, :] if c < SH // 2 else k_raw[:, c % 2, :]
            if layer == 1:
                wait_freed(pe, ("x3T", KD - 1))
            for c in range(SH // 2 + nk):
                feature_major(("in2", layer, c), unit(("w_in2", layer, c // 4), KD, 512), c % 4, actT, KD)
                if c >= 1 and layer == 0:
                    turn(("rope2", c - 1), "rot2", raw(c - 1), ("in2", 0, c - 1))
            if layer == 0:
                turn(("rope2", SH // 2 + nk - 1), "rot2", raw(SH // 2 + nk - 1), ("in2", 0, SH // 2 + nk - 1))
                for t in range(TILES):
                    token_major(("v2", 0, t, 0), unit(("w_in2", 0, 2), KD, 512), t, P, 3 * P, actT)
                for c in range(2):
                    feature_major(("qm2", 0, c), unit(("w_in2", 0, 3), KD, 256), c, actT, KD)
                pe.wait_ge(rope_ready, C_V + SH // 2 + nk)
            else:
                for t in range(TILES):
                    token_major(("v2", 1, t, 0), unit(("w_in2", 1, 3), KD, 512), t, 0, 512, actT)
                    token_major(("v2", 1, t, 1), unit(("w_in2", 1, 4), KD, 512), t, 0, 256, actT)
                for c in range(2):
                    feature_major(("qm2", 1, c), unit(("w_in2", 1, 4), KD, 512), 2 + c, actT, KD)
                bank = begin(("forget",))
                wf = col("w_forget", 0, KD * SH).rearrange("p (k n) -> p k n", k=KD)
                for k in range(KD):
                    ins = pe.matmul(bank[0:SH, 0:S], wf[:, k, :], actT[:, k, :], start=(k == 0), stop=(k == KD - 1))
                end(ins, ("forget",))
                pe.wait_ge(cum_ready, 1)
            wait_freed(pe, ("qm2", layer, 1))
            attention(pl.att2[layer], SH + MH2,
                      lambda kind, h: qm2[:, h // 2, :] if kind == "mem2" else q2[:, h // 2, :],
                      lambda kind, h: {"swa": lambda: kz[:, 2 * (h // 4) + h % 2, :], "fox": lambda: kz[:, h, :],
                                       "mem2": lambda: kmz[:, h, :]}[kind](),
                      lambda kind, h, k: {"swa": lambda: v2[:, k, h // 4 * P:(h // 4 + 1) * P],
                                          "fox": lambda: v2[:, k, h // 2 * P:(h // 2 + 1) * P],
                                          "mem2": lambda: vm2[:, k, h // 2 * P:(h // 2 + 1) * P]}[kind]())
            wait_freed(pe, ("V", pl.att2[layer] + SH + MH2 - 1))
            for t in range(TILES):
                for h in range(HALVES):
                    token_major(("out2", layer, t, h), unit(("w_out2", layer, h), KD, 512), t, 0, 512, actT)
            transposes(("aT", layer), x_tok, 5 + 2 * layer)
            wait_freed(pe, (("aT", layer), KD - 1))
            if layer == 0:
                for f in range(FC):
                    w = unit(("ff_in", f // 2), 2 * KD, S)
                    bank = begin(("ff", f))
                    for g in range(2):
                        for k in range(KD):
                            ins = pe.matmul(bank[:, g * S:(g + 1) * S], w[:, g * KD + k, f % 2 * P:(f % 2 + 1) * P], actT[:, k, :],
                                            start=(k == 0), stop=(k == KD - 1))
                    end(ins, ("ff", f))
                pe.wait_ge(ff_ready, FC)
                for t in range(TILES):
                    for h in range(HALVES):
                        begin(("down", t, h))
                f = 0
                for o, n in enumerate(OUT_ROWS):
                    w = unit(("ff_out", o), n, D)
                    for k in range(n):
                        for t in range(TILES):
                            for h in range(HALVES):
                                ins = pe.matmul(psum[:, pl.bank[("down", t, h)], :], ffT[:, f, t * P:(t + 1) * P],
                                                w[:, k, 512 * h:512 * h + 512], start=(f == 0), stop=(f == FC - 1))
                                if f == FC - 1:
                                    end(ins, ("down", t, h))
                        f += 1
                    if o < len(OUT_ROWS) - 1:
                        ins.then_inc(ff_out_used, 1)
                transposes("x3T", x_tok, 6)
        wr = col("w_router", 0, KD * NE).rearrange("p (k n) -> p k n", k=KD)
        for t in range(TILES):
            token_major(("router", t), wr, t, 0, NE, actT)
        pe.wait_ge(router_e, 2)
        bank = begin(("place",))
        pe.matmul(bank[:, 0:NE], before, r_mask[:, 0, :], start=True, stop=True)
        pe.matmul(bank[:, NE:2 * NE], before, r_mask[:, 1, :], start=True, stop=False)
        pe.matmul(bank[:, NE:2 * NE], ones, r_mask[:, 0, :], start=False, stop=True)
        pe.matmul(bank[:, 2 * NE:3 * NE], ones, r_mask[:, 0, :], start=True, stop=False)
        end(pe.matmul(bank[:, 2 * NE:3 * NE], ones, r_mask[:, 1, :], start=False, stop=True), ("place",))
        pe.wait_ge(routed, 1)
        wait_freed(pe, ("place",))

        def bank_of(j, b):
            i, back = E_PREV[j]
            by = E_BY[i]
            pe.wait_ge(e_freed[by], b * e_n[by] + E_NTH[i] + (0 if back else e_n[by]))
            return psum[:, E_BANK[j], :]

        def expert_unit(j, b):
            s = j % RING
            pe.wait_ge(weight_in[s], b * per_expert[s] + pl.loaded[s] + e_loaded[j])
            return slot(s)

        def expert(e, b, over):
            pe.wait_ge(picked, b + 1)
            for j in (G0, G1):
                bank = bank_of(j, b)
                for k in range(4):
                    for t in range(TILES):
                        ins = pe.matmul(bank[:, k * P:(k + 1) * P], x_tok[:, t, (4 * j + k) * P:(4 * j + k + 1) * P], pick[:, t, :],
                                        start=(t == 0), stop=(t == TILES - 1))
                ins.then_inc(e_product, 1)
            bank = bank_of(PT, b)
            for t in range(TILES):
                ins = pe.transpose(bank[:, t * P:(t + 1) * P], pickg[:, t, :], ident)
            ins.then_inc(e_product, 1)
            pe.wait_ge(e_freed["scalar"], b * e_n["scalar"] + e_n["scalar"] + E_NTH[G1])
            for n in range(FC // 2):
                bank = bank_of(UP0 + n, b)
                w = expert_unit(n, b).rearrange("p (g k f s) -> p g k f s", g=2, k=KD, f=2)
                for f in range(2):
                    for g in range(2):
                        for k in range(KD):
                            ins = pe.matmul(bank[:, (2 * f + g) * P:(2 * f + g + 1) * P], w[:, g, k, f, :], xeT[:, k, :],
                                            start=(k == 0), stop=(k == KD - 1))
                ins.then_inc(e_product, 1)
            banks = [bank_of(Y0 + h, b) for h in range(HALVES)]
            pe.wait_ge(e_freed["vector"], b * e_n["vector"] + e_n["vector"] + E_NTH[PART0 - 1])
            f = 0
            for o, n in enumerate(OUT_ROWS):
                w = expert_unit(FC // 2 + o, b)[:, 0:n * D].rearrange("p (k n) -> p k n", n=D)
                for k in range(n):
                    for h in range(HALVES):
                        ins = pe.matmul(banks[h], geT[:, f, :], w[:, k, 512 * h:512 * h + 512], start=(f == 0), stop=(f == FC - 1))
                        if f == FC - 1:
                            ins.then_inc(e_product, 1)
                    f += 1
                if o < len(OUT_ROWS) - 1:
                    ins.then_inc(e_product, 1)
            for t in range(TILES):
                for h in range(HALVES):
                    j = SUM0 + t * HALVES + h
                    bank = bank_of(j, b)
                    pe.wait_ge(e_freed["scalar"], b * e_n["scalar"] + e_n["scalar"] + E_NTH[Y0 + h])
                    pe.matmul(bank, pickT[:, t, :], ye[:, 512 * h:512 * h + 512], start=True, stop=True).then_inc(e_product, 1)

        def skip(b):
            pe.wait_ge(e_product, b * N_EP + N_EP)
            pe.sem_inc(e_product, N_EP)

        pe.sem_inc(e_product, N_EP)
        each_expert(pe, expert, skip)

    @block.vector
    def _(dve):
        own = Own(dve, vector_step)

        def give(ins, name, wait=False):
            ins.then_inc(freed["vector"], 1)
            assert pl.freed[name] == ("vector", give.n + 1), name
            give.n += 1
            if wait:
                dve.wait_ge(freed["vector"], give.n)

        give.n = 0
        n_square, n_normed, n_row, n_angle, n_rope = [0], [0], [0], [0], [0]

        def tell(ins, s, count, wait=False):
            count[0] += 1
            ins.then_inc(s, 1)
            if wait:
                dve.wait_ge(s, count[0])

        def rms_norm(src, dst):
            for t in range(TILES):
                own(dve.tensor_tensor_reduce(dst[:, t, :] if dst is not src else rms_junk, src[:, t, :], src[:, t, :], 1.0, 0.0, ALU.mult, ALU.add,
                                             stat[:, t:t + 1]))
            tell(dve.tensor_scalar(stat, stat, 1.0 / D, EPS, ALU.mult, ALU.add), square_ready, n_square)
            dve.wait_ge(root_ready, n_square[0])
            own(dve.reciprocal(rstd, rstd))
            row = wait_row(dve, n_row[0])
            n_row[0] += 1
            for t in range(TILES):
                tell(dve.scalar_tensor_tensor(dst[:, t, :], src[:, t, :], rstd[:, t:t + 1], row, ALU.mult, ALU.mult), normed, n_normed, True)
            dve.sem_inc(row_used, 1)

        rms_junk = work[:, 0, :]

        def layer_norm():
            for t in range(TILES):
                for h in range(2):
                    own(dve.bn_stats(bn[:, 12 * t + 6 * h:12 * t + 6 * h + 6], x_tok[:, t, 512 * h:512 * h + 512]))
                own(dve.bn_aggr(mv[:, 2 * t:2 * t + 2], bn[:, 12 * t:12 * t + 12]))
                own(dve.tensor_scalar(stat[:, t:t + 1], mv[:, 2 * t + 1:2 * t + 2], LN_EPS, None, ALU.add))
            dve.sem_inc(square_ready, 1)
            n_square[0] += 1
            dve.wait_ge(root_ready, n_square[0])
            own(dve.reciprocal(rstd, rstd))
            g, b = wait_row(dve, n_row[0]), wait_row(dve, n_row[0] + 1)
            n_row[0] += 2
            for t in range(TILES):
                own(dve.tensor_scalar(x_tok[:, t, :], x_tok[:, t, :], mv[:, 2 * t:2 * t + 1], rstd[:, t:t + 1], ALU.subtract, ALU.mult))
            for t in range(TILES):
                own(dve.tensor_tensor(x_tok[:, t, :], x_tok[:, t, :], g, ALU.mult))
            for t in range(TILES):
                tell(dve.tensor_tensor(x_tok[:, t, :], x_tok[:, t, :], b, ALU.add), normed, n_normed, True)
            dve.sem_inc(row_used, 2)

        TURN = 2 * math.pi
        T1 = 6.28125
        T2 = round((TURN - T1) * 2 ** 20) / 2 ** 20
        T3 = TURN - T1 - T2
        ROUND = 1.5 * 2 ** 23
        PI = 3.1415925

        def rope_tables(i):
            dve.wait_ge(pos_in, 16 * (i + 1))
            own(dve.tensor_copy(ang, pos_i))
            own(dve.tensor_scalar(ang, ang, C(("freq1", "freq2")[i]), None, ALU.mult))
            own(dve.tensor_scalar(turns, ang, 1.0 / TURN, ROUND, ALU.mult, ALU.add))
            own(dve.tensor_scalar(turns, turns, ROUND, None, ALU.subtract))
            for part in (T1, T2, T3):
                own(dve.scalar_tensor_tensor(ang, turns, -part, ang, ALU.mult, ALU.add))
            tell(dve.tensor_scalar(ang, ang, PI, -PI, ALU.min, ALU.max), angle_ready, n_angle, True)
            own(dve.scalar_tensor_tensor(turns, ang, -1.0, ang, ALU.mult, ALU.min))
            tell(dve.tensor_scalar(turns, turns, math.pi / 2, None, ALU.add), angle_ready, n_angle)

        def rope(name, raw, after, outs=None):
            bank = wait_product(dve, name)
            dve.wait_ge(table_ready, 2 if name[0] == "rope" else 4)
            t = rope_t[:, n_rope[0] % 2, :]
            wait_freed(dve, after)
            give(dve.tensor_tensor(t, bank[:, 0:S], rope_sin, ALU.mult), name, True)
            own(dve.tensor_tensor(raw, raw, rope_cos, ALU.mult))
            if outs is None:
                tell(dve.tensor_tensor(raw, raw, t, ALU.add), rope_ready, n_rope, True)
            else:
                own(dve.tensor_tensor(outs[0][0:HD2], raw[0:HD2], t[0:HD2], ALU.add))
                tell(dve.tensor_tensor(outs[1][HD2:P], raw[HD2:P], t[HD2:P], ALU.add), rope_ready, n_rope, True)

        n_max, n_probs = [0], [0]

        def attention(base, n, out):
            for i in range(n + 2):
                if i < n:
                    g = base + i
                    b = g % 2
                    kind, h = heads[g]
                    bank = wait_product(dve, ("S", g)).rearrange("p (t s) -> p t s", t=TILES)
                    mask = {"self1": "band", "swa": "chunks", "fox": "causal"}.get(kind)
                    scale = HD ** -0.5 if kind in ("self1", "mem1") else SCALE2
                    if mask:
                        ins = dve.scalar_tensor_tensor(s_buf[b], bank, scale, C(mask).rearrange("p (t s) -> p t s", t=TILES), ALU.mult, ALU.add)
                    else:
                        ins = dve.tensor_scalar(s_buf[b], bank, scale, None, ALU.mult)
                    give(ins, ("S", g), True)
                    m = nmax[:, 2 * b:2 * b + 2]
                    own(dve.tensor_reduce(m, s_buf[b], AX.X, ALU.max))
                    if kind in ("self1", "swa"):
                        ins = dve.tensor_scalar(m, m, col("sink" if kind == "self1" else "sink2", h), -1.0, ALU.max, ALU.mult)
                    else:
                        ins = dve.tensor_scalar(m, m, -1.0, None, ALU.mult)
                    tell(ins, max_ready, n_max)
                if 1 <= i <= n:
                    g = base + i - 1
                    b = g % 2
                    kind, h = heads[g]
                    dve.wait_ge(exp_ready, g + 1)
                    dd, ss = den[:, 2 * b:2 * b + 2], esum[:, 2 * b:2 * b + 2]
                    if kind in ("self1", "swa"):
                        own(dve.tensor_tensor(dd, ss, esink[:, 2 * b:2 * b + 2], ALU.add))
                        ss = dd
                    own(dve.reciprocal(dd, ss))
                    for t in range(TILES):
                        ins = dve.tensor_scalar(p_buf[b][:, t, :], p_buf[b][:, t, :], den[:, 2 * b + t:2 * b + t + 1], None, ALU.mult)
                    tell(ins, probs_ready, n_probs)
                if i >= 2:
                    g = base + i - 2
                    bank = wait_product(dve, ("V", g))
                    p0, p1, dst = out(*heads[g])
                    give(dve.tensor_copy(dst[p0:p1], bank[p0:p1, 0:S]), ("V", g))

        dve.wait_ge(mem_in, 16)
        dve.wait_ge(const_in, 32)
        for t in range(TILES):
            own(dve.tensor_tensor_reduce(region[:, 4096 + t * D:4096 + (t + 1) * D], work[:, t, :], work[:, t, :], 1.0, 0.0, ALU.mult, ALU.add, stat[:, t:t + 1]))
        tell(dve.tensor_scalar(stat, stat, 1.0 / D, EPS, ALU.mult, ALU.add), square_ready, n_square)
        dve.wait_ge(root_ready, 1)
        own(dve.reciprocal(rstd, rstd))
        row = wait_row(dve, 0)
        n_row[0] = 1
        for t in range(TILES):
            tell(dve.scalar_tensor_tensor(work[:, t, :], work[:, t, :], rstd[:, t:t + 1], row, ALU.mult, ALU.mult), normed, n_normed, True)
        dve.sem_inc(row_used, 1)
        rope_tables(0)
        dve.wait_ge(x_in, 16)
        dve.wait_ge(product_ready, pl.nth[("memT", KD - 1)])
        rms_norm(x_tok, work)
        for c in range(C_V):
            rope(("rope", c), qa[:, c, :] if c < C_K else ka[:, c - C_K, :], ("in", c))
        dve.wait_ge(product_ready, pl.nth[("hT", KD - 1)])
        for b in range(LB):
            wait_freed(dve, ("in", C_XL + b))
            w = lambda j: col("conv_w", j * LB + b)
            own(dve.tensor_scalar(xc[:, b, :], xl[:, b, :], w(2), col("conv_b", b), ALU.mult, ALU.add))
            own(dve.scalar_tensor_tensor(xc[:, b, 2:S], xl[:, b, 0:S - 2], w(0), xc[:, b, 2:S], ALU.mult, ALU.add))
            own(dve.scalar_tensor_tensor(xc[:, b, 1:S], xl[:, b, 0:S - 1], w(1), xc[:, b, 1:S], ALU.mult, ALU.add))
            dve.scalar_tensor_tensor(xc[:, b, 0:S - 1], xl[:, b, 1:S], w(3), xc[:, b, 0:S - 1], ALU.mult, ALU.add).then_inc(conv_ready, 1)
        attention(0, N1, lambda kind, h: (0, P, (qa if kind == "self1" else qm)[:, h, :]))
        lam = col("lam", 0, 12)
        own(dve.tensor_scalar(sp_p, lam, -1.0, None, ALU.mult))
        dve.tensor_tensor(sp_z, sp_p, lam, ALU.min).then_inc(lam_exp, 1)
        dve.wait_ge(lam_exp, 2)
        own(dve.tensor_scalar(sp_z, sp_e, 2.0, None, ALU.add))
        own(dve.reciprocal(sp_z, sp_z))
        own(dve.tensor_tensor(sp_e, sp_e, sp_z, ALU.mult))
        own(dve.tensor_tensor(sp_z, sp_e, sp_e, ALU.mult))
        own(dve.tensor_scalar(sp_p, sp_z, 1.0 / 17, 1.0 / 15, ALU.mult, ALU.add))
        for n in (13, 11, 9, 7, 5, 3, 1):
            own(dve.tensor_tensor(sp_p, sp_p, sp_z, ALU.mult))
            own(dve.tensor_scalar(sp_p, sp_p, 1.0 / n, None, ALU.add))
        own(dve.scalar_tensor_tensor(sp_e, sp_e, 2.0, sp_p, ALU.mult, ALU.mult))
        own(dve.tensor_scalar(sp_p, lam, -1.0, 0.0, ALU.mult, ALU.max))
        own(dve.tensor_tensor(sp_p, sp_p, sp_e, ALU.add))
        own(dve.tensor_scalar(sp_e, sp_p, -8.0, None, ALU.mult))
        dve.tensor_scalar(sp_p, sp_p, 8.0, None, ALU.mult).then_inc(lam_ready, 1)
        for d in range(2):
            for b in range(LB):
                r, i = lru_ri[:, b, 0, :], lru_ri[:, b, 1, :]
                dve.wait_ge(lru_at, d * LB + b + 1)
                own(dve.tensor_tensor(i, i, xc[:, b, :], ALU.mult))
                tmp = actT_flat[:, LB * S:LB * S + S]
                own(dve.tensor_tensor(tmp, lru_a[:, b, :], lru_a[:, b, :], ALU.mult))
                dve.scalar_tensor_tensor(r, tmp, 1.0, r, ALU.add, ALU.mult).then_inc(lru_sq_in, 1)
                dve.wait_ge(lru_sq_in, d * LB + b + 1)
            for b in range(LB):
                r, i = lru_ri[:, b, 0, :], lru_ri[:, b, 1, :]
                dve.wait_ge(lru_sq_out, d * LB + b + 1)
                own(dve.tensor_tensor(i, i, r, ALU.mult))
                if d == 0:
                    own(dve.tensor_tensor_scan(xl[:, b, :], lru_a[:, b, :], i, 0.0, ALU.mult, ALU.add))
                else:
                    own(dve.tensor_tensor_scan(r[:, ::-1], lru_a[:, b, ::-1], i[:, ::-1], 0.0, ALU.mult, ALU.add))
                    own(dve.tensor_tensor(r, r, xl[:, b, :], ALU.add))
                    own(dve.tensor_tensor(gl[:, b, :], gl[:, b, :], r, ALU.mult))
            dve.sem_inc(lru_done, 1)
        for br in range(3):
            for c in range(KD):
                bank = wait_product(dve, ("merge", br, c))[:, 0:S]
                if br == 0:
                    give(dve.tensor_tensor(gates[:, c, :], gates[:, c, :], bank, ALU.mult), ("merge", br, c), True)
                else:
                    gg = gates[:, br * KD + c, :]
                    give(dve.tensor_tensor(gg, gg, bank, ALU.mult), ("merge", br, c), True)
                    ins = dve.tensor_tensor(gates[:, c, :], gates[:, c, :], gg, ALU.add)
                    if br == 1:
                        own(ins)
                    else:
                        ins.then_inc(merged, 1)
        for t in range(TILES):
            for h in range(HALVES):
                bank = wait_product(dve, ("out1", t, h))
                xx = x_tok[:, t, 512 * h:512 * h + 512]
                give(dve.tensor_tensor(xx, xx, bank, ALU.add), ("out1", t, h), True)
        rms_norm(x_tok, work)
        for t in range(TILES):
            for g in range(4):
                wait_freed(dve, ("sc", t, g))
        dve.sem_inc(dots_done, DOTS0)

        def search_for(s, t):
            n = [0]

            def step(ins, wait=True):
                n[0] += 1
                ins.then_inc(search_step, 1)
                if wait:
                    wait_steps()

            def wait_steps():
                dve.wait_ge(search_step, s * N_SEARCH + n[0])

            def wait_turn():
                n[0] += 1
                dve.sem_inc(search_step, 1)

            head = bass.ds((s - t), 2) if not isinstance(s, int) else slice(s - t, s - t + 2)
            step(dve.tensor_copy(find, sc[:, t, head, :]))
            wait_turn()
            step(dve.max(top_v[:, 0, 0:8], find[:, 0, :]), False)
            step(dve.max(top_v[:, 1, 0:8], find[:, 1, :]))
            wait_turn()
            for x in range(2):
                step(dve.match_replace(find_less[:, x, :], top_v[:, x, 0:8], find[:, x, :], -3.0e38), False)
                step(dve.max_index(top_u[:, x, 0:8], top_v[:, x, 0:8], find[:, x, :]), x == 1)
            wait_turn()
            step(dve.max(top_v[:, 0, 8:16], find_less[:, 0, :]), False)
            step(dve.max(top_v[:, 1, 8:16], find_less[:, 1, :]))
            step(dve.tensor_tensor(cand.rearrange("p (i j) -> p i j", i=TOPK), top_v[:, 0, :].unsqueeze(2).to_broadcast([P, TOPK, TOPK]),
                                   top_v[:, 1, :].unsqueeze(1).to_broadcast([P, TOPK, TOPK]), ALU.add), False)
            for x in range(2):
                step(dve.max_index(top_u[:, x, 8:16], top_v[:, x, 8:16], find_less[:, x, :]), x == 1)
            step(dve.tensor_copy(top_f, top_u), False)
            step(dve.max(best[:, 0:8], cand))
            wait_turn()
            step(dve.match_replace(cand_less, best[:, 0:8], cand, -3.0e38), False)
            step(dve.max_index(best_u[:, 0:8], best[:, 0:8], cand))
            wait_turn()
            step(dve.max(best[:, 8:16], cand_less))
            step(dve.tensor_scalar(best_z, best, best[:, 0:1], None, ALU.subtract), False)
            wait_steps()
            dve.sem_inc(best_ready, 1)
            step(dve.max_index(best_u[:, 8:16], best[:, 8:16], cand_less))
            step(dve.tensor_scalar(place_u[:, 0, :], best_u, 4, None, ALU.logical_shift_right), False)
            step(dve.tensor_scalar(place_u[:, 1, :], best_u, 15, None, ALU.bitwise_and))
            step(dve.tensor_copy(place_f, place_u))
            step(dve.tensor_tensor(hot, place_f.unsqueeze(3).to_broadcast([P, 2, TOPK, TOPK]),
                                   C("iota")[:, 0:TOPK].unsqueeze(1).unsqueeze(1).to_broadcast([P, 2, TOPK, TOPK]), ALU.is_equal))
            step(dve.tensor_tensor(hot, hot, top_f.unsqueeze(2).to_broadcast([P, 2, TOPK, TOPK]), ALU.mult))
            step(dve.tensor_reduce(key_f, hot, AX.X, ALU.add))
            step(dve.scalar_tensor_tensor(idx_f, key_f[:, 0, :], float(PK), key_f[:, 1, :], ALU.mult, ALU.add))
            step(dve.tensor_copy(idx_u[:, t, :], idx_f))
            dve.sem_inc(search_done, 1)
            dve.wait_ge(best_exp, s + 1)
            step(dve.reciprocal(den[:, 0:1], esum[:, 0:1]))
            step(dve.tensor_scalar(gate_st[:, t, :], best_e, den[:, 0:1], None, ALU.mult))
            assert n[0] == N_SEARCH

        N_SEARCH = 34

        def peer_step(dots, total, search):
            if total is not None:
                s, t = total
                dve.wait_ge(v_used, USED0 + (s - 1) * TOPK)
                dve.tensor_copy(idx_v[:, t, :], idx_u[:, t, :]).then_inc(v_index, 1)
                dve.wait_ge(gelu_done, s + 1)
                dve.tensor_tensor(pick_w[:, t, :], u_act[:, t, :], gate_st[:, t, :], ALU.mult).then_inc(weights_done, 1)
                dve.wait_ge(v_index, s + 1)
                dve.wait_ge(weights_done, s + 1)
            if search is not None:
                search_for(*search)
            if dots is not None:
                s, t = dots
                for k in range(TOPK):
                    dve.wait_ge(u_in[k % UV], s * 32 + 16 * (k // UV + 1))
                    dve.tensor_tensor_reduce(u_ring[:, k % UV, :], u_ring[:, k % UV, :], work[:, t, :], 1.0, 0.0, ALU.mult, ALU.add,
                                             u_dot[:, t, k:k + 1]).then_inc(dots_done, 1)

        search_for(0, 0)
        own(dve.memset(kmz, 0.0))

        def memory_keys(layer):
            for c in range(2):
                bank = wait_product(dve, ("km2", layer, c))
                own(dve.tensor_copy(kmz[0:HD2, 2 * c, :], bank[0:HD2, 0:S]))
                give(dve.tensor_copy(kmz[HD2:P, 2 * c + 1, :], bank[HD2:P, 0:S]), ("km2", layer, c))

        memory_keys(0)
        peer_steps(dve, peer_step)
        dve.memset(kz, 0.0).then_inc(zeros_ready, 1)
        dve.wait_ge(zeros_ready, 1)
        rope_tables(1)
        dve.wait_ge(v_used, USED0 + STEPS * TOPK)
        for t in range(TILES):
            for half in range(HALVES):
                xx = x_tok[:, t, 512 * half:512 * half + 512]
                own(dve.tensor_tensor(xx, xx, psum[:, 2 * t + half, :], ALU.add))
        for t in range(TILES):
            own(dve.tensor_tensor_reduce(work[:, t, :], x_tok[:, t, :], x_tok[:, t, :], 1.0, 0.0, ALU.mult, ALU.add, stat[:, t:t + 1]))
        tell(dve.tensor_scalar(stat, stat, 1.0 / D, EPS, ALU.mult, ALU.add), square_ready, n_square)
        dve.wait_ge(root_ready, n_square[0])
        own(dve.reciprocal(rstd, rstd))
        row = wait_row(dve, n_row[0])
        n_row[0] += 1
        for t in range(TILES):
            tell(dve.scalar_tensor_tensor(x_tok[:, t, :], x_tok[:, t, :], rstd[:, t:t + 1], row, ALU.mult, ALU.mult), normed, n_normed, True)
        dve.sem_inc(row_used, 1)
        for layer in range(2):
            if layer == 1:
                own(dve.memset(kz, 0.0))
                dve.sem_inc(zeros_ready, 1)
                memory_keys(layer)
            if layer == 0:
                for c in range(SH // 2 + SKV):
                    if c < SH // 2:
                        rope(("rope2", c), q2[:, c, :], ("in2", 0, c))
                    else:
                        j = 2 * (c - SH // 2)
                        rope(("rope2", c), k_raw[:, c % 2, :], ("in2", 0, c), (kz[:, j, :], kz[:, j + 1, :]))
            else:
                bank = wait_product(dve, ("forget",))
                z = f_log[0:SH, :]
                t = f_tmp[0:SH, :]
                give(dve.tensor_scalar(z, bank[0:SH, 0:S], col("b_forget")[0:SH], None, ALU.add), ("forget",), True)
                own(dve.tensor_scalar(t, z, -1.0, None, ALU.mult))
                dve.tensor_tensor(t, t, z, ALU.min).then_inc(forget_exp, 1)
                dve.wait_ge(forget_e, 1)
                own(dve.tensor_scalar(z, z, 0.0, None, ALU.min))
                own(dve.tensor_tensor(z, z, t, ALU.subtract))
                own(dve.memset(t, 1.0))
                own(dve.tensor_tensor_scan(f_cum[0:SH, :], t, z, 0.0, ALU.mult, ALU.add))
                dve.tensor_scalar(f_cum[0:SH, :], f_cum[0:SH, :], -1.0 / SCALE2, None, ALU.mult).then_inc(cum_ready, 1)

            def out(kind, h):
                c = h // 2 if kind != "mem2" else SH // 2 + h // 2
                return h % 2 * HD2, h % 2 * HD2 + HD2, actT[:, c, :]

            attention(pl.att2[layer], SH + MH2, out)
            for t in range(TILES):
                for h in range(HALVES):
                    bank = wait_product(dve, ("out2", layer, t, h))
                    xx = x_tok[:, t, 512 * h:512 * h + 512]
                    give(dve.scalar_tensor_tensor(xx, xx, ALPHA, bank, ALU.mult, ALU.add), ("out2", layer, t, h), True)
            layer_norm()
            if layer == 0:
                for f in range(FC):
                    dve.wait_ge(silu_ready, f + 1)
                    bank = psum[:, pl.bank[("ff", f)], :]
                    give(dve.tensor_tensor(ffT[:, f, :], silu_ff[:, f % 2, :], bank[:, S:2 * S], ALU.mult), ("ff", f), True)
                    dve.sem_inc(ff_ready, 1)
                for t in range(TILES):
                    for h in range(HALVES):
                        bank = wait_product(dve, ("down", t, h))
                        xx = x_tok[:, t, 512 * h:512 * h + 512]
                        give(dve.scalar_tensor_tensor(xx, xx, ALPHA, bank, ALU.mult, ALU.add), ("down", t, h), True)
                layer_norm()
        own(dve.memset(ones, 1.0))
        own(dve.tensor_scalar(before, C("causal")[:, 0:P], -1.0, None, ALU.is_lt))
        for t in range(TILES):
            bank = wait_product(dve, ("router", t))
            give(dve.tensor_tensor(logits[:, t, :], bank[:, 0:NE], col("b_router", 0, NE), ALU.add), ("router", t), True)
            own(dve.max(r_top[:, t, :], logits[:, t, :]))
            own(dve.max_index(r_idx[:, t, :], r_top[:, t, :], logits[:, t, :]))
        own(dve.tensor_copy(r_idxf, r_idx))
        own(dve.tensor_tensor(r_e, r_top[:, :, 1], r_top[:, :, 0], ALU.subtract))
        dve.sem_inc(router_exp, 1)
        dve.wait_ge(router_e, 1)
        own(dve.tensor_scalar(r_den, r_e, 1.0, None, ALU.add))
        own(dve.reciprocal(r_g[:, :, 0], r_den))
        own(dve.tensor_tensor(r_g[:, :, 1], r_g[:, :, 0], r_e, ALU.mult))
        for t in range(TILES):
            own(dve.tensor_scalar(r_mask[:, t, :], C("iota")[:, 0:NE], r_idxf[:, t, 0:1], None, ALU.is_equal))
            own(dve.tensor_scalar(r_gate[:, t, :], r_mask[:, t, :], r_g[:, t, 0:1], None, ALU.mult))
            own(dve.tensor_scalar(r_hot[:, t, :], C("iota")[:, 0:NE], r_idxf[:, t, 1:2], None, ALU.is_equal))
            own(dve.tensor_tensor(r_mask[:, t, :], r_mask[:, t, :], r_hot[:, t, :], ALU.add))
            own(dve.scalar_tensor_tensor(r_gate[:, t, :], r_hot[:, t, :], r_g[:, t, 1:2], r_gate[:, t, :], ALU.mult, ALU.add))
        dve.sem_inc(router_e, 1)
        bank = wait_product(dve, ("place",))
        places = bank[:, 0:TILES * NE].rearrange("p (t e) -> p t e", t=TILES)
        own(dve.tensor_scalar(r_slot, r_mask, -1.0e6, 1.0e6, ALU.mult, ALU.add))
        own(dve.tensor_tensor(r_slot, r_slot, places, ALU.add))
        give(dve.tensor_copy(count_i, bank[:, 2 * NE:3 * NE]), ("place",), True)
        for t in range(TILES):
            own(dve.tensor_scalar(work[:, t, :], x_tok[:, t, :], ALPHA, None, ALU.mult))
        dve.sem_inc(e_freed["vector"], e_n["vector"])
        dve.sem_inc(routed, 1)

        def wait_e(j, b):
            dve.wait_ge(e_product, b * N_EP + j + 1 + N_EP)
            return psum[:, E_BANK[j], :]

        def expert(e, b, over):
            dve.wait_ge(e_product, b * N_EP + N_EP)
            dve.tensor_copy(r_shift, r_slot[:, :, bass.ds(e, 1)].rearrange("p t e -> p (t e)")).then_inc(pick_step, 1)
            dve.wait_ge(pick_step, 3 * b + 1)
            if over:
                dve.tensor_scalar(r_shift, r_shift, float(-P), None, ALU.add).then_inc(pick_step, 1)
            else:
                dve.sem_inc(pick_step, 1)
            dve.wait_ge(pick_step, 3 * b + 2)
            dve.tensor_copy(r_den, r_gate[:, :, bass.ds(e, 1)].rearrange("p t e -> p (t e)")).then_inc(pick_step, 1)
            dve.wait_ge(pick_step, 3 * b + 3)
            for t in range(TILES):
                dve.tensor_scalar(pick[:, t, :], C("iota"), r_shift[:, t:t + 1], None, ALU.is_equal)
                ins = dve.tensor_scalar(pickg[:, t, :], C("iota"), r_shift[:, t:t + 1], r_den[:, t:t + 1], ALU.is_equal, ALU.mult)
            ins.then_inc(picked, 1)
            for n in range(FC // 2):
                dve.wait_ge(e_silu, b * (FC // 2) + n + 1)
                bank = psum[:, E_BANK[UP0 + n], :].rearrange("p (f g s) -> p f g s", f=2, g=2)
                dve.tensor_tensor(geT[:, 2 * n:2 * n + 2, :], silu_e[:, n % 2, :, :], bank[:, :, 1, :], ALU.mult)\
                   .then_inc(e_freed["vector"], 1)
            for t in range(TILES):
                for h in range(HALVES):
                    bank = wait_e(SUM0 + t * HALVES + h, b)
                    ww = work[:, t, 512 * h:512 * h + 512]
                    dve.tensor_tensor(ww, ww, bank, ALU.add).then_inc(e_freed["vector"], 1)

        def skip(b):
            dve.sem_inc(pick_step, 3)
            dve.wait_ge(picked, b)
            dve.sem_inc(picked, 1)
            dve.wait_ge(e_freed["vector"], b * e_n["vector"] + e_n["vector"])
            dve.sem_inc(e_freed["vector"], e_n["vector"])

        each_expert(dve, expert, skip)
        dve.wait_ge(e_freed["vector"], (2 * NE + 1) * e_n["vector"])
        for t in range(TILES):
            own(dve.tensor_copy(x_tok[:, t, :], work[:, t, :]))
        layer_norm()

    ctx.close()


def ff_loads(pl, a):
    w = a["w_ffn_in_2"][0].rearrange("(k p) n -> p k n", p=P)
    for u in range(FC // 2):
        pl.add_unit(("ff_in", u), [(half * KD * S, KD, S, w[:, :, half * FF + S * u:half * FF + S * (u + 1)]) for half in range(2)],
                    ("ff", 2 * u + 1))
    w = a["w_ffn_out_2"][0].rearrange("(k p) n -> p k n", p=P)
    for o, n in enumerate([3] * 6 + [4]):
        pl.add_unit(("ff_out", o), [(0, n, D, w[:, 3 * o:3 * o + n, :])],
                    ("ff_out_used", o) if o < 6 else ("down", TILES - 1, HALVES - 1))


PLAIN = ["x", "mem", "positions", "positions_2", "w_mem_kv", "w_in", "lru_wr", "lru_wi", "p_attn", "p_lru", "p_mem", "w_out",
         "w_peer_q", "peer_u", "peer_v", "w_mem_kv_2", "w_in_fox_2", "w_out_2", "w_ffn_in_2", "w_ffn_out_2", "w_exp_in_2",
         "w_exp_out_2", "g_mem", "g_mix", "g_ffn", "g_final", "ln_attn_g_2", "ln_attn_b_2", "ln_ffn_g_2", "ln_ffn_b_2"]


def layouts(v):
    def by_partition(x):
        return np.ascontiguousarray(x).reshape(-1, P).T

    def on_all(x):
        return np.broadcast_to(x.reshape(1, -1), (P, x.size))

    def chunks(x):
        return x.reshape(KD, P, -1).transpose(1, 0, 2).reshape(P, -1)

    f = v["w_in_fox_2"][0]
    b_forget = np.zeros((P, 1), np.float32)
    b_forget[:SH, 0] = v["b_forget_2"][0]
    parts = {"gate_b": by_partition(v["gate_b"][0]), "conv_w": by_partition(v["conv_w"][0]), "conv_b": by_partition(v["conv_b"][0]),
             "lru_br": by_partition(v["lru_br"][0]), "lru_bi": by_partition(v["lru_bi"][0]), "lam": by_partition(v["lru_lambda"][0]),
             "sink": on_all(v["attn_sink"][0]), "sink2": on_all(v["attn_sinks_2"][0]), "b_router": on_all(v["b_router_2"][0]),
             "b_forget": b_forget, "w_forget": chunks(f[:, -SH:]), "w_router": chunks(v["w_router_2"][0])}
    out = {name: v[name] for name in PLAIN}
    out["columns"] = np.concatenate([parts[name] for name in COLS], axis=1)
    out["constants"] = constants()
    out["sub_keys_T"] = v["peer_sub_keys"][0].reshape(2 * PH, PK, P).transpose(2, 0, 1)
    out["mem_2_T"] = v["mem_2"][0].T
    w = v["w_in_swa_2"][0]
    q, kv = SH * HD2, SKV * HD2
    twice = lambda x: np.repeat(x.reshape(D, SKV, 1, HD2), 2, axis=2).reshape(D, 2 * kv)
    out["w_swa"] = np.concatenate([w[:, :q], twice(w[:, q:q + kv]), twice(w[:, q + kv:q + 2 * kv]), w[:, q + 2 * kv:]], axis=1)
    return {name: np.ascontiguousarray(x) for name, x in out.items()}


def kernel(**inputs):
    import concourse.bacc as bacc
    from concourse.bass_utils import run_bass_kernel_spmd

    arrays = layouts({name: np.asarray(x) for name, x in inputs.items()})
    nc = bacc.Bacc("TRN2", target_bir_lowering=False, num_devices=1)
    a = {name: nc.dram_tensor("in_" + name, x.shape, mybir.dt.from_np(x.dtype), kind="ExternalInput").ap() for name, x in arrays.items()}
    a["out"] = nc.dram_tensor("out", (1, S, D), F32, kind="ExternalOutput").ap()
    two_blocks(nc, a)
    r = run_bass_kernel_spmd(nc, [{"in_" + name: x for name, x in arrays.items()}], core_ids=[0])
    return r.results[0]["out"]
```

```python
import math
from contextlib import ExitStack

import numpy as np

import concourse.bass as bass
from concourse import mybir

F32, I32, U32, R32 = mybir.dt.float32, mybir.dt.int32, mybir.dt.uint32, mybir.dt.float32r
ALU, ACT, AX = mybir.AluOpType, mybir.ActivationFunctionType, mybir.AxisListType

P = 128
S, D = 256, 1024
TILES, KD = S // P, D // P
HALVES = D // 512
EPS, LN_EPS = 1e-6, 1e-5
NEG = -1e30
THETA = 500000.0

AH, AKV, HD = 6, 2, 128
GROUP = AH // AKV
LW, LB = 768, 6
CONV = 4
MH = 4
PH, PK, TOPK = 8, 128, 16
PICKS = PH * TOPK
SH, SKV, MH2, HD2 = 12, 3, 4, 64
FF = 2816
FC = FF // P
NE = 8
ALPHA = 4.0 ** 0.25
SCALE2 = HD2 ** -0.5

C_Q, C_K, C_V, C_XL, C_GL, C_QM, C_G = 0, 6, 8, 10, 16, 22, 26
N_IN = 50

LAG = 3
RING, UNIT = 6, KD * 512
BANKS = 8
UV = 8

COLS = {}
_at = 0
for _name, _n in (("gate_b", 24), ("conv_w", CONV * LB), ("conv_b", LB), ("lru_br", 12), ("lru_bi", 12), ("lam", 12),
                  ("sink", AH), ("sink2", SH), ("b_router", NE), ("b_forget", 1), ("w_forget", KD * SH),
                  ("w_router", KD * NE)):
    COLS[_name] = (_at, _n)
    _at += _n
N_COLS = _at
CONST = {}
_at = 0
for _name, _n in (("ident", P), ("rot1", P), ("rot2", P), ("iota", P), ("freq1", 1), ("freq2", 1),
                  ("band", TILES * S), ("chunks", TILES * S), ("causal", TILES * S)):
    CONST[_name] = (_at, _n)
    _at += _n
N_CONST = _at


def constants():
    c = np.zeros((P, N_CONST), np.float32)

    def put(name, value):
        at, n = CONST[name]
        c[:, at:at + n] = np.asarray(value, np.float32).reshape(P, n)

    def rotation(head, rot):
        m = np.zeros((P, P), np.float32)
        for base in range(0, P, head):
            for o in range(rot // 2):
                m[base + o + rot // 2, base + o] = -1.0
                m[base + o, base + o + rot // 2] = 1.0
        return m

    def freqs(head, rot):
        f = np.float32(THETA) ** (-np.arange(0, rot, 2, dtype=np.float32) / np.float32(rot))
        out = np.zeros(P, np.float32)
        for base in range(0, P, head):
            out[base:base + rot // 2] = f
            out[base + rot // 2:base + rot] = f
        return out

    put("ident", np.eye(P))
    put("rot1", rotation(HD, HD // 4))
    put("rot2", rotation(HD2, HD2 // 4))
    put("iota", np.broadcast_to(np.arange(P), (P, P)))
    put("freq1", freqs(HD, HD // 4))
    put("freq2", freqs(HD2, HD2 // 4))
    q = np.arange(S).reshape(TILES, P).T[:, :, None]
    k = np.arange(S)[None, None, :]
    put("band", np.where(np.abs(q - k) <= 128, 0.0, NEG))
    put("chunks", np.where((k // 64 <= q // 64) & (k // 64 >= q // 64 - 2), 0.0, NEG))
    put("causal", np.where(k <= q, 0.0, NEG))
    return c


class Plan:

    def __init__(self):
        self.products, self.nth, self.bank, self.freed = [], {}, {}, {}
        self.count = {"vector": 0, "scalar": 0}
        self.units, self.unit = [], {}
        self.loaded = [0] * RING
        self.at = 0

    def product(self, name, by):
        self.bank[name] = len(self.products) % BANKS
        self.products.append(name)
        self.nth[name] = len(self.products)
        self.count[by] += 1
        self.freed[name] = (by, self.count[by])

    def add_unit(self, name, loads, last, slot=None):
        slot = self.at % RING if slot is None else slot
        self.loaded[slot] += 16 * len(loads)
        before = [u for u in self.units if u[1] == slot]
        self.units.append((name, slot, loads, last, before[-1][3] if before else None))
        self.unit[name] = (slot, self.loaded[slot])
        self.at += 1


def make_plan():
    pl = Plan()
    pr = pl.product
    heads = []

    def transposed(tag):
        for k in range(KD):
            pr((tag, k), "scalar")

    def attention(kinds):
        base = len(heads)
        heads.extend(kinds)
        n = len(kinds)
        for i in range(n + LAG):
            if i < n:
                pr(("S", base + i), "vector")
            if 2 <= i < n + 2:
                pr(("T", base + i - 2), "scalar")
            if i >= LAG:
                pr(("V", base + i - LAG), "vector")
        return base

    transposed("memT")
    for c in range(MH):
        pr(("km", c), "scalar")
    for t in range(TILES):
        pr(("vm", t), "scalar")
    transposed("hT")
    for c in range(C_V):
        pr(("in", c), "scalar")
        if c >= 1:
            pr(("rope", c - 1), "vector")
    for t in range(TILES):
        pr(("v", t), "scalar")
        if t == 0:
            pr(("rope", C_V - 1), "vector")
    for c in range(C_XL, N_IN):
        pr(("in", c), "scalar")
    pl.att1 = attention([("self1", h) for h in range(AH)] + [("mem1", h) for h in range(MH)])
    for d in range(2):
        for b in range(LB):
            pr(("lru", d, b), "scalar")
    for br in range(3):
        for c in range(KD):
            pr(("merge", br, c), "vector")
    for t in range(TILES):
        for h in range(HALVES):
            pr(("out1", t, h), "vector")
    transposed("h2T")
    for g in range(4):
        for c in range(4 * g, 4 * g + 4):
            pr(("pq", c), "scalar")
        for t in range(TILES):
            pr(("sc", t, g), "scalar")

    def memory2(layer):
        for c in range(2):
            pr(("km2", layer, c), "scalar")
        for t in range(TILES):
            pr(("vm2", layer, t), "scalar")

    memory2(0)
    transposed("x2T")
    pl.att2 = []
    for layer in range(2):
        if layer:
            memory2(layer)
        nk = SKV if layer == 0 else SH // 2
        for c in range(SH // 2 + nk):
            pr(("in2", layer, c), "scalar")
            if c >= 1:
                if layer == 0:
                    pr(("rope2", c - 1), "vector")
        if layer == 0:
            pr(("rope2", SH // 2 + nk - 1), "vector")
        for t in range(TILES):
            for h in range(1 + layer):
                pr(("v2", layer, t, h), "scalar")
        for c in range(2):
            pr(("qm2", layer, c), "scalar")
        if layer == 1:
            pr(("forget",), "vector")
        kind = ("swa", "fox")[layer]
        pl.att2.append(attention([(kind, h) for h in range(SH)] + [("mem2", h) for h in range(MH2)]))
        for t in range(TILES):
            for h in range(HALVES):
                pr(("out2", layer, t, h), "vector")
        transposed(("aT", layer))
        if layer == 0:
            for f in range(FC):
                pr(("ff", f), "vector")
            for t in range(TILES):
                for h in range(HALVES):
                    pr(("down", t, h), "vector")
            transposed("x3T")
        else:
            for t in range(TILES):
                pr(("router", t), "vector")
            pr(("place",), "vector")
    pl.heads = heads
    return pl


def two_blocks(nc, a):
    pl = make_plan()
    ctx = ExitStack()
    sem = lambda name: ctx.enter_context(nc.semaphore(name))
    placed = ExitStack()
    taken = []

    def sb(name, n, dt=F32):
        taken.append(n)
        return placed.enter_context(nc.sbuf_tensor(name, [P, n], dt))


    def cols_of(w, c0, n):
        return w.rearrange("(k p) n -> p k n", p=P)[:, :, c0:c0 + n]

    def rows_of(w, k0, nk):
        return w.rearrange("(k p) n -> p k n", p=P)[:, k0:k0 + nk, :]

    for u in range(2):
        pl.add_unit(("mem_kv", u), [(0, KD, 512, cols_of(a["w_mem_kv"][0], 512 * u, 512))],
                    [("km", MH - 1), ("vm", TILES - 1)][u])
    for u in range(13):
        n = min(512, N_IN * P - 512 * u)
        last = ("in", min(4 * u + 3, N_IN - 1)) if u != 2 else ("in", 11)
        pl.add_unit(("w_in", u), [(0, KD, n, cols_of(a["w_in"][0], 512 * u, n))], last)
    pl.add_unit("lru_w", [(0, 12, P, a["lru_wr"][0].rearrange("d h c e -> c (d h) e")),
                          (12 * P, 12, P, a["lru_wi"][0].rearrange("d h c e -> c (d h) e"))], ("lru", 1, LB - 1))
    for br, (name, nk) in enumerate((("p_attn", AH), ("p_lru", LB), ("p_mem", MH))):
        for u in range(2):
            pl.add_unit((name, u), [(0, nk, 512, cols_of(a[name][0], 512 * u, 512))], ("merge", br, 4 * u + 3))
    for u in range(HALVES):
        pl.add_unit(("w_out", u), [(0, KD, 512, cols_of(a["w_out"][0], 512 * u, 512))], ("out1", TILES - 1, u))
    pl.add_unit("sub_keys", [(0, 2 * PH, PK, a["sub_keys_T"])], ("sc", TILES - 1, 3))
    peer_q = lambda u: (("peer_q", u), [(0, KD, 512, cols_of(a["w_peer_q"][0], 512 * u, 512))], ("pq", 4 * u + 3))
    for u in range(3):
        pl.add_unit(*peer_q(u))
    place = lambda name: pl.unit[name][0]
    U_SLOTS = (place(("w_out", 0)), place(("w_out", 1)))
    V_SLOTS = (place(("peer_q", 1)), place(("peer_q", 2)))
    pl.add_unit(*peer_q(3), slot=place(("peer_q", 0)))
    pl.at += (place("sub_keys") - pl.at) % RING
    for layer in range(2):
        pl.add_unit(("mem_kv2", layer), [(0, KD, 512, cols_of(a["w_mem_kv_2"][layer], 0, 512))],
                    ("vm2", layer, TILES - 1))
        w = a["w_swa"] if layer == 0 else a["w_in_fox_2"][0]
        width = w.shape[1] // P * P
        for u in range(-(-width // 512)):
            n = min(512, width - 512 * u)
            if layer == 0:
                last = (("in2", 0, 3), ("in2", 0, 7), ("v2", 0, 1, 0), ("qm2", 0, 1))[u]
            else:
                last = (("in2", 1, 3), ("in2", 1, 7), ("in2", 1, 11), ("v2", 1, 1, 0), ("qm2", 1, 1))[u]
            pl.add_unit(("w_in2", layer, u), [(0, KD, n, cols_of(w, 512 * u, n))], last)
        for u in range(HALVES):
            pl.add_unit(("w_out2", layer, u), [(0, KD, 512, cols_of(a["w_out_2"][layer], 512 * u, 512))],
                        ("out2", layer, TILES - 1, u))
        if layer == 0:
            ff_loads(pl, a)
    pl.at += -pl.at % RING

    OUT_ROWS = [3] * 6 + [4]
    e_units = [2] * (FC // 2) + [1] * len(OUT_ROWS)
    N_EU = len(e_units)
    assert N_EU % RING == 0
    e_loaded, per_expert = [], [0] * RING
    for j, n in enumerate(e_units):
        per_expert[j % RING] += 16 * n
        e_loaded.append(per_expert[j % RING])
    N_UP, N_SUM = FC // 2, TILES * HALVES
    N_PIECE = HALVES * N_EU
    SUMS = [("sum", n) for n in range(N_SUM)]
    GATHERED = [("gather", h) for h in range(HALVES)]

    def piece_end(i):
        if i < 2 * N_UP:
            return ("up" if i % 2 else "up_half", i // 2)
        return ("part", i) if i < N_PIECE - HALVES else ("y", i - N_PIECE + HALVES)

    HIS = 4
    Y, E_SEQ = [], []
    for i in range(N_PIECE):
        Y.append(piece_end(i))
        n, more = i // 2, [("piece", i + HIS)] if i + HIS < N_PIECE else []
        turned = ("ge", n - 2) if i % 2 and 2 <= n < N_UP + 2 else None
        if i < 2 * N_UP and i % 2:
            E_SEQ += [("up", n), ("piece", i + HIS - 1)]
        if i >= 2 * N_UP or i % 2:
            E_SEQ += more
        if turned:
            Y.append(turned)
            E_SEQ.append(turned)
    E_ORDER = {False: Y + GATHERED + SUMS + [("pickT", 0)], True: GATHERED + [("pickT", 0)] + Y + SUMS}
    N_EP = len(E_ORDER[False])
    FIRST = [("piece", i) for i in range(HIS)]
    E_SPLITS = [j for j in E_SEQ if j[0] != "up"]
    E_SPLITS = {False: E_SPLITS + FIRST + GATHERED, True: GATHERED + FIRST + E_SPLITS}
    N_SPLIT = len(E_SPLITS[False])

    ring = sb("weight_ring", RING * UNIT)
    slot = lambda s: ring[:, s * UNIT:(s + 1) * UNIT]
    const = sb("constants", N_CONST)
    cols = sb("columns", N_COLS)
    C = lambda name: const[:, CONST[name][0]:sum(CONST[name])]
    col = lambda name, i=0, n=1: cols[:, COLS[name][0] + i:COLS[name][0] + i + n]
    ident = C("ident")
    tok = lambda ap: ap.rearrange("p (t n) -> p t n", t=TILES)
    x_tok = tok(sb("x_tok", TILES * D)[:, :])
    actT_flat = sb("actT", KD * S)
    actT = actT_flat[:, :].rearrange("p (k s) -> p k s", k=KD)
    work_flat = sb("work_tok", TILES * D)
    work = tok(work_flat[:, :])
    rows = sb("rows", 2 * D)[:, :].rearrange("p (r n) -> p r n", r=2)
    small = sb("small", 96)
    n_small = [0]

    def cell(n):
        n_small[0] += n
        assert n_small[0] <= 96
        return small[:, n_small[0] - n:n_small[0]]

    REGION = 17920
    region = sb("region", REGION)
    top = [0]

    def area(n, inner=None, dt=None):
        v = region[:, top[0]:top[0] + n]
        top[0] += n
        assert top[0] <= REGION, top[0]
        if dt is not None:
            v = v.bitcast(dt)
        return v if inner is None else v.rearrange("p (a b) -> p a b", b=inner)

    def attention_scratch():
        return [area(512, S) for _ in range(2)], [area(512, S) for _ in range(2)], [area(512, S) for _ in range(2)]

    s_buf, p_buf, pt_buf = attention_scratch()
    lru_ri = region[:, 0:12 * S].rearrange("p (b g s) -> p b g s", b=LB, g=2)
    lru_a = actT_flat[:, 0:LB * S].rearrange("p (b s) -> p b s", b=LB)
    xc = work_flat[:, 0:LB * S].rearrange("p (b s) -> p b s", b=LB)
    qa, ka, va = area(AH * S, S), area(AKV * S, S), area(TILES * AKV * HD, AKV * HD)
    xl, gl = area(LB * S, S), area(LB * S, S)
    qm, km, vm = area(MH * S, S), area(MH * S, S), area(TILES * MH * HD, MH * HD)
    gates = area(24 * S, S)
    rope_cos, rope_sin = region[:, 0:S], region[:, S:2 * S]
    ang, turns, rope_t = region[:, 2 * S:3 * S], region[:, 3 * S:4 * S], region[:, 4 * S:6 * S].rearrange("p (b s) -> p b s", b=2)
    pos_i = region[:, 6 * S:7 * S].bitcast(I32)

    top[0] = 7 * S
    pq = area(2 * PH * S, S)
    sc = area(TILES * 2 * PH * PK).rearrange("p (t c k) -> p t c k", t=TILES, k=PK)
    diag = area(TOPK * P, P)
    idx_u, idx_v, gate_st, u_dot, u_act, pick_w = (area(TILES * TOPK, TOPK, dt) for dt in (I32, I32, None, None, None, None))
    find, find_less = area(2 * PK, PK), area(2 * PK, PK)
    top_v, top_u, top_f = area(2 * TOPK, TOPK), area(2 * TOPK, TOPK, U32), area(2 * TOPK, TOPK)
    cand, cand_less = area(TOPK * TOPK), area(TOPK * TOPK)
    best, best_u, best_z, best_e = area(TOPK), area(TOPK, None, U32), area(TOPK), area(TOPK)
    place_u, place_f, key_f, idx_f = area(2 * TOPK, TOPK, U32), area(2 * TOPK, TOPK), area(2 * TOPK, TOPK), area(TOPK)
    hot = area(2 * TOPK * TOPK).rearrange("p (x k c) -> p x k c", x=2, c=TOPK)
    peer_top = top[0]
    assert UV * D == 2 * UNIT and U_SLOTS[1] == U_SLOTS[0] + 1 and V_SLOTS[1] == V_SLOTS[0] + 1
    rows_of_slots = lambda ss: ring[:, ss[0] * UNIT:(ss[1] + 1) * UNIT].rearrange("p (r n) -> p r n", n=D)
    u_ring, v_ring = rows_of_slots(U_SLOTS), rows_of_slots(V_SLOTS)

    top[0] = 0
    attention_scratch()
    mem2T = region[:, REGION - KD * S:REGION].rearrange("p (k s) -> p k s", k=KD)
    q2, qm2 = area(SH // 2 * S, S), area(2 * S, S)
    kz = area(SH * S, S)
    assert top[0] <= 7 * S + 4 * PH * S
    v2 = area(TILES * SH * HD2, SH * HD2)
    k_raw = area(2 * S, S)
    f_log, f_cum, f_tmp = area(S), area(S), area(S)
    top[0] = max(top[0], peer_top)
    kmz, vm2 = area(MH2 * S, S), area(TILES * MH2 * HD2, MH2 * HD2)
    ffT = region[:, 0:FC * S].rearrange("p (f s) -> p f s", f=FC)
    silu_ff = region[:, FC * S:(FC + 2) * S].rearrange("p (b s) -> p b s", b=2)
    assert (FC + 2) * S <= top[0] <= REGION - KD * S
    N_HI = HIS * UNIT // 2
    top[0] = N_HI + 2 * FC * P
    pick = area(TILES * P, P)
    pickg = area(TILES * P, P)
    pickT = area(TILES * P, P)
    silu_e, gated = area(2 * S, S), area(2 * S, S)
    ye = area(D)
    logits, r_mask, r_hot = (area(TILES * NE, NE) for _ in range(3))
    r_gate, r_slot = (area(TILES * (NE + 1), NE + 1) for _ in range(2))
    r_top, r_idx, r_idxf = area(TILES * 8, 8), area(TILES * 8, 8, U32), area(TILES * 8, 8)
    r_e, r_den, r_g = area(TILES), area(TILES), area(TILES * 2, 2)
    r_shift = area(2)
    count_i = area(NE, None, I32)
    ones, before = area(P), area(P)

    stat, rstd = cell(2), cell(2)
    bn, mv = cell(TILES * 12), cell(TILES * 2)
    nmax, esum, esink, den = cell(4), cell(4), cell(4), cell(4)
    sp_e, sp_z, sp_p = cell(12), cell(12), cell(12)
    placed.close()
    again = lambda name, n, dt: ctx.enter_context(nc.sbuf_tensor(name, [P, n], dt))
    assert taken[0] == RING * UNIT and taken[-1] == REGION
    slots_low = [again(f"weights_low{i}", UNIT, R32) for i in range(RING)]
    for i, n in enumerate(taken[1:-1]):
        if i == 3:
            assert n == 2 * KD * P
            xe_hi, xe_low = (again(name, KD * P, R32)[:, :].rearrange("p (k s) -> p k s", k=KD) for name in ("tokens_hi", "tokens_low"))
        else:
            again(f"kept{i}", n, F32)
    piece_hi = again("piece_hi", N_HI, R32)[:, :].rearrange("p (i n) -> p i n", i=HIS)
    ge_hi, ge_low = (again(name, FC * P, R32)[:, :].rearrange("p (f s) -> p f s", f=FC) for name in ("gated_hi", "gated_low"))
    again("region_rest", REGION - N_HI - 2 * FC * P, F32)
    psum = ctx.enter_context(nc.psum_tensor("psum", [P, BANKS, 512], F32))

    weight_in = [sem(f"weight_in{s}") for s in range(RING)]
    product_ready = sem("product_ready")
    freed = {"vector": sem("freed_by_vector"), "scalar": sem("freed_by_scalar")}
    x_in, const_in, mem_in, pos_in, mem2_in = (sem(n) for n in ("x_in", "const_in", "mem_in", "pos_in", "mem2_in"))
    row_in = [sem("row_in0"), sem("row_in1")]
    row_used = sem("row_used")
    vector_step, scalar_step, pool_step = sem("vector_step"), sem("scalar_step"), sem("pool_step")
    square_ready, root_ready, normed = sem("square_ready"), sem("root_ready"), sem("normed")
    angle_ready, table_ready, rope_ready = sem("angle_ready"), sem("table_ready"), sem("rope_ready")
    max_ready, exp_ready, probs_ready = sem("max_ready"), sem("exp_ready"), sem("probs_ready")
    sums_ready = sem("sums_ready")
    lam_exp, lam_ready, conv_ready = sem("lam_exp"), sem("lam_ready"), sem("conv_ready")
    lru_at, lru_sq_in, lru_sq_out, lru_done = sem("lru_at"), sem("lru_sq_in"), sem("lru_sq_out"), sem("lru_done")
    merged = sem("merged")
    best_ready, best_exp = sem("best_ready"), sem("best_exp")
    search_step, search_done, v_index, gathers = sem("search_step"), sem("search_done"), sem("v_index"), sem("gathers")
    u_in, v_in = [sem(f"u_in{k}") for k in range(UV)], [sem(f"v_in{k}") for k in range(UV)]
    dots_done, gelu_done, weights_done, diag_done = (sem(n) for n in ("dots_done", "gelu_done", "pick_weights_done", "diag_done"))
    v_used = sem("v_used")
    zeros_ready, forget_exp, forget_e, cum_ready = (sem(n) for n in ("zeros_ready", "forget_exp", "forget_e", "cum_ready"))
    silu_ready, ff_ready, ff_out_used = sem("silu_ready"), sem("ff_ready"), sem("ff_out_used")
    router_exp, router_e, routed, picked = (sem(n) for n in ("router_exp", "router_e", "routed", "picked"))
    e_product = sem("expert_product")
    e_freed = {"vector": sem("expert_freed_by_vector"), "scalar": sem("expert_freed_by_scalar")}
    e_hi, e_low = sem("expert_hi"), sem("expert_low")
    e_silu, pick_step = sem("expert_silu"), sem("pick_step")
    out_done = sem("out_done")

    rows_order = ["g_mem", "g_mix", "g_ffn", "g_final"]
    for layer in range(2):
        for part in ("attn", "ffn"):
            rows_order += [("ln_" + part + "_g_2", layer), ("ln_" + part + "_b_2", layer)]

    heads = pl.heads
    N1 = len([h for h in heads if h[0] in ("self1", "mem1")])

    def wait_product(eng, name):
        eng.wait_ge(product_ready, pl.nth[name])
        return psum[:, pl.bank[name], :]

    def wait_freed(eng, name):
        by, n = pl.freed[name]
        eng.wait_ge(freed[by], n)

    def wait_row(eng, i):
        eng.wait_ge(row_in[i % 2], 16 * (i // 2 + 1))
        return rows[:, i % 2, :]

    class Own:

        def __init__(self, eng, s):
            self.eng, self.s, self.n = eng, s, 0

        def __call__(self, ins):
            self.n += 1
            ins.then_inc(self.s, 1)
            self.eng.wait_ge(self.s, self.n)

    STEPS = PH * TILES
    DOTS0, USED0 = UV, TOPK + 1

    def peer_steps(eng, step, apart):
        step((0, 0), None, (1, 1))
        step((1, 1), (0, 0), (2, 0))
        step((2, 0), (1, 1), (3, 1))
        apart()
        with eng.Fori(1, PH - 1) as h:
            step((h * TILES + 1, 1), (h * TILES, 0), (h * TILES + 2, 0))
            step((h * TILES + 2, 0), (h * TILES + 1, 1), (h * TILES + 3, 1))
        step((STEPS - 1, 1), (STEPS - 2, 0), None)
        step(None, (STEPS - 1, 1), None)

    at_step = lambda now, s: now is not None and isinstance(now[0], int) and now[0] == s
    peer_bank = lambda t, half: (pl.nth["vm2", 0, TILES - 1] + HALVES * t + half) % BANKS

    E_BANK = {("pickT", 0): 6}
    for n in range(N_UP):
        E_BANK["up", n] = n % 4
        E_BANK["ge", n] = 4 + n % 2
    for n in range(N_SUM):
        E_BANK["sum", n] = n
    for h in range(HALVES):
        E_BANK["gather", h], E_BANK["y", h] = 4 + h, 6 + h
    e_by = lambda j: "vector" if j[0] in ("up", "ge", "gather", "sum") else "scalar"
    e_at = lambda j, over: E_ORDER[over].index(j)
    e_read = {over: {by: [j for j in E_ORDER[over] if j in E_BANK and e_by(j) == by] for by in ("vector", "scalar")} for over in (False, True)}
    e_nth = lambda j, over: e_read[over][e_by(j)].index(j) + 1
    e_n = {by: len(js) for by, js in e_read[False].items()}

    def e_before(j, over):
        same = [i for i in E_ORDER[over] if E_BANK.get(i) == E_BANK[j]]
        at = same.index(j)
        return (same[at - 1], False) if at else (same[-1], True)

    def halves(i, words):
        j, h = divmod(i, 2)
        if j < N_UP:
            return words.rearrange("p (g m) -> p g m", g=2)[:, :, h * 4 * S:(h + 1) * 4 * S]
        n = OUT_ROWS[j - N_UP]
        return words[:, 0:n * D].rearrange("p (k n) -> p k n", n=D)[:, :, 512 * h:512 * h + 512]

    piece = lambda i: halves(i, slot(i // 2 % RING))
    low_of = lambda i: halves(i, slots_low[i // 2 % RING])

    def hi_of(i):
        if i < 2 * N_UP:
            return piece_hi[:, i % HIS, :].rearrange("p (g m) -> p g m", g=2)
        n = OUT_ROWS[i // 2 - N_UP]
        return piece_hi[:, i % HIS, 0:n * 512].rearrange("p (k n) -> p k n", n=512)

    def wait_split(eng, s, what, b, over):
        eng.wait_ge(s, b * N_SPLIT + N_SPLIT + E_SPLITS[over].index(what) + 1)

    def turn_before(what, b, over):
        return b - 1 if what in FIRST + GATHERED and not over else b

    def each_expert(eng, body, skip):
        with eng.Fori(0, NE - 1) as e:
            body(e, e, False)
        body(NE - 1, NE - 1, False)
        eng.wait_ge(routed, 1)
        with eng.Fori(0, NE) as e:
            n = eng.value_load(count_i[0:1, bass.ds(e, 1)], min_val=0, max_val=S)
            with eng.If(n > P):
                body(e, e + NE, True)
            with eng.Else():
                skip(e + NE)

    block = ctx.enter_context(nc.Block())

    @block.sync
    def _(sp):
        after = [u[0] for u in pl.units].index(("peer_q", 3)) + 1
        peer_slots = [next(n for n in range(after, len(pl.units)) if pl.units[n][1] == s) for s in U_SLOTS + V_SLOTS]
        sp.dma_start(work[:, :, :], a["mem"][0].rearrange("(t p) n -> p t n", p=P)).then_inc(mem_in, 16)
        sp.dma_start(const[:, :], a["constants"]).then_inc(const_in, 16)
        sp.dma_start(cols[:, :], a["columns"]).then_inc(const_in, 16)
        sp.dma_start(x_tok[:, :, :], a["x"][0].rearrange("(t p) n -> p t n", p=P)).then_inc(x_in, 16)
        for n, (name, s, loads, _, before) in enumerate(pl.units):
            if n in peer_slots:
                sp.wait_ge(*((dots_done, DOTS0 + STEPS * TOPK) if s in U_SLOTS else (v_used, USED0 + STEPS * TOPK)))
            elif before is not None:
                if before[0] == "ff_out_used":
                    sp.wait_ge(ff_out_used, before[1] + 1)
                else:
                    sp.wait_ge(product_ready, pl.nth[before])
            for at, nk, n, src in loads:
                sp.dma_start(slot(s)[:, at:at + nk * n].rearrange("p (k n) -> p k n", k=nk), src).then_inc(weight_in[s], 16)
        sp.wait_ge(product_ready, pl.nth["out2", 1, TILES - 1, HALVES - 1])

        def expert_loads(e, b, over):
            one = slice(e, e + 1) if isinstance(e, int) else bass.ds(e, 1)
            for j in range(N_EU):
                s = j % RING
                if j >= RING:
                    sp.wait_ge(e_product, b * N_EP + N_EP + last_use(j - RING, over) + 1)
                elif over:
                    sp.wait_ge(e_product, b * N_EP + N_EP)
                else:
                    sp.wait_ge(e_product, b * N_EP + last_use(j - RING + N_EU, over) + 1)
                if j < FC // 2:
                    w = a["w_exp_in_2"][0][one, :, :].rearrange("e (k p) n -> p (e k) n", p=P)
                    for half in range(2):
                        sp.dma_start(slot(s)[:, half * 8 * S:(half + 1) * 8 * S].rearrange("p (k n) -> p k n", k=KD),
                                     w[:, :, half * FF + S * j:half * FF + S * (j + 1)]).then_inc(weight_in[s], 16)
                else:
                    o = j - FC // 2
                    w = a["w_exp_out_2"][0][one, :, :].rearrange("e (k p) n -> p (e k) n", p=P)
                    sp.dma_start(slot(s)[:, 0:OUT_ROWS[o] * D].rearrange("p (k n) -> p k n", n=D),
                                 w[:, 3 * o:3 * o + OUT_ROWS[o], :]).then_inc(weight_in[s], 16)

        def last_use(j, over):
            return e_at(piece_end(2 * j + 1), over)

        def skip(b):
            for s in range(RING):
                sp.wait_ge(weight_in[s], b * per_expert[s] + pl.loaded[s])
                sp.sem_inc(weight_in[s], per_expert[s])

        each_expert(sp, expert_loads, skip)
        sp.wait_ge(normed, 8 * TILES)
        sp.dma_start(a["out"].rearrange("b (t p) n -> p (b t) n", p=P), x_tok[:, :, :]).then_inc(out_done, 16)
        sp.wait_ge(out_done, 16)

    @block.gpsimd
    def _(pool):
        own = Own(pool, pool_step)
        pool.dma_start(pos_i, a["positions"][0].partition_broadcast(P)).then_inc(pos_in, 16)

        def load_row(i):
            if i >= 2:
                pool.wait_ge(row_used, i - 1)
            name = rows_order[i]
            src = a[name[0]][name[1]] if isinstance(name, tuple) else (a[name] if name == "g_final" else a[name][0])
            pool.dma_start(rows[:, i % 2, :], src.partition_broadcast(P)).then_inc(row_in[i % 2], 16)

        for i in range(4):
            load_row(i)
        pool.wait_ge(product_ready, pl.nth[("out1", TILES - 1, HALVES - 1)])
        pool.dma_start(mem2T[:, :, :], a["mem_2_T"].rearrange("(k p) s -> p k s", p=P)).then_inc(mem2_in, 16)
        pool.dma_start(pos_i, a["positions_2"][0].partition_broadcast(P)).then_inc(pos_in, 16)

        def gather_u(s, t, k):
            if k == 0:
                pool.wait_ge(search_done, s + 1)
            pool.wait_ge(dots_done, s * TOPK + k + 1)
            pool.sem_inc(gathers, 1)
            pool.indirect_dma_start(u_ring[:, k % UV, :], None, a["peer_u"][0],
                                    bass.IndirectOffsetOnAxis(idx_u[:, t, k:k + 1], 0)).then_inc(u_in[k % UV], 16)

        def gather_v(s, t, k):
            if k == 0:
                pool.wait_ge(v_index, s + 1)
            pool.wait_ge(v_used, USED0 + s * TOPK + k - UV + 1)
            pool.sem_inc(gathers, 1)
            pool.indirect_dma_start(v_ring[:, k % UV, :], None, a["peer_v"][0],
                                    bass.IndirectOffsetOnAxis(idx_v[:, t, k:k + 1], 0)).then_inc(v_in[k % UV], 16)

        AHEAD = 4

        def gathers_of_step(dots, total, search):
            if at_step(total, 0):
                pool.wait_ge(product_ready, pl.nth["pq", 11])
            for k in range(-AHEAD, TOPK):
                if dots is not None and k + AHEAD < TOPK:
                    gather_u(*dots, k + AHEAD)
                if total is not None and k >= 0:
                    gather_v(*total, k)

        peer_steps(pool, gathers_of_step, lambda: None)
        for i in range(4, len(rows_order)):
            load_row(i)

    @block.scalar
    def _(act):
        own = Own(act, scalar_step)

        def give(ins, name):
            ins.then_inc(freed["scalar"], 1)
            assert pl.freed[name] == ("scalar", give.n + 1), name
            give.n += 1

        give.n = 0

        def copy_out(name, dst, func=ACT.Copy, n=None, **kw):
            src = wait_product(act, name)
            n = n or dst.free_size()
            src = src[:, 0:n]
            if len(dst.shape) == 3:
                src = src.rearrange("p (a b) -> p a b", b=dst.shape[2])
            give(act.activation(dst, src, func, **kw), name)

        n_root = [0]

        def root():
            n_root[0] += 1
            act.wait_ge(square_ready, n_root[0])
            act.activation(rstd, stat, ACT.Sqrt).then_inc(root_ready, 1)

        def transposed(tag):
            for k in range(KD):
                copy_out((tag, k), actT[:, k, :])

        def rope_tables(i):
            act.wait_ge(angle_ready, 2 * i + 1)
            act.activation(rope_sin, ang, ACT.Sin).then_inc(table_ready, 1)
            act.wait_ge(angle_ready, 2 * i + 2)
            act.activation(rope_cos, turns, ACT.Sin).then_inc(table_ready, 1)

        def attention(base, n):
            for i in range(n + 2):
                if i >= 2:
                    g = base + i - 2
                    copy_out(("T", g), pt_buf[g % 2])
                if 1 <= i <= n:
                    g = base + i - 1
                    b = g % 2
                    act.wait_ge(sums_ready, g + 1)
                    for t in range(TILES):
                        ins = act.activation(p_buf[b][:, t, :], p_buf[b][:, t, :], ACT.Copy, scale=den[:, 2 * b + t:2 * b + t + 1])
                    ins.then_inc(probs_ready, 1)
                if i < n:
                    g = base + i
                    b = g % 2
                    kind, h = heads[g]
                    act.wait_ge(max_ready, g + 1)
                    for t in range(TILES):
                        ins = act.activation(p_buf[b][:, t, :], s_buf[b][:, t, :], ACT.Exp, bias=nmax[:, 2 * b + t:2 * b + t + 1],
                                             accum_out=esum[:, 2 * b + t:2 * b + t + 1])
                    if kind in ("self1", "swa"):
                        sink = col("sink" if kind == "self1" else "sink2", h)
                        ins = act.activation(esink[:, 2 * b:2 * b + 2], nmax[:, 2 * b:2 * b + 2], ACT.Exp, bias=sink)
                    ins.then_inc(exp_ready, 1)

        root()
        transposed("memT")
        act.wait_ge(const_in, 32)
        for c in range(MH):
            copy_out(("km", c), km[:, c, :])
        for t in range(TILES):
            copy_out(("vm", t), vm[:, t, :])
        root()
        transposed("hT")
        rope_tables(0)
        for c in range(C_V):
            copy_out(("in", c), qa[:, c, :] if c < C_K else ka[:, c - C_K, :])
        for t in range(TILES):
            copy_out(("v", t), va[:, t, :])
        for c in range(C_XL, C_GL):
            copy_out(("in", c), xl[:, c - C_XL, :])
        for c in range(C_GL, C_QM):
            copy_out(("in", c), gl[:, c - C_GL, :], ACT.Gelu_apprx_tanh)
        for c in range(C_QM, C_G):
            copy_out(("in", c), qm[:, c - C_QM, :])
        for c in range(C_G, N_IN):
            copy_out(("in", c), gates[:, c - C_G, :], ACT.Sigmoid, bias=col("gate_b", c - C_G))
        attention(0, N1)
        act.wait_ge(lam_exp, 1)
        act.activation(sp_e, sp_z, ACT.Exp).then_inc(lam_exp, 1)
        act.wait_ge(lam_ready, 1)
        for d in range(2):
            if d:
                act.wait_ge(lru_done, 1)
            for b in range(LB):
                bank = wait_product(act, ("lru", d, b))
                act.activation(lru_ri[:, b, 0, :], bank[:, 0:S], ACT.Sigmoid, bias=col("lru_br", d * LB + b))
                give(act.activation(lru_ri[:, b, 1, :], bank[:, S:2 * S], ACT.Sigmoid, bias=col("lru_bi", d * LB + b)),
                     ("lru", d, b))
            act.wait_ge(freed["scalar"], pl.freed[("lru", d, LB - 1)][1])
            for b in range(LB):
                own(act.activation(lru_a[:, b, :], lru_ri[:, b, 0, :], ACT.Exp, scale=sp_e[:, d * LB + b:d * LB + b + 1]))
                act.activation(lru_ri[:, b, 0, :], lru_ri[:, b, 0, :], ACT.Tanh,
                               scale=sp_p[:, d * LB + b:d * LB + b + 1]).then_inc(lru_at, 1)
            for b in range(LB):
                act.wait_ge(lru_sq_in, d * LB + b + 1)
                act.activation(lru_ri[:, b, 0, :], lru_ri[:, b, 0, :], ACT.Sqrt).then_inc(lru_sq_out, 1)
        root()
        transposed("h2T")
        def queries(c0, c1):
            for c in range(c0, c1):
                copy_out(("pq", c), pq[:, c, :])

        def scores(g):
            for t in range(TILES):
                copy_out(("sc", t, g), sc[:, t, 4 * g:4 * g + 4, :])

        def memory2(layer):
            for c in range(2):
                bank = wait_product(act, ("km2", layer, c))
                act.activation(kmz[0:HD2, 2 * c, :], bank[0:HD2, 0:S], ACT.Copy)
                give(act.activation(kmz[HD2:P, 2 * c + 1, :], bank[HD2:P, 0:S], ACT.Copy), ("km2", layer, c))
            for t in range(TILES):
                copy_out(("vm2", layer, t), vm2[:, t, :])

        def best_exps(s):
            act.wait_ge(best_ready, s + 1)
            act.activation(best_e, best_z, ACT.Exp, accum_out=esum[:, 0:1]).then_inc(best_exp, 1)

        def diagonals(s, t):
            act.wait_ge(weights_done, s + 1)
            for k in range(TOPK):
                act.wait_ge(v_used, USED0 + (s - 1) * TOPK + k + 1)
                act.activation(diag[:, k, :], ident, ACT.Copy, scale=pick_w[:, t, k:k + 1]).then_inc(diag_done, 1)

        def gelu(s, t):
            act.wait_ge(dots_done, DOTS0 + s * TOPK + TOPK)
            act.activation(u_act[:, t, :], u_dot[:, t, :], ACT.Gelu_apprx_tanh).then_inc(gelu_done, 1)

        def peer_step(dots, total, search):
            if at_step(dots, 0):
                queries(0, 4)
                scores(0)
                queries(4, 5)
                best_exps(0)
                queries(5, 7)
                best_exps(1)
                queries(7, 8)
                scores(1)
                queries(8, 12)
                scores(2)
                queries(12, 14)
                gelu(0, 0)
                return
            if total is not None:
                diagonals(*total)
            if at_step(dots, 1):
                queries(14, 16)
            if search is not None:
                best_exps(search[0])
            if at_step(dots, 1):
                scores(3)
            if dots is not None:
                gelu(*dots)

        act.wait_ge(zeros_ready, 1)
        peer_steps(act, peer_step, lambda: memory2(0))
        rope_tables(1)
        root()
        transposed("x2T")
        for layer in range(2):
            if layer:
                memory2(layer)
            nk = SKV if layer == 0 else SH // 2
            for c in range(SH // 2 + nk):
                name = ("in2", layer, c)
                if c < SH // 2:
                    copy_out(name, q2[:, c, :])
                elif layer == 0:
                    if c >= SH // 2 + 2:
                        act.wait_ge(rope_ready, C_V + c - 1)
                    copy_out(name, k_raw[:, c % 2, :])
                else:
                    bank = wait_product(act, name)
                    j = 2 * (c - SH // 2)
                    act.wait_ge(zeros_ready, 3)
                    act.activation(kz[0:HD2, j, :], bank[0:HD2, 0:S], ACT.Copy)
                    give(act.activation(kz[HD2:P, j + 1, :], bank[HD2:P, 0:S], ACT.Copy), name)
            for t in range(TILES):
                if layer == 0:
                    copy_out(("v2", 0, t, 0), v2[:, t, 0:2 * SKV * HD2])
                else:
                    copy_out(("v2", 1, t, 0), v2[:, t, 0:512])
                    copy_out(("v2", 1, t, 1), v2[:, t, 512:SH * HD2])
            for c in range(2):
                copy_out(("qm2", layer, c), qm2[:, c, :])
            if layer == 1:
                act.wait_ge(forget_exp, 1)
                own(act.activation(f_tmp[0:SH, :], f_tmp[0:SH, :], ACT.Exp))
                act.activation(f_tmp[0:SH, :], f_tmp[0:SH, :], ACT.Ln, bias=1.0).then_inc(forget_e, 1)
            attention(pl.att2[layer], SH + MH2)
            root()
            transposed(("aT", layer))
            if layer == 0:
                for f in range(FC):
                    bank = wait_product(act, ("ff", f))
                    if f >= 2:
                        act.wait_ge(ff_ready, f - 1)
                    act.activation(silu_ff[:, f % 2, :], bank[:, 0:S], ACT.Silu).then_inc(silu_ready, 1)
                root()
                transposed("x3T")
        act.wait_ge(router_exp, 1)
        act.activation(r_e, r_e, ACT.Exp).then_inc(router_e, 1)
        act.wait_ge(routed, 1)

        def wait_e(j, b, over):
            act.wait_ge(e_product, b * N_EP + e_at(j, over) + 1 + N_EP)
            return psum[:, E_BANK[j], :]

        def split(what, b, over):
            kind, n = what
            if kind == "gather":
                src, dst = wait_e(what, b, over).rearrange("p (k s) -> p k s", k=4), xe_hi[:, 4 * n:4 * n + 4, :]
            elif kind == "ge":
                src, dst = wait_e(what, b, over)[:, 0:S].rearrange("p (f s) -> p f s", f=2), ge_hi[:, 2 * n:2 * n + 2, :]
            else:
                src, dst = piece(n), hi_of(n)
                if n % 2 == 0:
                    u = n // 2
                    turn = b if over or n >= HIS else b + 1
                    act.wait_ge(weight_in[u % RING], turn * per_expert[u % RING] + pl.loaded[u % RING] + e_loaded[u])
                if n >= HIS or not over:
                    act.wait_ge(e_product, b * N_EP + N_EP + e_at(piece_end((n - HIS) % N_PIECE), over) + 1)
            act.activation(dst, src, ACT.Copy).then_inc(e_hi, 1)

        def turned_selection(b, over):
            bank = wait_e(("pickT", 0), b, over)[:, 0:TILES * P]
            act.activation(pickT[:, :, :], bank.rearrange("p (t s) -> p t s", t=TILES), ACT.Copy).then_inc(e_freed["scalar"], 1)

        def expert(e, b, over):
            if over:
                for j in GATHERED:
                    split(j, b, over)
                turned_selection(b, over)
                for j in FIRST:
                    split(j, b, over)
            for j in E_SEQ:
                if j[0] != "up":
                    split(j, b, over)
                    continue
                n = j[1]
                bank = wait_e(j, b, over)
                act.wait_ge(e_freed["vector"], b * e_n["vector"] + (e_n["vector"] + e_nth(("up", n - 2), over) if n >= 2
                            else e_nth(("up", N_UP - 2 + (n + N_UP) % 2), over)))
                act.activation(silu_e[:, n % 2, :], bank[:, 0:S], ACT.Silu).then_inc(e_silu, 1)
            y_out = lambda h: act.activation(ye[:, 512 * h:512 * h + 512], wait_e(("y", h), b, over), ACT.Copy).then_inc(e_freed["scalar"], 1)
            if over:
                for h in range(HALVES):
                    y_out(h)
                return
            for i in range(HIS):
                if not isinstance(b, int):
                    split(("piece", i), b, over)
                if i >= HIS - HALVES:
                    y_out(i - HIS + HALVES)
            if isinstance(b, int):
                act.wait_ge(e_hi, b * N_SPLIT + N_SPLIT + E_SPLITS[over].index(FIRST[0]))
                act.sem_inc(e_hi, HIS)
            for j in GATHERED:
                split(j, b, over)
            turned_selection(b, over)

        def skip(b):
            act.wait_ge(e_freed["scalar"], b * e_n["scalar"] + e_n["scalar"])
            act.sem_inc(e_freed["scalar"], e_n["scalar"])
            act.wait_ge(e_silu, b * (FC // 2))
            act.sem_inc(e_silu, FC // 2)
            act.wait_ge(e_hi, b * N_SPLIT + N_SPLIT)
            act.sem_inc(e_hi, N_SPLIT)

        act.sem_inc(e_freed["scalar"], HALVES)
        act.sem_inc(e_hi, N_SPLIT - HIS - HALVES)
        for j in FIRST + GATHERED:
            split(j, -1, False)
        turned_selection(-1, False)
        each_expert(act, expert, skip)
        root()

    @block.tensor
    def _(pe):
        def begin(name):
            i = pl.nth[name] - 1
            if i >= BANKS:
                wait_freed(pe, pl.products[i - BANKS])
            return psum[:, pl.bank[name], :]

        def end(ins, name):
            assert pl.nth[name] == end.n + 1, name
            end.n += 1
            ins.then_inc(product_ready, 1)

        end.n = 0

        def unit(name, nk, n, at=0):
            s, count = pl.unit[name]
            pe.wait_ge(weight_in[s], count)
            return slot(s)[:, at:at + nk * n].rearrange("p (k n) -> p k n", k=nk)

        def transposes(tag, src, nth):
            pe.wait_ge(normed, 2 * nth)
            for k in range(KD):
                bank = begin((tag, k))
                for t in range(TILES):
                    ins = pe.transpose(bank[:, t * P:(t + 1) * P], src[:, t, k * P:(k + 1) * P], ident)
                end(ins, (tag, k))

        def feature_major(name, w, c, src, nk):
            bank = begin(name)
            for k in range(nk):
                ins = pe.matmul(bank[:, 0:S], w[:, k, c * P:(c + 1) * P], src[:, k, :], start=(k == 0), stop=(k == nk - 1))
            end(ins, name)

        def token_major(name, w, t, n0, n, src, nk=KD):
            bank = begin(name)
            for k in range(nk):
                ins = pe.matmul(bank[:, 0:n], src[:, k, t * P:(t + 1) * P], w[:, k, n0:n0 + n], start=(k == 0), stop=(k == nk - 1))
            end(ins, name)

        def turn(name, rot, src, after):
            wait_freed(pe, after)
            end(pe.matmul(begin(name)[:, 0:S], C(rot), src, start=True, stop=True), name)

        def attention(base, n, queries, keys, values):
            for i in range(n + LAG):
                if i < n:
                    g = base + i
                    kind, h = heads[g]
                    bank = begin(("S", g))
                    for t in range(TILES):
                        fox = kind == "fox"
                        ins = pe.matmul(bank[:, t * S:(t + 1) * S], queries(kind, h)[:, t * P:(t + 1) * P], keys(kind, h),
                                        start=True, stop=not fox)
                        if fox:
                            ins = pe.matmul(bank[:, t * S:(t + 1) * S], ident[0:SH, h:h + 1].to_broadcast([SH, P]), f_cum[0:SH, :],
                                            start=False, stop=True)
                    end(ins, ("S", g))
                if 2 <= i < n + 2:
                    g = base + i - 2
                    pe.wait_ge(probs_ready, g + 1)
                    bank = begin(("T", g))
                    for k in range(TILES):
                        for t in range(TILES):
                            ins = pe.transpose(bank[:, k * S + t * P:k * S + (t + 1) * P], p_buf[g % 2][:, t, k * P:(k + 1) * P], ident)
                    end(ins, ("T", g))
                if i >= LAG:
                    g = base + i - LAG
                    bank = begin(("V", g))
                    wait_freed(pe, ("T", g))
                    for k in range(TILES):
                        ins = pe.matmul(bank[:, 0:S], values(*heads[g], k), pt_buf[g % 2][:, k, :], start=(k == 0), stop=(k == TILES - 1))
                    end(ins, ("V", g))

        pe.wait_ge(const_in, 32)
        transposes("memT", work, 1)
        wait_freed(pe, ("memT", KD - 1))
        w = unit(("mem_kv", 0), KD, 512)
        for c in range(MH):
            feature_major(("km", c), w, c, actT, KD)
        w = unit(("mem_kv", 1), KD, 512)
        for t in range(TILES):
            token_major(("vm", t), w, t, 0, 512, actT)
        transposes("hT", work, 2)
        wait_freed(pe, ("hT", KD - 1))
        qk = lambda c: qa[:, c, :] if c < C_K else ka[:, c - C_K, :]
        for c in range(C_V):
            feature_major(("in", c), unit(("w_in", c // 4), KD, 512), c % 4, actT, KD)
            if c >= 1:
                turn(("rope", c - 1), "rot1", qk(c - 1), ("in", c - 1))
        for t in range(TILES):
            token_major(("v", t), unit(("w_in", 2), KD, 512), t, 0, AKV * HD, actT)
            if t == 0:
                turn(("rope", C_V - 1), "rot1", qk(C_V - 1), ("in", C_V - 1))
        for c in range(C_XL, N_IN):
            feature_major(("in", c), unit(("w_in", c // 4), KD, 512 if c < 48 else 256), c % 4, actT, KD)
        pe.wait_ge(rope_ready, C_V)
        attention(0, N1, lambda kind, h: (qa if kind == "self1" else qm)[:, h, :],
                  lambda kind, h: ka[:, h // GROUP, :] if kind == "self1" else km[:, h, :],
                  lambda kind, h, k: va[:, k, h // GROUP * HD:(h // GROUP + 1) * HD] if kind == "self1" else vm[:, k, h * HD:(h + 1) * HD])
        wr, wi = unit("lru_w", 12, P), unit("lru_w", 12, P, 12 * P)
        pe.wait_ge(conv_ready, LB)
        for d in range(2):
            for b in range(LB):
                bank = begin(("lru", d, b))
                pe.matmul(bank[:, 0:S], wr[:, d * LB + b, :], xc[:, b, :], start=True, stop=True)
                end(pe.matmul(bank[:, S:2 * S], wi[:, d * LB + b, :], xc[:, b, :], start=True, stop=True), ("lru", d, b))
        wait_freed(pe, ("V", N1 - 1))
        for br, (name, nk, src) in enumerate((("p_attn", AH, qa), ("p_lru", LB, gl), ("p_mem", MH, qm))):
            if br == 1:
                pe.wait_ge(lru_done, 2)
            for c in range(KD):
                feature_major(("merge", br, c), unit((name, c // 4), nk, 512), c % 4, src, nk)
        pe.wait_ge(merged, KD)
        for t in range(TILES):
            for h in range(HALVES):
                token_major(("out1", t, h), unit(("w_out", h), KD, 512), t, 0, 512, gates)
        transposes("h2T", work, 3)
        wait_freed(pe, ("h2T", KD - 1))
        pe.sem_inc(v_used, USED0)
        keys = unit("sub_keys", 2 * PH, PK)
        for g in range(4):
            for c in range(4 * g, 4 * g + 4):
                feature_major(("pq", c), unit(("peer_q", g), KD, 512), c % 4, actT, KD)
            wait_freed(pe, ("pq", 4 * g + 3))
            for t in range(TILES):
                bank = begin(("sc", t, g))
                for c in range(4):
                    ins = pe.matmul(bank[:, c * PK:(c + 1) * PK], pq[:, 4 * g + c, t * P:(t + 1) * P], keys[:, 4 * g + c, :],
                                    start=True, stop=True)
                end(ins, ("sc", t, g))

        def memory2(layer):
            w = unit(("mem_kv2", layer), KD, 512)
            for c in range(2):
                feature_major(("km2", layer, c), w, c, mem2T, KD)
            for t in range(TILES):
                token_major(("vm2", layer, t), w, t, 256, 256, mem2T)

        wait_freed(pe, ("sc", TILES - 1, 3))

        def weighted_sum(s, t, first):
            for k in range(TOPK):
                pe.wait_ge(diag_done, s * TOPK + k + 1)
                pe.wait_ge(v_in[k % UV], s * 32 + 16 * (k // UV + 1))
                for half in range(HALVES):
                    ins = pe.matmul(psum[:, peer_bank(t, half), :], diag[:, k, :], v_ring[:, k % UV, 512 * half:512 * half + 512],
                                    start=(first and k == 0), stop=(k == TOPK - 1), skip_group_check=True)
                ins.then_inc(v_used, 1)

        for t in range(TILES):
            weighted_sum(t, t, True)
        pe.wait_ge(mem2_in, 16)
        memory2(0)
        with pe.Fori(1, PH) as h:
            for t in range(TILES):
                weighted_sum(h * TILES + t, t, False)
        transposes("x2T", x_tok, 4)
        wait_freed(pe, ("x2T", KD - 1))
        for layer in range(2):
            if layer:
                memory2(layer)
            nk = SKV if layer == 0 else SH // 2
            raw = lambda c: q2[:, c, :] if c < SH // 2 else k_raw[:, c % 2, :]
            if layer == 1:
                wait_freed(pe, ("x3T", KD - 1))
            for c in range(SH // 2 + nk):
                feature_major(("in2", layer, c), unit(("w_in2", layer, c // 4), KD, 512), c % 4, actT, KD)
                if c >= 1 and layer == 0:
                    turn(("rope2", c - 1), "rot2", raw(c - 1), ("in2", 0, c - 1))
            if layer == 0:
                turn(("rope2", SH // 2 + nk - 1), "rot2", raw(SH // 2 + nk - 1), ("in2", 0, SH // 2 + nk - 1))
                for t in range(TILES):
                    token_major(("v2", 0, t, 0), unit(("w_in2", 0, 2), KD, 512), t, P, 3 * P, actT)
                for c in range(2):
                    feature_major(("qm2", 0, c), unit(("w_in2", 0, 3), KD, 256), c, actT, KD)
                pe.wait_ge(rope_ready, C_V + SH // 2 + nk)
            else:
                for t in range(TILES):
                    token_major(("v2", 1, t, 0), unit(("w_in2", 1, 3), KD, 512), t, 0, 512, actT)
                    token_major(("v2", 1, t, 1), unit(("w_in2", 1, 4), KD, 512), t, 0, 256, actT)
                for c in range(2):
                    feature_major(("qm2", 1, c), unit(("w_in2", 1, 4), KD, 512), 2 + c, actT, KD)
                bank = begin(("forget",))
                wf = col("w_forget", 0, KD * SH).rearrange("p (k n) -> p k n", k=KD)
                for k in range(KD):
                    ins = pe.matmul(bank[0:SH, 0:S], wf[:, k, :], actT[:, k, :], start=(k == 0), stop=(k == KD - 1))
                end(ins, ("forget",))
                pe.wait_ge(cum_ready, 1)
            wait_freed(pe, ("qm2", layer, 1))
            attention(pl.att2[layer], SH + MH2,
                      lambda kind, h: qm2[:, h // 2, :] if kind == "mem2" else q2[:, h // 2, :],
                      lambda kind, h: {"swa": lambda: kz[:, 2 * (h // 4) + h % 2, :], "fox": lambda: kz[:, h, :],
                                       "mem2": lambda: kmz[:, h, :]}[kind](),
                      lambda kind, h, k: {"swa": lambda: v2[:, k, h // 4 * P:(h // 4 + 1) * P],
                                          "fox": lambda: v2[:, k, h // 2 * P:(h // 2 + 1) * P],
                                          "mem2": lambda: vm2[:, k, h // 2 * P:(h // 2 + 1) * P]}[kind]())
            wait_freed(pe, ("V", pl.att2[layer] + SH + MH2 - 1))
            for t in range(TILES):
                for h in range(HALVES):
                    token_major(("out2", layer, t, h), unit(("w_out2", layer, h), KD, 512), t, 0, 512, actT)
            transposes(("aT", layer), x_tok, 5 + 2 * layer)
            wait_freed(pe, (("aT", layer), KD - 1))
            if layer == 0:
                for f in range(FC):
                    w = unit(("ff_in", f // 2), 2 * KD, S)
                    bank = begin(("ff", f))
                    for g in range(2):
                        for k in range(KD):
                            ins = pe.matmul(bank[:, g * S:(g + 1) * S], w[:, g * KD + k, f % 2 * P:(f % 2 + 1) * P], actT[:, k, :],
                                            start=(k == 0), stop=(k == KD - 1))
                    end(ins, ("ff", f))
                pe.wait_ge(ff_ready, FC)
                for t in range(TILES):
                    for h in range(HALVES):
                        begin(("down", t, h))
                f = 0
                for o, n in enumerate(OUT_ROWS):
                    w = unit(("ff_out", o), n, D)
                    for k in range(n):
                        for t in range(TILES):
                            for h in range(HALVES):
                                ins = pe.matmul(psum[:, pl.bank[("down", t, h)], :], ffT[:, f, t * P:(t + 1) * P],
                                                w[:, k, 512 * h:512 * h + 512], start=(f == 0), stop=(f == FC - 1))
                                if f == FC - 1:
                                    end(ins, ("down", t, h))
                        f += 1
                    if o < len(OUT_ROWS) - 1:
                        ins.then_inc(ff_out_used, 1)
                transposes("x3T", x_tok, 6)
        pe.sem_inc(e_product, e_at(GATHERED[0], False))
        wr = col("w_router", 0, KD * NE).rearrange("p (k n) -> p k n", k=KD)
        for t in range(TILES):
            token_major(("router", t), wr, t, 0, NE, actT)
        pe.wait_ge(router_e, 2)
        bank = begin(("place",))
        pe.matmul(bank[:, 0:NE], before, r_mask[:, 0, :], start=True, stop=True)
        pe.matmul(bank[:, NE:2 * NE], before, r_mask[:, 1, :], start=True, stop=False)
        pe.matmul(bank[:, NE:2 * NE], ones, r_mask[:, 0, :], start=False, stop=True)
        pe.matmul(bank[:, 2 * NE:3 * NE], ones, r_mask[:, 0, :], start=True, stop=False)
        end(pe.matmul(bank[:, 2 * NE:3 * NE], ones, r_mask[:, 1, :], start=False, stop=True), ("place",))
        pe.wait_ge(routed, 1)
        wait_freed(pe, ("place",))

        def bank_of(j, b, over):
            i, back = e_before(j, over)
            by = e_by(i)
            if not back:
                pe.wait_ge(e_freed[by], b * e_n[by] + e_nth(i, over) + e_n[by])
            elif over:
                pe.wait_ge(e_freed["vector"], b * e_n["vector"] + e_n["vector"])
                pe.wait_ge(e_freed["scalar"], b * e_n["scalar"] + e_n["scalar"])
            else:
                pe.wait_ge(e_freed[by], b * e_n[by] + e_nth(i, over))
            return psum[:, E_BANK[j], :]

        def gather_tokens(b, over):
            pe.wait_ge(picked, b + 2)
            for j in GATHERED:
                bank = psum[:, E_BANK[j], :] if isinstance(b, int) and b < 0 else bank_of(j, b, over)
                for k in range(4):
                    at = (4 * j[1] + k) * P
                    for t in range(TILES):
                        ins = pe.matmul(bank[:, k * P:(k + 1) * P], x_tok[:, t, at:at + P], pick[:, t, :],
                                        start=(t == 0), stop=(t == TILES - 1))
                ins.then_inc(e_product, 1)

        def turn_selection(b, over):
            j = ("pickT", 0)
            bank = psum[:, E_BANK[j], :] if isinstance(b, int) and b < 0 else bank_of(j, b, over)
            for t in range(TILES):
                ins = pe.transpose(bank[:, t * P:(t + 1) * P], pickg[:, t, :], ident)
            ins.then_inc(e_product, 1)

        def expert(e, b, over):
            if over:
                gather_tokens(b, over)
                turn_selection(b, over)
            wait_split(pe, e_low, GATHERED[-1], turn_before(GATHERED[-1], b, over), over)
            for j in Y:
                if j[0] == "ge":
                    n = j[1]
                    bank = bank_of(j, b, over)
                    pe.wait_ge(e_freed["vector"], b * e_n["vector"] + e_n["vector"] + e_nth(("up", n), over))
                    for f in range(2):
                        ins = pe.transpose(bank[:, f * P:(f + 1) * P], gated[:, n % 2, f * P:(f + 1) * P], ident)
                    ins.then_inc(e_product, 1)
                    continue
                i = next(i for i in range(N_PIECE) if piece_end(i) == j)
                hi, low = hi_of(i), low_of(i)
                if i < 2 * N_UP:
                    n, half = divmod(i, 2)
                    bank = bank_of(("up", n), b, over) if half == 0 else psum[:, E_BANK["up", n], :]
                    bank = bank.rearrange("p (g n) -> p g n", g=2)
                    wait_split(pe, e_low, ("piece", i), turn_before(("piece", i), b, over), over)
                    for m in range(4):
                        k = 4 * half + m
                        h_, l_ = hi[:, :, m * S:(m + 1) * S], low[:, :, m * S:(m + 1) * S]
                        pe.matmul(bank, xe_hi[:, k, :], h_, start=(k == 0), stop=False)
                        pe.matmul(bank, xe_hi[:, k, :], l_, start=False, stop=False)
                        ins = pe.matmul(bank, xe_low[:, k, :], h_, start=False, stop=(k == KD - 1))
                else:
                    o, h = divmod(i - 2 * N_UP, HALVES)
                    bank = bank_of(("y", h), b, over) if o == 0 else psum[:, E_BANK["y", h], :]
                    f0 = sum(OUT_ROWS[:o])
                    wait_split(pe, e_low, ("ge", (f0 + OUT_ROWS[o] - 1) // 2), b, over)
                    wait_split(pe, e_low, ("piece", i), b, over)
                    for k in range(OUT_ROWS[o]):
                        f = f0 + k
                        pe.matmul(bank, ge_hi[:, f, :], hi[:, k, :], start=(f == 0), stop=False)
                        pe.matmul(bank, ge_hi[:, f, :], low[:, k, :], start=False, stop=False)
                        ins = pe.matmul(bank, ge_low[:, f, :], hi[:, k, :], start=False, stop=(f == FC - 1))
                ins.then_inc(e_product, 1)
            if not over:
                gather_tokens(b, over)
            for j in SUMS:
                t, h = divmod(j[1], HALVES)
                bank = bank_of(j, b, over)
                pe.wait_ge(e_freed["scalar"], b * e_n["scalar"] + e_n["scalar"] + e_nth(("y", h), over))
                pe.matmul(bank, pickT[:, t, :], ye[:, 512 * h:512 * h + 512], start=True, stop=True).then_inc(e_product, 1)
            if not over:
                turn_selection(b, over)

        def skip(b):
            pe.wait_ge(e_product, b * N_EP + N_EP)
            pe.sem_inc(e_product, N_EP)

        gather_tokens(-1, False)
        pe.wait_ge(e_product, e_at(GATHERED[-1], False) + 1)
        pe.sem_inc(e_product, N_SUM)
        turn_selection(-1, False)
        each_expert(pe, expert, skip)

    @block.vector
    def _(dve):
        own = Own(dve, vector_step)

        def give(ins, name, wait=False):
            ins.then_inc(freed["vector"], 1)
            assert pl.freed[name] == ("vector", give.n + 1), name
            give.n += 1
            if wait:
                dve.wait_ge(freed["vector"], give.n)

        give.n = 0
        n_square, n_normed, n_row, n_angle, n_rope = [0], [0], [0], [0], [0]

        def tell(ins, s, count, wait=False):
            count[0] += 1
            ins.then_inc(s, 1)
            if wait:
                dve.wait_ge(s, count[0])

        def rms_norm(src, dst):
            for t in range(TILES):
                own(dve.tensor_tensor_reduce(dst[:, t, :] if dst is not src else rms_junk, src[:, t, :], src[:, t, :], 1.0, 0.0, ALU.mult, ALU.add,
                                             stat[:, t:t + 1]))
            tell(dve.tensor_scalar(stat, stat, 1.0 / D, EPS, ALU.mult, ALU.add), square_ready, n_square)
            dve.wait_ge(root_ready, n_square[0])
            own(dve.reciprocal(rstd, rstd))
            row = wait_row(dve, n_row[0])
            n_row[0] += 1
            for t in range(TILES):
                tell(dve.scalar_tensor_tensor(dst[:, t, :], src[:, t, :], rstd[:, t:t + 1], row, ALU.mult, ALU.mult), normed, n_normed, True)
            dve.sem_inc(row_used, 1)

        rms_junk = work[:, 0, :]

        def layer_norm():
            for t in range(TILES):
                for h in range(2):
                    own(dve.bn_stats(bn[:, 12 * t + 6 * h:12 * t + 6 * h + 6], x_tok[:, t, 512 * h:512 * h + 512]))
                own(dve.bn_aggr(mv[:, 2 * t:2 * t + 2], bn[:, 12 * t:12 * t + 12]))
                own(dve.tensor_scalar(stat[:, t:t + 1], mv[:, 2 * t + 1:2 * t + 2], LN_EPS, None, ALU.add))
            dve.sem_inc(square_ready, 1)
            n_square[0] += 1
            dve.wait_ge(root_ready, n_square[0])
            own(dve.reciprocal(rstd, rstd))
            g, b = wait_row(dve, n_row[0]), wait_row(dve, n_row[0] + 1)
            n_row[0] += 2
            for t in range(TILES):
                own(dve.tensor_scalar(x_tok[:, t, :], x_tok[:, t, :], mv[:, 2 * t:2 * t + 1], rstd[:, t:t + 1], ALU.subtract, ALU.mult))
            for t in range(TILES):
                own(dve.tensor_tensor(x_tok[:, t, :], x_tok[:, t, :], g, ALU.mult))
            for t in range(TILES):
                tell(dve.tensor_tensor(x_tok[:, t, :], x_tok[:, t, :], b, ALU.add), normed, n_normed, True)
            dve.sem_inc(row_used, 2)

        TURN = 2 * math.pi
        T1 = 6.28125
        T2 = round((TURN - T1) * 2 ** 20) / 2 ** 20
        T3 = TURN - T1 - T2
        ROUND = 1.5 * 2 ** 23
        PI = 3.1415925

        def rope_tables(i):
            dve.wait_ge(pos_in, 16 * (i + 1))
            own(dve.tensor_copy(ang, pos_i))
            own(dve.tensor_scalar(ang, ang, C(("freq1", "freq2")[i]), None, ALU.mult))
            own(dve.tensor_scalar(turns, ang, 1.0 / TURN, ROUND, ALU.mult, ALU.add))
            own(dve.tensor_scalar(turns, turns, ROUND, None, ALU.subtract))
            for part in (T1, T2, T3):
                own(dve.scalar_tensor_tensor(ang, turns, -part, ang, ALU.mult, ALU.add))
            tell(dve.tensor_scalar(ang, ang, PI, -PI, ALU.min, ALU.max), angle_ready, n_angle, True)
            own(dve.scalar_tensor_tensor(turns, ang, -1.0, ang, ALU.mult, ALU.min))
            tell(dve.tensor_scalar(turns, turns, math.pi / 2, None, ALU.add), angle_ready, n_angle)

        def rope(name, raw, after, outs=None):
            bank = wait_product(dve, name)
            dve.wait_ge(table_ready, 2 if name[0] == "rope" else 4)
            t = rope_t[:, n_rope[0] % 2, :]
            wait_freed(dve, after)
            give(dve.tensor_tensor(t, bank[:, 0:S], rope_sin, ALU.mult), name, True)
            own(dve.tensor_tensor(raw, raw, rope_cos, ALU.mult))
            if outs is None:
                tell(dve.tensor_tensor(raw, raw, t, ALU.add), rope_ready, n_rope, True)
            else:
                own(dve.tensor_tensor(outs[0][0:HD2], raw[0:HD2], t[0:HD2], ALU.add))
                tell(dve.tensor_tensor(outs[1][HD2:P], raw[HD2:P], t[HD2:P], ALU.add), rope_ready, n_rope, True)

        n_max = [0]
        no_mask = C("band")[:, 0:1].to_broadcast([P, S])

        def attention(base, n, out):
            for i in range(n + LAG):
                if i < n:
                    g = base + i
                    b = g % 2
                    kind, h = heads[g]
                    bank = wait_product(dve, ("S", g)).rearrange("p (t s) -> p t s", t=TILES)
                    mask = {"self1": "band", "swa": "chunks", "fox": "causal"}.get(kind)
                    scale = HD ** -0.5 if kind in ("self1", "mem1") else SCALE2
                    m = nmax[:, 2 * b:2 * b + 2]
                    for t in range(TILES):
                        ins = dve.tensor_tensor_reduce(s_buf[b][:, t, :], bank[:, t, :], C(mask)[:, t * S:(t + 1) * S] if mask else no_mask,
                                                       scale, -3.0e38, ALU.add, ALU.max, m[:, t:t + 1])
                    give(ins, ("S", g), True)
                    if kind in ("self1", "swa"):
                        ins = dve.tensor_scalar(m, m, col("sink" if kind == "self1" else "sink2", h), -1.0, ALU.max, ALU.mult)
                    else:
                        ins = dve.tensor_scalar(m, m, -1.0, None, ALU.mult)
                    tell(ins, max_ready, n_max)
                if 1 <= i <= n:
                    g = base + i - 1
                    b = g % 2
                    kind, h = heads[g]
                    dve.wait_ge(exp_ready, g + 1)
                    dd, ss = den[:, 2 * b:2 * b + 2], esum[:, 2 * b:2 * b + 2]
                    if kind in ("self1", "swa"):
                        own(dve.tensor_tensor(dd, ss, esink[:, 2 * b:2 * b + 2], ALU.add))
                        ss = dd
                    dve.reciprocal(dd, ss).then_inc(sums_ready, 1)
                if i >= LAG:
                    g = base + i - LAG
                    bank = wait_product(dve, ("V", g))
                    p0, p1, dst = out(*heads[g])
                    give(dve.tensor_copy(dst[p0:p1], bank[p0:p1, 0:S]), ("V", g))

        dve.wait_ge(mem_in, 16)
        dve.wait_ge(const_in, 32)
        for t in range(TILES):
            own(dve.tensor_tensor_reduce(region[:, 4096 + t * D:4096 + (t + 1) * D], work[:, t, :], work[:, t, :], 1.0, 0.0, ALU.mult, ALU.add, stat[:, t:t + 1]))
        tell(dve.tensor_scalar(stat, stat, 1.0 / D, EPS, ALU.mult, ALU.add), square_ready, n_square)
        dve.wait_ge(root_ready, 1)
        own(dve.reciprocal(rstd, rstd))
        row = wait_row(dve, 0)
        n_row[0] = 1
        for t in range(TILES):
            tell(dve.scalar_tensor_tensor(work[:, t, :], work[:, t, :], rstd[:, t:t + 1], row, ALU.mult, ALU.mult), normed, n_normed, True)
        dve.sem_inc(row_used, 1)
        rope_tables(0)
        dve.wait_ge(x_in, 16)
        dve.wait_ge(product_ready, pl.nth[("memT", KD - 1)])
        rms_norm(x_tok, work)
        for c in range(C_V):
            rope(("rope", c), qa[:, c, :] if c < C_K else ka[:, c - C_K, :], ("in", c))
        dve.wait_ge(product_ready, pl.nth[("hT", KD - 1)])
        for b in range(LB):
            wait_freed(dve, ("in", C_XL + b))
            w = lambda j: col("conv_w", j * LB + b)
            own(dve.tensor_scalar(xc[:, b, :], xl[:, b, :], w(2), col("conv_b", b), ALU.mult, ALU.add))
            own(dve.scalar_tensor_tensor(xc[:, b, 2:S], xl[:, b, 0:S - 2], w(0), xc[:, b, 2:S], ALU.mult, ALU.add))
            own(dve.scalar_tensor_tensor(xc[:, b, 1:S], xl[:, b, 0:S - 1], w(1), xc[:, b, 1:S], ALU.mult, ALU.add))
            dve.scalar_tensor_tensor(xc[:, b, 0:S - 1], xl[:, b, 1:S], w(3), xc[:, b, 0:S - 1], ALU.mult, ALU.add).then_inc(conv_ready, 1)
        attention(0, N1, lambda kind, h: (0, P, (qa if kind == "self1" else qm)[:, h, :]))
        lam = col("lam", 0, 12)
        own(dve.tensor_scalar(sp_p, lam, -1.0, None, ALU.mult))
        dve.tensor_tensor(sp_z, sp_p, lam, ALU.min).then_inc(lam_exp, 1)
        dve.wait_ge(lam_exp, 2)
        own(dve.tensor_scalar(sp_z, sp_e, 2.0, None, ALU.add))
        own(dve.reciprocal(sp_z, sp_z))
        own(dve.tensor_tensor(sp_e, sp_e, sp_z, ALU.mult))
        own(dve.tensor_tensor(sp_z, sp_e, sp_e, ALU.mult))
        own(dve.tensor_scalar(sp_p, sp_z, 1.0 / 17, 1.0 / 15, ALU.mult, ALU.add))
        for n in (13, 11, 9, 7, 5, 3, 1):
            own(dve.tensor_tensor(sp_p, sp_p, sp_z, ALU.mult))
            own(dve.tensor_scalar(sp_p, sp_p, 1.0 / n, None, ALU.add))
        own(dve.scalar_tensor_tensor(sp_e, sp_e, 2.0, sp_p, ALU.mult, ALU.mult))
        own(dve.tensor_scalar(sp_p, lam, -1.0, 0.0, ALU.mult, ALU.max))
        own(dve.tensor_tensor(sp_p, sp_p, sp_e, ALU.add))
        own(dve.tensor_scalar(sp_e, sp_p, -8.0, None, ALU.mult))
        dve.tensor_scalar(sp_p, sp_p, 8.0, None, ALU.mult).then_inc(lam_ready, 1)
        for d in range(2):
            for b in range(LB):
                r, i = lru_ri[:, b, 0, :], lru_ri[:, b, 1, :]
                dve.wait_ge(lru_at, d * LB + b + 1)
                own(dve.tensor_tensor(i, i, xc[:, b, :], ALU.mult))
                tmp = actT_flat[:, LB * S:LB * S + S]
                own(dve.tensor_tensor(tmp, lru_a[:, b, :], lru_a[:, b, :], ALU.mult))
                dve.scalar_tensor_tensor(r, tmp, 1.0, r, ALU.add, ALU.mult).then_inc(lru_sq_in, 1)
                dve.wait_ge(lru_sq_in, d * LB + b + 1)
            for b in range(LB):
                r, i = lru_ri[:, b, 0, :], lru_ri[:, b, 1, :]
                dve.wait_ge(lru_sq_out, d * LB + b + 1)
                own(dve.tensor_tensor(i, i, r, ALU.mult))
                if d == 0:
                    own(dve.tensor_tensor_scan(xl[:, b, :], lru_a[:, b, :], i, 0.0, ALU.mult, ALU.add))
                else:
                    own(dve.tensor_tensor_scan(r[:, ::-1], lru_a[:, b, ::-1], i[:, ::-1], 0.0, ALU.mult, ALU.add))
                    own(dve.tensor_tensor(r, r, xl[:, b, :], ALU.add))
                    own(dve.tensor_tensor(gl[:, b, :], gl[:, b, :], r, ALU.mult))
            dve.sem_inc(lru_done, 1)
        for br in range(3):
            for c in range(KD):
                bank = wait_product(dve, ("merge", br, c))[:, 0:S]
                if br == 0:
                    give(dve.tensor_tensor(gates[:, c, :], gates[:, c, :], bank, ALU.mult), ("merge", br, c), True)
                else:
                    gg = gates[:, br * KD + c, :]
                    give(dve.tensor_tensor(gg, gg, bank, ALU.mult), ("merge", br, c), True)
                    ins = dve.tensor_tensor(gates[:, c, :], gates[:, c, :], gg, ALU.add)
                    if br == 1:
                        own(ins)
                    else:
                        ins.then_inc(merged, 1)
        for t in range(TILES):
            for h in range(HALVES):
                bank = wait_product(dve, ("out1", t, h))
                xx = x_tok[:, t, 512 * h:512 * h + 512]
                give(dve.tensor_tensor(xx, xx, bank, ALU.add), ("out1", t, h), True)
        rms_norm(x_tok, work)
        dve.sem_inc(dots_done, DOTS0)
        dve.memset(kmz, 0.0).then_inc(zeros_ready, 1)
        dve.wait_ge(zeros_ready, 1)

        def search_for(s, t):
            n = [0]

            def step(ins, wait=True):
                n[0] += 1
                ins.then_inc(search_step, 1)
                if wait:
                    wait_steps()

            def wait_steps():
                dve.wait_ge(search_step, s * N_SEARCH + n[0])

            def wait_turn():
                n[0] += 1
                dve.sem_inc(search_step, 1)

            head = bass.ds((s - t), 2) if not isinstance(s, int) else slice(s - t, s - t + 2)
            step(dve.tensor_copy(find, sc[:, t, head, :]))
            wait_turn()
            step(dve.max(top_v[:, 0, 0:8], find[:, 0, :]), False)
            step(dve.max(top_v[:, 1, 0:8], find[:, 1, :]))
            wait_turn()
            for x in range(2):
                step(dve.match_replace(find_less[:, x, :], top_v[:, x, 0:8], find[:, x, :], -3.0e38), False)
                step(dve.max_index(top_u[:, x, 0:8], top_v[:, x, 0:8], find[:, x, :]), x == 1)
            wait_turn()
            step(dve.max(top_v[:, 0, 8:16], find_less[:, 0, :]), False)
            step(dve.max(top_v[:, 1, 8:16], find_less[:, 1, :]))
            step(dve.tensor_tensor(cand.rearrange("p (i j) -> p i j", i=TOPK), top_v[:, 0, :].unsqueeze(2).to_broadcast([P, TOPK, TOPK]),
                                   top_v[:, 1, :].unsqueeze(1).to_broadcast([P, TOPK, TOPK]), ALU.add), False)
            for x in range(2):
                step(dve.max_index(top_u[:, x, 8:16], top_v[:, x, 8:16], find_less[:, x, :]), x == 1)
            step(dve.tensor_copy(top_f, top_u), False)
            step(dve.max(best[:, 0:8], cand))
            wait_turn()
            step(dve.match_replace(cand_less, best[:, 0:8], cand, -3.0e38), False)
            step(dve.max_index(best_u[:, 0:8], best[:, 0:8], cand))
            wait_turn()
            step(dve.max(best[:, 8:16], cand_less))
            step(dve.tensor_scalar(best_z, best, best[:, 0:1], None, ALU.subtract), False)
            wait_steps()
            dve.sem_inc(best_ready, 1)
            step(dve.max_index(best_u[:, 8:16], best[:, 8:16], cand_less))
            step(dve.tensor_scalar(place_u[:, 0, :], best_u, 4, None, ALU.logical_shift_right), False)
            step(dve.tensor_scalar(place_u[:, 1, :], best_u, 15, None, ALU.bitwise_and))
            step(dve.tensor_copy(place_f, place_u))
            step(dve.tensor_tensor(hot, place_f.unsqueeze(3).to_broadcast([P, 2, TOPK, TOPK]),
                                   C("iota")[:, 0:TOPK].unsqueeze(1).unsqueeze(1).to_broadcast([P, 2, TOPK, TOPK]), ALU.is_equal))
            step(dve.tensor_tensor(hot, hot, top_f.unsqueeze(2).to_broadcast([P, 2, TOPK, TOPK]), ALU.mult))
            step(dve.tensor_reduce(key_f, hot, AX.X, ALU.add))
            step(dve.scalar_tensor_tensor(idx_f, key_f[:, 0, :], float(PK), key_f[:, 1, :], ALU.mult, ALU.add))
            step(dve.tensor_copy(idx_u[:, t, :], idx_f))
            dve.sem_inc(search_done, 1)
            dve.wait_ge(best_exp, s + 1)
            step(dve.reciprocal(den[:, 0:1], esum[:, 0:1]))
            step(dve.tensor_scalar(gate_st[:, t, :], best_e, den[:, 0:1], None, ALU.mult))
            assert n[0] == N_SEARCH

        N_SEARCH = 34

        def peer_step(dots, total, search):
            if total is not None:
                s, t = total
                dve.wait_ge(v_used, USED0 + (s - 1) * TOPK)
                dve.tensor_copy(idx_v[:, t, :], idx_u[:, t, :]).then_inc(v_index, 1)
                dve.wait_ge(gelu_done, s + 1)
                dve.tensor_tensor(pick_w[:, t, :], u_act[:, t, :], gate_st[:, t, :], ALU.mult).then_inc(weights_done, 1)
                dve.wait_ge(v_index, s + 1)
                dve.wait_ge(weights_done, s + 1)
            if search is not None:
                search_for(*search)
            if dots is not None:
                s, t = dots
                for k in range(TOPK):
                    dve.wait_ge(u_in[k % UV], s * 32 + 16 * (k // UV + 1))
                    dve.tensor_tensor_reduce(u_ring[:, k % UV, :], u_ring[:, k % UV, :], work[:, t, :], 1.0, 0.0, ALU.mult, ALU.add,
                                             u_dot[:, t, k:k + 1]).then_inc(dots_done, 1)

        def all_scores():
            wait_freed(dve, ("sc", TILES - 1, 3))

        wait_freed(dve, ("sc", TILES - 1, 0))
        search_for(0, 0)
        peer_steps(dve, peer_step, all_scores)
        dve.memset(kz, 0.0).then_inc(zeros_ready, 1)
        dve.wait_ge(zeros_ready, 2)
        rope_tables(1)
        dve.wait_ge(v_used, USED0 + STEPS * TOPK)
        for t in range(TILES):
            for half in range(HALVES):
                xx = x_tok[:, t, 512 * half:512 * half + 512]
                own(dve.tensor_tensor(xx, xx, psum[:, peer_bank(t, half), :], ALU.add))
        for t in range(TILES):
            own(dve.tensor_tensor_reduce(work[:, t, :], x_tok[:, t, :], x_tok[:, t, :], 1.0, 0.0, ALU.mult, ALU.add, stat[:, t:t + 1]))
        tell(dve.tensor_scalar(stat, stat, 1.0 / D, EPS, ALU.mult, ALU.add), square_ready, n_square)
        dve.wait_ge(root_ready, n_square[0])
        own(dve.reciprocal(rstd, rstd))
        row = wait_row(dve, n_row[0])
        n_row[0] += 1
        for t in range(TILES):
            tell(dve.scalar_tensor_tensor(x_tok[:, t, :], x_tok[:, t, :], rstd[:, t:t + 1], row, ALU.mult, ALU.mult), normed, n_normed, True)
        dve.sem_inc(row_used, 1)
        for layer in range(2):
            if layer == 1:
                own(dve.memset(kz, 0.0))
                dve.sem_inc(zeros_ready, 1)
            if layer == 0:
                for c in range(SH // 2 + SKV):
                    if c < SH // 2:
                        rope(("rope2", c), q2[:, c, :], ("in2", 0, c))
                    else:
                        j = 2 * (c - SH // 2)
                        rope(("rope2", c), k_raw[:, c % 2, :], ("in2", 0, c), (kz[:, j, :], kz[:, j + 1, :]))
            else:
                bank = wait_product(dve, ("forget",))
                z = f_log[0:SH, :]
                t = f_tmp[0:SH, :]
                give(dve.tensor_scalar(z, bank[0:SH, 0:S], col("b_forget")[0:SH], None, ALU.add), ("forget",), True)
                own(dve.tensor_scalar(t, z, -1.0, None, ALU.mult))
                dve.tensor_tensor(t, t, z, ALU.min).then_inc(forget_exp, 1)
                dve.wait_ge(forget_e, 1)
                own(dve.tensor_scalar(z, z, 0.0, None, ALU.min))
                own(dve.tensor_tensor(z, z, t, ALU.subtract))
                own(dve.memset(t, 1.0))
                own(dve.tensor_tensor_scan(f_cum[0:SH, :], t, z, 0.0, ALU.mult, ALU.add))
                dve.tensor_scalar(f_cum[0:SH, :], f_cum[0:SH, :], -1.0 / SCALE2, None, ALU.mult).then_inc(cum_ready, 1)

            def out(kind, h):
                c = h // 2 if kind != "mem2" else SH // 2 + h // 2
                return h % 2 * HD2, h % 2 * HD2 + HD2, actT[:, c, :]

            attention(pl.att2[layer], SH + MH2, out)
            for t in range(TILES):
                for h in range(HALVES):
                    bank = wait_product(dve, ("out2", layer, t, h))
                    xx = x_tok[:, t, 512 * h:512 * h + 512]
                    give(dve.scalar_tensor_tensor(xx, xx, ALPHA, bank, ALU.mult, ALU.add), ("out2", layer, t, h), True)
            layer_norm()
            if layer == 0:
                for f in range(FC):
                    dve.wait_ge(silu_ready, f + 1)
                    bank = psum[:, pl.bank[("ff", f)], :]
                    give(dve.tensor_tensor(ffT[:, f, :], silu_ff[:, f % 2, :], bank[:, S:2 * S], ALU.mult), ("ff", f), True)
                    dve.sem_inc(ff_ready, 1)
                for t in range(TILES):
                    for h in range(HALVES):
                        bank = wait_product(dve, ("down", t, h))
                        xx = x_tok[:, t, 512 * h:512 * h + 512]
                        give(dve.scalar_tensor_tensor(xx, xx, ALPHA, bank, ALU.mult, ALU.add), ("down", t, h), True)
                layer_norm()
        own(dve.memset(ones, 1.0))
        own(dve.tensor_scalar(before, C("causal")[:, 0:P], -1.0, None, ALU.is_lt))
        for t in range(TILES):
            bank = wait_product(dve, ("router", t))
            give(dve.tensor_tensor(logits[:, t, :], bank[:, 0:NE], col("b_router", 0, NE), ALU.add), ("router", t), True)
            own(dve.max(r_top[:, t, :], logits[:, t, :]))
            own(dve.max_index(r_idx[:, t, :], r_top[:, t, :], logits[:, t, :]))
        own(dve.tensor_copy(r_idxf, r_idx))
        own(dve.tensor_tensor(r_e, r_top[:, :, 1], r_top[:, :, 0], ALU.subtract))
        dve.sem_inc(router_exp, 1)
        dve.wait_ge(router_e, 1)
        own(dve.tensor_scalar(r_den, r_e, 1.0, None, ALU.add))
        own(dve.reciprocal(r_g[:, :, 0], r_den))
        own(dve.tensor_tensor(r_g[:, :, 1], r_g[:, :, 0], r_e, ALU.mult))
        for t in range(TILES):
            own(dve.tensor_scalar(r_mask[:, t, :], C("iota")[:, 0:NE], r_idxf[:, t, 0:1], None, ALU.is_equal))
            own(dve.tensor_scalar(r_gate[:, t, 0:NE], r_mask[:, t, :], r_g[:, t, 0:1], None, ALU.mult))
            own(dve.tensor_scalar(r_hot[:, t, :], C("iota")[:, 0:NE], r_idxf[:, t, 1:2], None, ALU.is_equal))
            own(dve.tensor_tensor(r_mask[:, t, :], r_mask[:, t, :], r_hot[:, t, :], ALU.add))
            own(dve.scalar_tensor_tensor(r_gate[:, t, 0:NE], r_hot[:, t, :], r_g[:, t, 1:2], r_gate[:, t, 0:NE], ALU.mult, ALU.add))
        dve.sem_inc(router_e, 1)
        bank = wait_product(dve, ("place",))
        places = bank[:, 0:TILES * NE].rearrange("p (t e) -> p t e", t=TILES)
        own(dve.memset(r_slot, 1.0e6))
        own(dve.memset(r_gate[:, :, NE:NE + 1], 0.0))
        own(dve.tensor_scalar(r_slot[:, :, 0:NE], r_mask, -1.0e6, 1.0e6, ALU.mult, ALU.add))
        own(dve.tensor_tensor(r_slot[:, :, 0:NE], r_slot[:, :, 0:NE], places, ALU.add))
        give(dve.tensor_copy(count_i, bank[:, 2 * NE:3 * NE]), ("place",), True)
        dve.sem_inc(e_freed["vector"], e_n["vector"] - HALVES - N_SUM)
        dve.sem_inc(e_low, N_SPLIT - HIS - HALVES)
        dve.sem_inc(routed, 1)

        def wait_e(j, b, over):
            dve.wait_ge(e_product, b * N_EP + e_at(j, over) + 1 + N_EP)
            return psum[:, E_BANK[j], :]

        def select(e, b, over):
            if not isinstance(b, int) or b > 0:
                dve.wait_ge(e_product, b * N_EP)
            one = slice(e, e + 1) if isinstance(e, int) else bass.ds(e, 1)
            dve.tensor_copy(r_shift, r_slot[:, :, one].rearrange("p t e -> p (t e)")).then_inc(pick_step, 1)
            dve.wait_ge(pick_step, 3 * b + 1)
            if over:
                dve.tensor_scalar(r_shift, r_shift, float(-P), None, ALU.add).then_inc(pick_step, 1)
            else:
                dve.sem_inc(pick_step, 1)
            dve.wait_ge(pick_step, 3 * b + 2)
            dve.tensor_copy(r_den, r_gate[:, :, one].rearrange("p t e -> p (t e)")).then_inc(pick_step, 1)
            dve.wait_ge(pick_step, 3 * b + 3)
            for t in range(TILES):
                dve.tensor_scalar(pick[:, t, :], C("iota"), r_shift[:, t:t + 1], None, ALU.is_equal)
                ins = dve.tensor_scalar(pickg[:, t, :], C("iota"), r_shift[:, t:t + 1], r_den[:, t:t + 1], ALU.is_equal, ALU.mult)
            ins.then_inc(picked, 1)

        def split(what, b, over):
            kind, n = what
            wait_split(dve, e_hi, what, b, over)
            if kind == "piece":
                dve.tensor_tensor(low_of(n), piece(n), hi_of(n).bitcast(F32), ALU.subtract).then_inc(e_low, 1)
                return
            if kind == "gather":
                bank, hi, low = psum[:, E_BANK[what], :].rearrange("p (k s) -> p k s", k=4), xe_hi[:, 4 * n:4 * n + 4, :], xe_low[:, 4 * n:4 * n + 4, :]
            else:
                bank, hi, low = psum[:, E_BANK[what], 0:S].rearrange("p (f s) -> p f s", f=2), ge_hi[:, 2 * n:2 * n + 2, :], ge_low[:, 2 * n:2 * n + 2, :]
            dve.tensor_tensor(low, bank, hi.bitcast(F32), ALU.subtract).then_inc(e_low, 1)
            dve.wait_ge(e_low, b * N_SPLIT + N_SPLIT + E_SPLITS[over].index(what) + 1)
            dve.sem_inc(e_freed["vector"], 1)

        def expert(e, b, over):
            select(e if over else e + 1, b + 1, over)
            if over:
                for j in GATHERED + FIRST:
                    split(j, b, over)
            for j in E_SEQ:
                if j[0] != "up":
                    split(j, b, over)
                    continue
                n = j[1]
                dve.wait_ge(e_silu, b * N_UP + n + 1)
                if n >= 2:
                    wait_e(("ge", n - 2), b, over)
                dve.tensor_tensor(gated[:, n % 2, :], silu_e[:, n % 2, :], psum[:, E_BANK[j], S:2 * S], ALU.mult)\
                   .then_inc(e_freed["vector"], 1)
            if not over:
                if isinstance(b, int):
                    dve.wait_ge(e_low, b * N_SPLIT + N_SPLIT + E_SPLITS[over].index(FIRST[0]))
                    dve.sem_inc(e_low, HIS)
                for j in (GATHERED if isinstance(b, int) else FIRST + GATHERED):
                    split(j, b, over)
            for j in SUMS:
                t, h = divmod(j[1], HALVES)
                bank = wait_e(j, b, over)
                ww = work[:, t, 512 * h:512 * h + 512]
                dve.tensor_tensor(ww, ww, bank, ALU.add).then_inc(e_freed["vector"], 1)

        def skip(b):
            dve.sem_inc(pick_step, 3)
            dve.wait_ge(picked, b + 1)
            dve.sem_inc(picked, 1)
            dve.wait_ge(e_low, b * N_SPLIT + N_SPLIT)
            dve.sem_inc(e_low, N_SPLIT)
            dve.wait_ge(e_freed["vector"], b * e_n["vector"] + e_n["vector"])
            dve.sem_inc(e_freed["vector"], e_n["vector"])

        select(0, 0, False)
        for j in FIRST + GATHERED:
            split(j, -1, False)
        dve.sem_inc(e_freed["vector"], N_SUM)
        for t in range(TILES):
            own(dve.tensor_scalar(work[:, t, :], x_tok[:, t, :], ALPHA, None, ALU.mult))
        each_expert(dve, expert, skip)
        dve.wait_ge(e_freed["vector"], (2 * NE + 1) * e_n["vector"])
        for t in range(TILES):
            own(dve.tensor_copy(x_tok[:, t, :], work[:, t, :]))
        layer_norm()

    ctx.close()


def ff_loads(pl, a):
    w = a["w_ffn_in_2"][0].rearrange("(k p) n -> p k n", p=P)
    for u in range(FC // 2):
        pl.add_unit(("ff_in", u), [(half * KD * S, KD, S, w[:, :, half * FF + S * u:half * FF + S * (u + 1)]) for half in range(2)],
                    ("ff", 2 * u + 1))
    w = a["w_ffn_out_2"][0].rearrange("(k p) n -> p k n", p=P)
    for o, n in enumerate([3] * 6 + [4]):
        pl.add_unit(("ff_out", o), [(0, n, D, w[:, 3 * o:3 * o + n, :])],
                    ("ff_out_used", o) if o < 6 else ("down", TILES - 1, HALVES - 1))


PLAIN = ["x", "mem", "positions", "positions_2", "w_mem_kv", "w_in", "lru_wr", "lru_wi", "p_attn", "p_lru", "p_mem", "w_out",
         "w_peer_q", "peer_u", "peer_v", "w_mem_kv_2", "w_in_fox_2", "w_out_2", "w_ffn_in_2", "w_ffn_out_2", "w_exp_in_2",
         "w_exp_out_2", "g_mem", "g_mix", "g_ffn", "g_final", "ln_attn_g_2", "ln_attn_b_2", "ln_ffn_g_2", "ln_ffn_b_2"]


def layouts(v):
    def by_partition(x):
        return np.ascontiguousarray(x).reshape(-1, P).T

    def on_all(x):
        return np.broadcast_to(x.reshape(1, -1), (P, x.size))

    def chunks(x):
        return x.reshape(KD, P, -1).transpose(1, 0, 2).reshape(P, -1)

    f = v["w_in_fox_2"][0]
    b_forget = np.zeros((P, 1), np.float32)
    b_forget[:SH, 0] = v["b_forget_2"][0]
    parts = {"gate_b": by_partition(v["gate_b"][0]), "conv_w": by_partition(v["conv_w"][0]), "conv_b": by_partition(v["conv_b"][0]),
             "lru_br": by_partition(v["lru_br"][0]), "lru_bi": by_partition(v["lru_bi"][0]), "lam": by_partition(v["lru_lambda"][0]),
             "sink": on_all(v["attn_sink"][0]), "sink2": on_all(v["attn_sinks_2"][0]), "b_router": on_all(v["b_router_2"][0]),
             "b_forget": b_forget, "w_forget": chunks(f[:, -SH:]), "w_router": chunks(v["w_router_2"][0])}
    out = {name: v[name] for name in PLAIN}
    out["columns"] = np.concatenate([parts[name] for name in COLS], axis=1)
    out["constants"] = constants()
    out["sub_keys_T"] = v["peer_sub_keys"][0].reshape(2 * PH, PK, P).transpose(2, 0, 1)
    out["mem_2_T"] = v["mem_2"][0].T
    w = v["w_in_swa_2"][0]
    q, kv = SH * HD2, SKV * HD2
    twice = lambda x: np.repeat(x.reshape(D, SKV, 1, HD2), 2, axis=2).reshape(D, 2 * kv)
    out["w_swa"] = np.concatenate([w[:, :q], twice(w[:, q:q + kv]), twice(w[:, q + kv:q + 2 * kv]), w[:, q + 2 * kv:]], axis=1)
    return {name: np.ascontiguousarray(x) for name, x in out.items()}


def kernel(**inputs):
    import concourse.bacc as bacc
    from concourse.bass_utils import run_bass_kernel_spmd

    arrays = layouts({name: np.asarray(x) for name, x in inputs.items()})
    nc = bacc.Bacc("TRN2", target_bir_lowering=False, num_devices=1)
    a = {name: nc.dram_tensor("in_" + name, x.shape, mybir.dt.from_np(x.dtype), kind="ExternalInput").ap() for name, x in arrays.items()}
    a["out"] = nc.dram_tensor("out", (1, S, D), F32, kind="ExternalOutput").ap()
    two_blocks(nc, a)
    r = run_bass_kernel_spmd(nc, [{"in_" + name: x for name, x in arrays.items()}], core_ids=[0])
    return r.results[0]["out"]
```
